# Optimizing a Trainium2 kernel written in Bass

```python
import jax, jax.numpy as jnp
from jax import lax
import numpy as np
import math

D_MODEL = 1024
BATCH = 1
SEQ = 256
DEPTH = 2

N_MIXERS = 2
SB_HEADS = 16
SB_HEAD_DIM = D_MODEL // SB_HEADS
Q_BLOCK = 128
RET_HEADS = 8
RET_QK_DIM = D_MODEL // RET_HEADS
RET_V_DIM = 2 * RET_QK_DIM
RET_CHUNK = 128
ROPE_BASE = 10000.0
N_EXPERTS = 16
N_GROUPS = 4
EXPERTS_PER_GROUP = N_EXPERTS // N_GROUPS
TOP_K = 2
D_EXPERT = D_MODEL // 2
N_SB = (DEPTH + 1) // 2
N_RET = DEPTH // 2
DEEPNORM_ALPHA = (2 * DEPTH) ** 0.25
DEEPNORM_BETA = (8 * DEPTH) ** -0.25
LN_EPS = 1e-5


def layer_norm(x, g, b):
    xf = x.astype(jnp.float32)
    mu = jnp.mean(xf, axis=-1, keepdims=True)
    var = jnp.mean(jnp.square(xf - mu), axis=-1, keepdims=True)
    y = (xf - mu) * lax.rsqrt(var + LN_EPS) * g.astype(jnp.float32) + b.astype(jnp.float32)
    return y.astype(x.dtype)

def adaln_params(c, w, b):
    m = jax.nn.silu(c) @ w + b
    shift, scale, gate = jnp.split(m, 3, axis=-1)
    return shift[:, None, :], scale[:, None, :], gate[:, None, :]

def stick_breaking_attention(h, w_in, w_out):
    B, S, _ = h.shape
    qkv = (h @ w_in).reshape(B, S, 3, SB_HEADS, SB_HEAD_DIM)
    q = qkv[:, :, 0].transpose(0, 2, 1, 3)
    k = qkv[:, :, 1].transpose(0, 2, 1, 3)
    v = qkv[:, :, 2].transpose(0, 2, 1, 3)
    n_blocks = S // Q_BLOCK
    q_blocks = q.reshape(B, SB_HEADS, n_blocks, Q_BLOCK, SB_HEAD_DIM).transpose(2, 0, 1, 3, 4)
    key_pos = jnp.arange(S)
    scale = SB_HEAD_DIM ** -0.5

    def block(args):
        qb, i = args
        z = jnp.einsum('bhqd,bhkd->bhqk', qb, k).astype(jnp.float32) * scale
        q_pos = i * Q_BLOCK + jnp.arange(Q_BLOCK)
        causal = key_pos[None, :] < q_pos[:, None]
        log_keep = jnp.where(causal, jax.nn.log_sigmoid(-z), 0.0)
        suffix = lax.cumsum(log_keep, axis=3, reverse=True) - log_keep
        a = jnp.where(causal, jnp.exp(jax.nn.log_sigmoid(z) + suffix), 0.0)
        return jnp.einsum('bhqk,bhkd->bhqd', a.astype(v.dtype), v)

    o = lax.map(block, (q_blocks, jnp.arange(n_blocks)))
    o = o.transpose(1, 0, 3, 2, 4).reshape(B, S, D_MODEL)
    return o @ w_out

def rotary(x, cos, sin):
    half = x.shape[-1] // 2
    x1, x2 = x[..., :half], x[..., half:]
    return jnp.concatenate([x1 * cos - x2 * sin, x2 * cos + x1 * sin], axis=-1)

def retention(h, positions, w_in, gn_g, w_out):
    B, S, _ = h.shape
    f32 = jnp.float32
    proj = h @ w_in
    q, k, v, g = jnp.split(proj, [D_MODEL, 2 * D_MODEL, 4 * D_MODEL], axis=-1)
    q = q.reshape(B, S, RET_HEADS, RET_QK_DIM).astype(f32)
    k = k.reshape(B, S, RET_HEADS, RET_QK_DIM).astype(f32) * (RET_QK_DIM ** -0.5)
    v = v.reshape(B, S, RET_HEADS, RET_V_DIM).astype(f32)
    inv_freq = 1.0 / (ROPE_BASE ** (jnp.arange(0, RET_QK_DIM, 2, dtype=f32) / RET_QK_DIM))
    ang = positions.astype(f32)[..., None] * inv_freq
    cos = jnp.cos(ang)[:, :, None, :]
    sin = jnp.sin(ang)[:, :, None, :]
    q = rotary(q, cos, sin)
    k = rotary(k, cos, sin)

    log_gamma = jnp.log(1.0 - jnp.exp2(-5.0 - jnp.arange(RET_HEADS, dtype=f32)))
    n = jnp.arange(RET_CHUNK, dtype=f32)
    diff = n[:, None] - n[None, :]
    dmask = jnp.where(diff >= 0, jnp.exp(jnp.maximum(diff, 0.0) * log_gamma[:, None, None]), 0.0)
    xi = jnp.exp((n + 1.0) * log_gamma[:, None])
    zeta = jnp.exp((RET_CHUNK - 1.0 - n) * log_gamma[:, None])
    chunk_decay = jnp.exp(RET_CHUNK * log_gamma)
    n_chunks = S // RET_CHUNK

    def chunks(t):
        return t.reshape(B, n_chunks, RET_CHUNK, RET_HEADS, t.shape[-1]).transpose(1, 0, 3, 2, 4)

    def step(state, xs):
        qc, kc, vc = xs
        qk = jnp.einsum('bhnd,bhmd->bhnm', qc, kc) * dmask
        inner = jnp.einsum('bhnm,bhme->bhne', qk, vc)
        cross = jnp.einsum('bhnd,bhde->bhne', qc, state) * xi[None, :, :, None]
        state = state * chunk_decay[None, :, None, None] + jnp.einsum(
            'bhmd,bhme->bhde', kc * zeta[None, :, :, None], vc)
        return state, inner + cross

    state0 = jnp.zeros((B, RET_HEADS, RET_QK_DIM, RET_V_DIM), f32)
    _, o = lax.scan(step, state0, (chunks(q), chunks(k), chunks(v)))
    o = o.transpose(1, 0, 3, 2, 4).reshape(B, S, RET_HEADS, RET_V_DIM)
    mu = jnp.mean(o, axis=-1, keepdims=True)
    var = jnp.mean(jnp.square(o - mu), axis=-1, keepdims=True)
    o = ((o - mu) * lax.rsqrt(var + LN_EPS)).reshape(B, S, 2 * D_MODEL) * gn_g.astype(f32)
    return (jax.nn.silu(g) * o.astype(h.dtype)) @ w_out

def grouped_moe(h, router_w, router_b, w_gate, w_up, w_down):
    B, S, Dm = h.shape
    t = h.reshape(B * S, Dm)
    logits = t.astype(jnp.float32) @ router_w.astype(jnp.float32) + router_b.astype(jnp.float32)
    probs = jax.nn.softmax(logits, axis=-1)
    grouped = probs.reshape(-1, N_GROUPS, EXPERTS_PER_GROUP)
    group_score = jnp.sum(lax.top_k(grouped, TOP_K)[0], axis=-1)
    sel_group = jnp.argmax(group_score, axis=-1)
    expert_group = jnp.arange(N_EXPERTS) // EXPERTS_PER_GROUP
    in_group = expert_group[None, :] == sel_group[:, None]
    masked = jnp.where(in_group, logits, -jnp.inf)
    top_val, top_idx = lax.top_k(masked, TOP_K)
    top_w = jax.nn.softmax(top_val, axis=-1)
    combine = jnp.sum(jax.nn.one_hot(top_idx, N_EXPERTS, dtype=jnp.float32) * top_w[..., None], axis=1)
    out = jnp.zeros(t.shape, jnp.float32)
    for e in range(N_EXPERTS):
        hidden = jax.nn.silu(t @ w_gate[e]) * (t @ w_up[e])
        out = out + combine[:, e:e + 1] * (hidden @ w_down[e]).astype(jnp.float32)
    return out.astype(h.dtype).reshape(B, S, Dm)

def first_inputs(seed: int = 0) -> dict:
    key = jax.random.key(seed)
    ks = jax.random.split(key, 20)
    D, F = D_MODEL, D_EXPERT
    nrm = jax.random.normal
    x = nrm(ks[0], (BATCH, SEQ, D), jnp.float32)
    c = nrm(ks[1], (BATCH, D), jnp.float32)
    positions = jnp.broadcast_to(jnp.arange(SEQ, dtype=jnp.int32)[None, :], (BATCH, SEQ))
    ada_w = nrm(ks[2], (DEPTH, 2, D, 3 * D), jnp.float32) * (0.5 * D ** -0.5)
    ada_b = nrm(ks[3], (DEPTH, 2, 3 * D), jnp.float32) * 0.02
    ln_g = 1.0 + 0.02 * nrm(ks[4], (DEPTH, 2, D), jnp.float32)
    ln_b = 0.02 * nrm(ks[5], (DEPTH, 2, D), jnp.float32)
    sb_col = jnp.concatenate([jnp.ones((2 * D,), jnp.float32), jnp.full((D,), DEEPNORM_BETA, jnp.float32)])
    sb_w_in = nrm(ks[6], (N_SB, D, 3 * D), jnp.float32) * (D ** -0.5) * sb_col
    sb_w_out = nrm(ks[7], (N_SB, D, D), jnp.float32) * (D ** -0.5) * DEEPNORM_BETA
    ret_col = jnp.concatenate([jnp.ones((2 * D,), jnp.float32), jnp.full((2 * D,), DEEPNORM_BETA, jnp.float32),
                               jnp.ones((2 * D,), jnp.float32)])
    ret_w_in = nrm(ks[8], (N_RET, D, 6 * D), jnp.float32) * (D ** -0.5) * ret_col
    ret_gn_g = 1.0 + 0.02 * nrm(ks[9], (N_RET, 2 * D), jnp.float32)
    ret_w_out = nrm(ks[10], (N_RET, 2 * D, D), jnp.float32) * ((2 * D) ** -0.5) * DEEPNORM_BETA
    router_w = nrm(ks[11], (D, N_EXPERTS), jnp.float32) * (D ** -0.5)
    router_b = nrm(ks[12], (N_EXPERTS,), jnp.float32) * 0.01
    moe_w_gate = nrm(ks[13], (DEPTH, N_EXPERTS, D, F), jnp.float32) * (D ** -0.5)
    moe_w_up = nrm(ks[14], (DEPTH, N_EXPERTS, D, F), jnp.float32) * (D ** -0.5) * DEEPNORM_BETA
    moe_w_down = nrm(ks[15], (DEPTH, N_EXPERTS, F, D), jnp.float32) * (F ** -0.5) * DEEPNORM_BETA
    return {"x": x, "c": c, "positions": positions, "ada_w": ada_w, "ada_b": ada_b,
            "ln_g": ln_g, "ln_b": ln_b, "sb_w_in": sb_w_in, "sb_w_out": sb_w_out,
            "ret_w_in": ret_w_in, "ret_gn_g": ret_gn_g, "ret_w_out": ret_w_out,
            "router_w": router_w, "router_b": router_b, "moe_w_gate": moe_w_gate,
            "moe_w_up": moe_w_up, "moe_w_down": moe_w_down}

def first_block(x, c, positions, ada_w, ada_b, ln_g, ln_b, sb_w_in, sb_w_out, ret_w_in, ret_gn_g,
              ret_w_out, router_w, router_b, moe_w_gate, moe_w_up, moe_w_down):
    for i in range(DEPTH):
        shift, scale, gate = adaln_params(c, ada_w[i, 0], ada_b[i, 0])
        h = x * (1.0 + scale) + shift
        if i % N_MIXERS == 0:
            y = stick_breaking_attention(h, sb_w_in[i // 2], sb_w_out[i // 2])
        else:
            y = retention(h, positions, ret_w_in[i // 2], ret_gn_g[i // 2], ret_w_out[i // 2])
        x = layer_norm(DEEPNORM_ALPHA * x + (1.0 + gate) * y, ln_g[i, 0], ln_b[i, 0])
        shift, scale, gate = adaln_params(c, ada_w[i, 1], ada_b[i, 1])
        h = x * (1.0 + scale) + shift
        y = grouped_moe(h, router_w, router_b, moe_w_gate[i], moe_w_up[i], moe_w_down[i])
        x = layer_norm(DEEPNORM_ALPHA * x + (1.0 + gate) * y, ln_g[i, 1], ln_b[i, 1])
    return x


DEPTH_2 = 1

SSM_WIDTH = D_MODEL // 2
SSM_GROUP = 16
SSM_GROUPS = SSM_WIDTH // SSM_GROUP
SSM_STATE = 64
DT_MIN = 1e-3
DT_MAX = 1e-1
ATTN_HEADS = 8
ATTN_KV_HEADS = 2
HEAD_DIM = 64
ATTN_WIDTH = ATTN_HEADS * HEAD_DIM
IDX_HEADS = 8
IDX_DIM = 32
TOPK_MAX = 256
ROPE_THETA = 10000.0
NEG_BIG = -1e30
PEER_HEADS = 8
PEER_KEYS = 128
PEER_EXPERTS = PEER_KEYS * PEER_KEYS
PEER_KEY_DIM = 128
PEER_TOPK = 16
PEER_CHUNK = 128
NORM_EPS = 1e-6

IN_SPLITS = (SSM_WIDTH, ATTN_WIDTH, ATTN_KV_HEADS * HEAD_DIM, ATTN_KV_HEADS * HEAD_DIM,
             IDX_HEADS * IDX_DIM, IDX_DIM, IDX_HEADS, D_MODEL, D_MODEL)
IN_WIDTH = sum(IN_SPLITS)


def rmsnorm(x, g):
    xf = x.astype(jnp.float32)
    y = xf * lax.rsqrt(jnp.mean(xf * xf, axis=-1, keepdims=True) + NORM_EPS)
    return (y * g.astype(jnp.float32)).astype(x.dtype)

def rope_tables(seq, dim):
    pos = jnp.arange(seq, dtype=jnp.float32)
    inv = ROPE_THETA ** (-jnp.arange(0, dim, 2, dtype=jnp.float32) / dim)
    ang = pos[:, None] * inv[None, :]
    return jnp.cos(ang), jnp.sin(ang)

def apply_rope(x, cos, sin):
    half = x.shape[-1] // 2
    shape = (cos.shape[0],) + (1,) * (x.ndim - 3) + (half,)
    c = cos.reshape(shape)
    s = sin.reshape(shape)
    xf = x.astype(jnp.float32)
    x1, x2 = xf[..., :half], xf[..., half:]
    return jnp.concatenate([x1 * c - x2 * s, x2 * c + x1 * s], axis=-1).astype(x.dtype)

def s5_branch(u, a_re, a_im, log_dt, b_re, b_im, c_re, c_im, d_skip, w_glu):
    bsz, seq, _ = u.shape
    f32 = jnp.float32
    uf = u.astype(f32).reshape(bsz, seq, SSM_GROUPS, SSM_GROUP)
    lam = lax.complex(a_re.astype(f32), a_im.astype(f32))
    dt = jnp.exp(log_dt.astype(f32))[:, None]
    a_bar = jnp.exp(lam * dt)
    b = lax.complex(b_re.astype(f32), b_im.astype(f32))
    b_bar = ((a_bar - 1.0) / lam)[..., None] * b
    bu = jnp.einsum('gpc,bsgc->bsgp', b_bar, uf)
    a_seq = jnp.broadcast_to(a_bar, bu.shape)

    def combine(left, right):
        a1, s1 = left
        a2, s2 = right
        return a2 * a1, a2 * s1 + s2

    _, states = lax.associative_scan(combine, (a_seq, bu), axis=1)
    c = lax.complex(c_re.astype(f32), c_im.astype(f32))
    y = jnp.real(jnp.einsum('gcp,bsgp->bsgc', c, states))
    y = y + d_skip.astype(f32).reshape(SSM_GROUPS, SSM_GROUP) * uf
    y = jax.nn.gelu(y.reshape(bsz, seq, SSM_WIDTH))
    y = y * jax.nn.sigmoid(y @ w_glu.astype(f32))
    return y.astype(u.dtype)

def dsa_branch(q, k, v, qi, ki, wi):
    bsz, seq = q.shape[0], q.shape[1]
    topk = min(TOPK_MAX, seq // 4)
    nb = seq // Q_BLOCK
    grp = ATTN_HEADS // ATTN_KV_HEADS
    f32 = jnp.float32
    kf = ki.astype(f32)
    idx_scale = (IDX_HEADS ** -0.5) * (IDX_DIM ** -0.5)
    s_pos = jnp.arange(seq)

    def to_blocks(t):
        return t.reshape((bsz, nb, Q_BLOCK) + t.shape[2:]).swapaxes(0, 1)

    def one_block(args):
        qb, qib, wib, blk = args
        t_pos = blk * Q_BLOCK + jnp.arange(Q_BLOCK)
        rel = jax.nn.relu(jnp.einsum('bthd,bsd->bths', qib.astype(f32), kf))
        score = jnp.einsum('bths,bth->bts', rel, wib.astype(f32)) * idx_scale
        causal = s_pos[None, :] <= t_pos[:, None]
        score = jnp.where(causal[None], score, NEG_BIG)
        _, sel = lax.top_k(score, topk)
        valid = sel <= t_pos[None, :, None]
        kg = jax.vmap(lambda kk, ii: kk[ii])(k, sel)
        vg = jax.vmap(lambda vv, ii: vv[ii])(v, sel)
        qg = qb.reshape(bsz, Q_BLOCK, ATTN_KV_HEADS, grp, HEAD_DIM).astype(f32)
        logits = jnp.einsum('btngd,btknd->btngk', qg, kg.astype(f32)) * (HEAD_DIM ** -0.5)
        logits = jnp.where(valid[:, :, None, None, :], logits, NEG_BIG)
        p = jax.nn.softmax(logits, axis=-1)
        o = jnp.einsum('btngk,btknd->btngd', p, vg.astype(f32))
        return o.reshape(bsz, Q_BLOCK, ATTN_WIDTH).astype(qb.dtype)

    out = lax.map(one_block, (to_blocks(q), to_blocks(qi), to_blocks(wi), jnp.arange(nb)))
    return out.swapaxes(0, 1).reshape(bsz, seq, ATTN_WIDTH)

def peer_ffn(x, w_q, sub_k1, sub_k2, u_tab, v_tab):
    bsz, seq, d = x.shape
    f32 = jnp.float32
    q = (x @ w_q).astype(f32).reshape(bsz, seq, PEER_HEADS, 2, PEER_KEY_DIM)
    s1 = jnp.einsum('bshd,hnd->bshn', q[..., 0, :], sub_k1.astype(f32))
    s2 = jnp.einsum('bshd,hnd->bshn', q[..., 1, :], sub_k2.astype(f32))
    v1, i1 = lax.top_k(s1, PEER_TOPK)
    v2, i2 = lax.top_k(s2, PEER_TOPK)
    cand_s = (v1[..., :, None] + v2[..., None, :]).reshape(bsz, seq, PEER_HEADS, PEER_TOPK * PEER_TOPK)
    cand_i = (i1[..., :, None] * PEER_KEYS + i2[..., None, :]).reshape(bsz, seq, PEER_HEADS, PEER_TOPK * PEER_TOPK)
    top_s, pos = lax.top_k(cand_s, PEER_TOPK)
    experts = jnp.take_along_axis(cand_i, pos, axis=-1)
    gates = jax.nn.softmax(top_s, axis=-1)
    n_tok = bsz * seq
    n_chunks = n_tok // PEER_CHUNK
    n_sel = PEER_HEADS * PEER_TOPK
    xc_all = x.reshape(n_chunks, PEER_CHUNK, d)
    ec_all = experts.reshape(n_chunks, PEER_CHUNK, n_sel)
    gc_all = gates.reshape(n_chunks, PEER_CHUNK, n_sel)

    def chunk(args):
        xc, ec, gc = args
        u = u_tab[ec].astype(f32)
        act = jax.nn.gelu(jnp.einsum('ced,cd->ce', u, xc.astype(f32))) * gc
        return jnp.einsum('ce,ced->cd', act, v_tab[ec].astype(f32)).astype(x.dtype)

    out = lax.map(chunk, (xc_all, ec_all, gc_all))
    return out.reshape(bsz, seq, d)

def second_inputs(seed: int = 0) -> dict:
    key = jax.random.key(seed)
    ks = jax.random.split(key, 24)
    f32 = jnp.float32
    L, D, G, P, N = DEPTH_2, D_MODEL, SSM_GROUPS, SSM_STATE, SSM_GROUP
    nrm = lambda k, shape, s: jax.random.normal(k, shape, f32) * s
    x = jax.random.normal(ks[0], (BATCH, SEQ, D), f32)
    norm1_g = 1.0 + nrm(ks[1], (L, D), 0.02)
    w_in = nrm(ks[2], (L, D, IN_WIDTH), D ** -0.5)
    a_re = -0.5 * (1.0 + nrm(ks[3], (L, G, P), 0.01))
    a_im = jnp.broadcast_to(math.pi * jnp.arange(P, dtype=f32), (L, G, P)) + nrm(ks[4], (L, G, P), 0.01)
    log_dt = jax.random.uniform(ks[5], (L, G), f32, math.log(DT_MIN), math.log(DT_MAX))
    b_re = nrm(ks[6], (L, G, P, N), (2.0 * N) ** -0.5)
    b_im = nrm(ks[7], (L, G, P, N), (2.0 * N) ** -0.5)
    c_re = nrm(ks[8], (L, G, N, P), P ** -0.5)
    c_im = nrm(ks[9], (L, G, N, P), P ** -0.5)
    d_skip = nrm(ks[10], (L, SSM_WIDTH), 1.0)
    w_glu = nrm(ks[11], (L, SSM_WIDTH, SSM_WIDTH), SSM_WIDTH ** -0.5)
    w_ssm_up = nrm(ks[12], (L, SSM_WIDTH, D), SSM_WIDTH ** -0.5)
    w_attn_up = nrm(ks[13], (L, ATTN_WIDTH, D), ATTN_WIDTH ** -0.5)
    w_out = nrm(ks[14], (L, D, D), D ** -0.5)
    norm2_g = 1.0 + nrm(ks[15], (L, D), 0.02)
    peer_wq = nrm(ks[16], (L, D, PEER_HEADS * 2 * PEER_KEY_DIM), D ** -0.5)
    peer_k1 = nrm(ks[17], (L, PEER_HEADS, PEER_KEYS, PEER_KEY_DIM), PEER_KEY_DIM ** -0.5)
    peer_k2 = nrm(ks[18], (L, PEER_HEADS, PEER_KEYS, PEER_KEY_DIM), PEER_KEY_DIM ** -0.5)
    peer_u = nrm(ks[19], (L, PEER_EXPERTS, D), D ** -0.5)
    peer_v = nrm(ks[20], (L, PEER_EXPERTS, D), PEER_HEADS ** -0.5)
    norm_f_g = 1.0 + nrm(ks[21], (D,), 0.02)
    return {"x": x, "norm1_g": norm1_g, "w_in": w_in, "a_re": a_re, "a_im": a_im,
            "log_dt": log_dt, "b_re": b_re, "b_im": b_im, "c_re": c_re, "c_im": c_im,
            "d_skip": d_skip, "w_glu": w_glu, "w_ssm_up": w_ssm_up, "w_attn_up": w_attn_up,
            "w_out": w_out, "norm2_g": norm2_g, "peer_wq": peer_wq, "peer_k1": peer_k1,
            "peer_k2": peer_k2, "peer_u": peer_u, "peer_v": peer_v, "norm_f_g": norm_f_g}

def second_block(x, norm1_g, w_in, a_re, a_im, log_dt, b_re, b_im, c_re, c_im, d_skip, w_glu,
              w_ssm_up, w_attn_up, w_out, norm2_g, peer_wq, peer_k1, peer_k2, peer_u, peer_v,
              norm_f_g):
    bsz, seq, _ = x.shape
    cos_a, sin_a = rope_tables(seq, HEAD_DIM)
    cos_i, sin_i = rope_tables(seq, IDX_DIM)
    offsets = np.cumsum(IN_SPLITS)[:-1].tolist()
    h = x
    for layer in range(DEPTH_2):
        xn = rmsnorm(h, norm1_g[layer])
        proj = xn @ w_in[layer]
        u, q, k, v, qi, ki, wi, g_ssm, g_attn = jnp.split(proj, offsets, axis=-1)
        y_ssm = s5_branch(u, a_re[layer], a_im[layer], log_dt[layer], b_re[layer], b_im[layer],
                          c_re[layer], c_im[layer], d_skip[layer], w_glu[layer])
        q = apply_rope(q.reshape(bsz, seq, ATTN_HEADS, HEAD_DIM), cos_a, sin_a)
        k = apply_rope(k.reshape(bsz, seq, ATTN_KV_HEADS, HEAD_DIM), cos_a, sin_a)
        v = v.reshape(bsz, seq, ATTN_KV_HEADS, HEAD_DIM)
        qi = apply_rope(qi.reshape(bsz, seq, IDX_HEADS, IDX_DIM), cos_i, sin_i)
        ki = apply_rope(ki, cos_i, sin_i)
        y_attn = dsa_branch(q, k, v, qi, ki, wi)
        merged = (jax.nn.sigmoid(g_ssm) * (y_ssm @ w_ssm_up[layer])
                  + jax.nn.sigmoid(g_attn) * (y_attn @ w_attn_up[layer]))
        h = h + merged @ w_out[layer]
        hn = rmsnorm(h, norm2_g[layer])
        h = h + peer_ffn(hn, peer_wq[layer], peer_k1[layer], peer_k2[layer], peer_u[layer], peer_v[layer])
    return rmsnorm(h, norm_f_g)


def setup_inputs(seed=0):
    out = dict(first_inputs(seed))
    for name, value in second_inputs(seed + 1).items():
        if name != "x":
            out[name + "_2"] = value
    return out


def reference(
    x, c, positions, ada_w, ada_b, ln_g, ln_b, sb_w_in, sb_w_out, ret_w_in, ret_gn_g, ret_w_out,
    router_w, router_b, moe_w_gate, moe_w_up, moe_w_down, norm1_g_2, w_in_2, a_re_2, a_im_2,
    log_dt_2, b_re_2, b_im_2, c_re_2, c_im_2, d_skip_2, w_glu_2, w_ssm_up_2, w_attn_up_2,
    w_out_2, norm2_g_2, peer_wq_2, peer_k1_2, peer_k2_2, peer_u_2, peer_v_2, norm_f_g_2,
):
    x = first_block(
        x, c, positions, ada_w, ada_b, ln_g, ln_b, sb_w_in, sb_w_out, ret_w_in, ret_gn_g,
        ret_w_out, router_w, router_b, moe_w_gate, moe_w_up, moe_w_down,
    )
    return second_block(
        x, norm1_g_2, w_in_2, a_re_2, a_im_2, log_dt_2, b_re_2, b_im_2, c_re_2, c_im_2,
        d_skip_2, w_glu_2, w_ssm_up_2, w_attn_up_2, w_out_2, norm2_g_2, peer_wq_2, peer_k1_2,
        peer_k2_2, peer_u_2, peer_v_2, norm_f_g_2,
    )


_drawn_inputs = setup_inputs


def setup_inputs(seed=0):
    import zlib

    import numpy as np

    out = dict(_drawn_inputs(seed))
    spreads = {}
    factors = {'ret_gn_g': 2.8,
     'a_re_2': 200.0,
     'norm_f_g_2': 22.945,
     'a_im_2': 30.376,
     'log_dt_2': 30.824,
     'b_re_2': 37.92,
     'b_im_2': 37.152,
     'c_re_2': 35.232,
     'c_im_2': 38.168}
    for name, (base, spread) in spreads.items():
        noise = np.random.default_rng([zlib.crc32(name.encode()), seed]).standard_normal(out[name].shape)
        drawn = base * np.exp(spread * noise) if base else spread * noise
        out[name] = __import__('jax').numpy.asarray(drawn.astype(out[name].dtype))
    for name, factor in factors.items():
        out[name] = (out[name] * factor).astype(out[name].dtype)
    return out
```

```python
from contextlib import ExitStack

import concourse.bass as bass
import numpy as np
from concourse import mybir
from concourse.alu_op_type import AluOpType as ALU

F32 = mybir.dt.float32
I32 = mybir.dt.int32
U32 = mybir.dt.uint32
ACT = mybir.ActivationFunctionType
AX = mybir.AxisListType

P = 128
T = 256
TT = T // P
D = 1024
KD = D // P
CHUNK = 4096
COLS = CHUNK // KD
RING = 6
DEPTH = 2
ALPHA = float((2 * DEPTH) ** 0.25)
LN_EPS = 1e-5
RMS_EPS = 1e-6
SB_HEADS = 16
SB_DIM = D // SB_HEADS
RET_HEADS = 8
RET_V = 2 * D // RET_HEADS
EXPERTS = 16
GROUPS = 4
PER_GROUP = EXPERTS // GROUPS
IDX_SCALE = 1.0 / 16.0
NEG = -1e30
TWO_PI = float(np.float32(6.283185))
ROUND = 12582912.0

STREAM = [("ada00", 6), ("sb_in", 6), ("sb_out", 2),
          ("ada01", 6), ("moe0", 3 * EXPERTS),
          ("ada10", 6), ("ret_in", 12), ("ret_out", 4),
          ("ada11", 6), ("moe1", 3 * EXPERTS),
          ("in2", 8), ("w_glu", 1), ("ssm_up", 1), ("attn_up", 1), ("w_out2", 2), ("peer_wq", 4), ("peer_keys", 1)]
START = {}
_n = 0
for _name, _count in STREAM:
    START[_name] = _n
    _n += _count
CHUNKS = _n
SHORT = {START["in2"] + 3: KD * 136, START["w_glu"]: 4 * 512, START["peer_keys"]: 2048}


def next_start(name):
    order = [n for n, _ in STREAM]
    i = order.index(name)
    return START[order[i + 1]] if i + 1 < len(order) else CHUNKS


class Core:

    def __init__(self, nc, ctx, inputs):
        self.nc = nc
        self.ctx = ctx
        self.A = inputs
        self.fetched = 0
        self.bank = ctx.enter_context(nc.psum_tensor("bank", [P, 8, 512], F32))
        self.consts = self.sb("consts", [P, 7, P])
        self.ident = self.consts[:, 0, :]
        self.tri_neg = self.consts[:, 1, :]
        self.ones_neg = self.consts[:, 2, :]
        self.swap128 = self.consts[:, 3, :]
        self.swap64 = self.consts[:, 4, :]
        self.swap32 = self.consts[:, 5, :]
        self.iota = self.consts[:, 6, :]
        self.x = self.sb("x", [P, TT, D])
        self.hT = self.sb("hT", [P, KD, T])
        self.mod = self.sb("mod", [P, 3 * D])
        self.landed = [nc.alloc_semaphore(f"landed{s}") for s in range(RING)]
        self.chunk_used = nc.alloc_semaphore("chunk_used")
        self.stored = nc.alloc_semaphore("stored")
        self.stage_sems = []
        self.loaded = nc.alloc_semaphore("consts_loaded")

    def sb(self, name, shape, dt=F32):
        return self.ctx.enter_context(self.nc.sbuf_tensor(name, shape, dt))

    def sem(self, name):
        self.stage_sems.append(self.nc.alloc_semaphore(name))
        return self.stage_sems[-1]

    def recycle_sems(self):
        self.nc.clear_and_free_semaphores(self.stage_sems)
        self.nc.all_engine_barrier()
        self.stage_sems = []


class Chain:

    def __init__(self, eng, sem):
        self.eng, self.sem, self.n = eng, sem, 0

    def step(self, ins):
        self.n += 1
        ins.then_inc(self.sem, 1)
        return ins

    def settle(self):
        self.eng.wait_ge(self.sem, self.n)

    def do(self, ins):
        self.step(ins)
        self.settle()



def fetch_chunks(sp, K, upto):
    upto = min(upto, CHUNKS)
    for n in range(K.fetched, upto):
        if n >= RING:
            sp.wait_ge(K.chunk_used, n - RING + 1)
        size = SHORT.get(n, CHUNK)
        sp.dma_start(K.ring[:, n % RING, 0:size], K.A["stream"][n, :, 0:size]).then_inc(K.landed[n % RING], 16)
    K.fetched = max(K.fetched, upto)


def wait_chunk(pe, K, n):
    pe.wait_ge(K.landed[n % RING], 16 * (n // RING + 1))


def feature_product(pe, K, n, xT, bank0, slot=None, land=None):
    if n is not None:
        slot, land = n % RING, 16 * (n // RING + 1)
    pe.wait_ge(K.landed[slot], land)
    w = K.ring[:, slot, :].rearrange("p (k c) -> p k c", k=KD)
    for c in range(4):
        out = K.bank[:, bank0 + c // 2, (c % 2) * T:(c % 2 + 1) * T]
        for k in range(KD):
            last = pe.matmul(out, w[:, k, c * P:(c + 1) * P], xT[:, k, :], start=(k == 0), stop=(k == KD - 1))
    last.then_inc(K.chunk_used, 1)


def token_product(pe, K, n, xT, banks, cols=COLS, kt=KD, start=True, stop=True):
    wait_chunk(pe, K, n)
    w = K.ring[:, n % RING, 0:kt * cols].rearrange("p (k c) -> p k c", k=kt)
    for tt in range(TT):
        for k in range(kt):
            last = pe.matmul(banks[tt], xT[:, k, tt * P:(tt + 1) * P], w[:, k, :],
                             start=(start and k == 0), stop=(stop and k == kt - 1))
    last.then_inc(K.chunk_used, 1)



def load_stage(K, scope):
    nc = K.nc
    K.ring = scope.enter_context(nc.sbuf_tensor("ring", [P, RING, CHUNK], F32))
    K.silu_c = scope.enter_context(nc.sbuf_tensor("silu_c", [P, KD], F32))
    K.c_wide = scope.enter_context(nc.sbuf_tensor("c_wide", [P, KD, P], F32))
    c_in, act_done, wide_done = K.sem("c_in"), K.sem("silu_c_done"), K.sem("c_wide_done")
    with nc.Block() as block:
        @block.sync
        def _(sp):
            sp.dma_start(K.silu_c[:], K.A["c_cols"]).then_inc(c_in, 16)
            fetch_chunks(sp, K, RING)

        @block.scalar
        def _(act):
            act.dma_start(K.consts[:], K.A["consts"]).then_inc(K.loaded, 16)
            act.dma_start(K.x[:], K.A["x_tokens"]).then_inc(K.loaded, 16)
            act.wait_ge(c_in, 16)
            act.activation(K.silu_c[:], K.silu_c[:], ACT.Silu).then_inc(act_done, 1)

        @block.vector
        def _(dve):
            dve.wait_ge(act_done, 1)
            dve.tensor_copy(K.c_wide[:], K.silu_c[:].unsqueeze(2).to_broadcast([P, KD, P])).then_inc(wide_done, 1)
            dve.wait_ge(wide_done, 1)



def ada_stage(K, name, row):
    nc = K.nc
    n0 = START[name]
    bias_in = K.sem(f"{name}_bias_in")
    chain = K.sem(f"{name}_dve")
    h_ready = K.sem(f"{name}_h")
    turned = K.sem(f"{name}_turned")
    evac = K.sem(f"{name}_evac")
    with ExitStack() as stage, nc.Block() as block:
        h = stage.enter_context(nc.sbuf_tensor(f"{name}_hbuf", [P, TT, D], F32))

        @block.sync
        def _(sp):
            fetch_chunks(sp, K, next_start(name) + RING)

        @block.scalar
        def _(act):
            act.dma_start(K.mod[:], K.A["ada_b"][row:row + 1, :].to_broadcast([P, 3 * D])).then_inc(bias_in, 16)
            evacuate_turned(act, K, turned, evac)

        @block.tensor
        def _(pe):
            for j in range(6):
                wait_chunk(pe, K, n0 + j)
                w = K.ring[:, (n0 + j) % RING, :].rearrange("p (k c) -> p k c", k=KD)
                for k in range(KD):
                    last = pe.matmul(K.bank[:, j, :], K.c_wide[:, k, :], w[:, k, :], start=(k == 0), stop=(k == KD - 1))
                last.then_inc(K.chunk_used, 1)
            pe.wait_ge(K.loaded, 32)
            turn_tokens(pe, K, h, h_ready, turned)

        @block.vector
        def _(dve):
            c = Chain(dve, chain)
            dve.wait_ge(bias_in, 16)
            dve.wait_ge(K.loaded, 32)
            for j in range(6):
                dve.wait_ge(K.chunk_used, n0 + j + 1)
                part = K.mod[:, j * COLS:(j + 1) * COLS]
                c.step(dve.scalar_tensor_tensor(part, K.bank[:, j, :], 0.0 if j < 2 else 1.0, part, ALU.add, ALU.add))
            for tt in range(TT):
                c.settle()
                c.do(dve.tensor_tensor(h[:, tt, :], K.x[:, tt, :], K.mod[:, D:2 * D], ALU.mult))
                dve.tensor_tensor(h[:, tt, :], h[:, tt, :], K.mod[:, 0:D], ALU.add).then_inc(h_ready, 1)


def turn_tokens(pe, K, h, h_ready, turned):
    for tt in range(TT):
        pe.wait_ge(h_ready, tt + 1)
        for k in range(KD):
            out = K.bank[:, (6 + k // 2) % 8, (k % 2) * T + tt * P:(k % 2) * T + (tt + 1) * P]
            last = pe.transpose(out, h[:, tt, k * P:(k + 1) * P], K.ident)
    last.then_inc(turned, 1)


def evacuate_turned(act, K, turned, evac):
    act.wait_ge(turned, 1)
    for b in range(4):
        act.activation(K.hT[:, 2 * b:2 * b + 2, :], K.bank[:, (6 + b) % 8, :].rearrange("p (k t) -> p k t", k=2),
                       ACT.Copy).then_inc(evac, 1)



def layer_norm_stage(K, name, row, project):
    nc = K.nc
    rows_in, chain, var_ready, rstd_ready = (K.sem(f"{name}_norm_{s}") for s in ("rows_in", "dve", "var", "std"))
    with ExitStack() as stage, nc.Block() as block:
        sb = lambda n, s: stage.enter_context(nc.sbuf_tensor(f"{name}_{n}", s, F32))
        g_row, b_row = sb("g", [P, D]), sb("b", [P, D])
        s = sb("s", [P, TT, D])
        stats, mv, std = sb("stats", [P, TT, 2, 6]), sb("mv", [P, TT, 2]), sb("std", [P, TT])
        eps = sb("eps", [P, 1])

        @block.sync
        def _(sp):
            sp.dma_start(g_row[:], K.A["ln_g"][row:row + 1, :].to_broadcast([P, D])).then_inc(rows_in, 16)
            sp.dma_start(b_row[:], K.A["ln_b"][row:row + 1, :].to_broadcast([P, D])).then_inc(rows_in, 16)

        @block.tensor
        def _(pe):
            project(pe)

        @block.scalar
        def _(act):
            act.wait_ge(var_ready, 1)
            act.activation(std[:], mv[:, :, 1], ACT.Sqrt, bias=eps[:]).then_inc(rstd_ready, 1)

        @block.vector
        def _(dve):
            c = Chain(dve, chain)
            c.step(dve.memset(eps[:], LN_EPS))
            dve.wait_ge(K.chunk_used, next_start(name))
            for tt in range(TT):
                y = K.bank[:, 2 * tt:2 * tt + 2, :].rearrange("p b c -> p (b c)")
                c.do(dve.tensor_tensor(s[:, tt, :], y, K.mod[:, 2 * D:3 * D], ALU.mult))
                c.do(dve.scalar_tensor_tensor(s[:, tt, :], K.x[:, tt, :], ALPHA, s[:, tt, :], ALU.mult, ALU.add))
                for j in range(2):
                    c.step(dve.bn_stats(stats[:, tt, j, :], s[:, tt, j * 512:(j + 1) * 512]))
                c.settle()
                last = dve.bn_aggr(mv[:, tt, :], stats[:, tt, :, :])
                if tt == 0:
                    c.step(last)
            last.then_inc(var_ready, 1)
            dve.wait_ge(rstd_ready, 1)
            c.do(dve.reciprocal(std[:], std[:]))
            dve.wait_ge(rows_in, 32)
            for tt in range(TT):
                c.do(dve.tensor_scalar(s[:, tt, :], s[:, tt, :], mv[:, tt, 0:1], std[:, tt:tt + 1], ALU.subtract, ALU.mult))
                c.do(dve.tensor_tensor(s[:, tt, :], s[:, tt, :], g_row[:], ALU.mult))
                c.step(dve.tensor_tensor(K.x[:, tt, :], s[:, tt, :], b_row[:], ALU.add))
            c.settle()



def stick_breaking_stage(K):
    nc = K.nc
    n0 = START["sb_in"]
    W = T + P
    act_done, dve_done, q_zeroed, zeroed = (K.sem(f"sb_{s}") for s in ("act_done", "dve_done", "q_zeroed", "v_zeroed"))
    with ExitStack() as stage:
        sb = lambda n, s: stage.enter_context(nc.sbuf_tensor(f"sb_{n}", s, F32))
        oT = sb("oT", [P, KD, T])
        heads = stage.enter_context(ExitStack())
        sb = lambda n, s: heads.enter_context(nc.sbuf_tensor(f"sb_{n}", s, F32))
        qz = sb("qz", [P, SB_HEADS, T])
        kT = sb("kT", [P, KD, T])
        vz = sb("vz", [P, TT, SB_HEADS, P])

        with nc.Block() as block:
            @block.sync
            def _(sp):
                fetch_chunks(sp, K, START["sb_out"] + RING)

            @block.gpsimd
            def _(pool):
                pool.memset(vz[:], 0.0).then_inc(zeroed, 1)

            @block.tensor
            def _(pe):
                for j in range(6):
                    b = 2 * j % 8
                    if j >= 4:
                        pe.wait_ge(act_done, j - 3)
                        pe.wait_ge(dve_done, j - 3)
                    if j < 4:
                        feature_product(pe, K, n0 + j, K.hT, b)
                    else:
                        token_product(pe, K, n0 + j, K.hT, [K.bank[:, b + tt, :] for tt in range(TT)])

            def empty(eng, i, done):
                def scaled(out, src, scale):
                    if i == 0:
                        return eng.activation(out, src, ACT.Copy, scale=scale)
                    return eng.tensor_scalar(out, src, scale, None, ALU.mult)

                eng.wait_ge(q_zeroed, 1)
                for j in range(6):
                    if j == 4:
                        eng.wait_ge(zeroed, 1)
                    src = K.bank[:, 2 * j % 8 + i, :]
                    eng.wait_ge(K.chunk_used, n0 + j + 1)
                    if 2 <= j < 4:
                        c = 4 * (j - 2) + 2 * i
                        scaled(kT[:, c:c + 2, :], src.rearrange("p (c t) -> p c t", c=2), 1.0).then_inc(done, 1)
                        continue
                    for half in range(2):
                        lo = half * SB_DIM
                        if j < 2:
                            head = 8 * j + 4 * i + half
                            last = scaled(qz[lo:lo + SB_DIM, head:head + 3:2, :],
                                          src[lo:lo + SB_DIM, :].rearrange("p (c t) -> p c t", c=2), SB_DIM ** -0.5)
                        else:
                            head = 8 * (j - 4) + half
                            heads_v = src.rearrange("p (h two d) -> p h two d", two=2, d=SB_DIM)
                            last = scaled(vz[:, i, head:head + 7:2, lo:lo + SB_DIM], heads_v[:, :, half, :], 1.0)
                    last.then_inc(done, 1)

            @block.scalar
            def _(act):
                empty(act, 0, act_done)

            @block.vector
            def _(dve):
                dve.memset(qz[:], 0.0).then_inc(q_zeroed, 1)
                empty(dve, 1, dve_done)

        z_made, z_abs, soft, sp_made, sp_masked, s_made, a_made, a_masked, o_made, o_done = (
            K.sem(f"sb_{s}") for s in ("z_made", "z_abs", "soft", "sp_made", "sp_masked", "s_made", "a_made",
                                       "a_masked", "o_made", "o_done"))
        act_chain = K.sem("sb_act")
        with nc.Block() as block:
            NB = 3
            zabs, soft_b, sp_b, a_b = (sb(n, [P, NB, W]) for n in ("zabs", "softb", "spb", "ab"))
            zbank = lambda h: K.bank[:, h % 2, 0:W]
            sbank = lambda h: K.bank[:, 2 + h % 2, 0:W]

            def diagonal(buf):
                return buf.rearrange("p (b q) -> p b q", q=P)[:, 0:3:2, :]

            @block.tensor
            def _(pe):
                def scores(h, out, tile, stop):
                    if tile == 0:
                        return pe.matmul(out[:, 0:T], kT[:, h // 2, 0:P], qz[:, h, :], start=True, stop=stop)
                    return pe.matmul(out[:, T:W], kT[:, h // 2, P:T], qz[:, h, P:T], start=True, stop=stop)

                for i in range(SB_HEADS + 3):
                    if i < SB_HEADS:
                        if i >= 2:
                            pe.wait_ge(sp_made, i - 1)
                        scores(i, zbank(i), 0, True)
                        scores(i, zbank(i), 1, True).then_inc(z_made, 1)
                    h = i - 1
                    if 0 <= h < SB_HEADS:
                        if h >= 2:
                            pe.wait_ge(a_made, h - 1)
                        scores(h, sbank(h), 0, False)
                        pe.wait_ge(sp_masked, h + 1)
                        sp = sp_b[:, h % NB, :]
                        pe.matmul(sbank(h)[:, P:T], K.ones_neg, sp[:, T:W], start=False, stop=False)
                        pe.matmul(sbank(h)[:, 0:T], K.tri_neg, sp[:, 0:T], start=False, stop=True)
                        scores(h, sbank(h), 1, False)
                        pe.matmul(sbank(h)[:, T:W], K.tri_neg, sp[:, T:W], start=False, stop=True).then_inc(s_made, 1)
                    h = i - 3
                    if h >= 0:
                        pair, a = h // 2, a_b[:, h % NB, :]
                        out = K.bank[:, 4 + pair % 2, 0:T]
                        if h % 2 == 0 and pair >= 2:
                            pe.wait_ge(o_done, pair - 1)
                        pe.wait_ge(a_masked, h + 1)
                        parts = [(out, vz[:, 0, h, :], a[:, 0:T]), (out[:, P:T], vz[:, 1, h, :], a[:, T:W])]
                        for n, (o, v, prob) in enumerate(parts if h % 2 == 0 else parts[::-1]):
                            last = pe.matmul(o, v, prob, start=(h % 2 == 0 and n == 0), stop=(h % 2 == 1 and n == 1),
                                             skip_group_check=True)
                        last.then_inc(o_made, 1)

            @block.vector
            def _(dve):
                for i in range(SB_HEADS + 4):
                    h = i - 1
                    if 0 <= h < SB_HEADS:
                        dve.wait_ge(soft, 2 * h + 2)
                        if h >= NB:
                            dve.wait_ge(s_made, h - NB + 1)
                        dve.scalar_tensor_tensor(sp_b[:, h % NB, :], zbank(h), 0.0, soft_b[:, h % NB, :], ALU.max,
                                                 ALU.add).then_inc(sp_made, 1)
                    h = i - 4
                    if h >= 0 and h % 2 == 1:
                        dve.wait_ge(o_made, h + 1)
                        dve.tensor_copy(oT[:, h // 2, :], K.bank[:, 4 + h // 2 % 2, 0:T]).then_inc(o_done, 1)

            @block.scalar
            def _(act):
                act.preload_act_table_set("natural_log_exp_and_others")
                for i in range(SB_HEADS + 1):
                    if i < SB_HEADS:
                        act.wait_ge(z_made, i + 1)
                        act.activation(zabs[:, i % NB, :], zbank(i), ACT.Abs).then_inc(z_abs, 1)
                        act.wait_ge(z_abs, i + 1)
                        if i >= NB:
                            act.wait_ge(sp_made, i - NB + 1)
                        act.activation(zabs[:, i % NB, :], zabs[:, i % NB, :], ACT.Exp, scale=-1.0).then_inc(soft, 1)
                        act.wait_ge(soft, 2 * i + 1)
                        act.activation(soft_b[:, i % NB, :], zabs[:, i % NB, :], ACT.Ln, bias=1.0).then_inc(soft, 1)
                    h = i - 1
                    if h >= 0:
                        act.wait_ge(s_made, h + 1)
                        if h >= NB:
                            act.wait_ge(o_made, h - NB + 1)
                        act.activation(a_b[:, h % NB, :], sbank(h), ACT.Exp).then_inc(a_made, 1)

            @block.gpsimd
            def _(pool):
                mask = dict(compare_op=ALU.is_gt, fill=0.0, base=0, pattern=[[0, 2], [1, P]], channel_multiplier=-1)
                for i in range(SB_HEADS + 1):
                    if i < SB_HEADS:
                        pool.wait_ge(sp_made, i + 1)
                        d = diagonal(sp_b[:, i % NB, :])
                        pool.affine_select(out=d, in_=d, **mask).then_inc(sp_masked, 1)
                    if i >= 1:
                        pool.wait_ge(a_made, i)
                        d = diagonal(a_b[:, (i - 1) % NB, :])
                        pool.affine_select(out=d, in_=d, **mask).then_inc(a_masked, 1)

        heads.close()

        def project(pe):
            for dh in range(2):
                token_product(pe, K, START["sb_out"] + dh, oT, [K.bank[:, 2 * tt + dh, :] for tt in range(TT)])
        layer_norm_stage(K, "sb_out", 0, project)



def moe_stage(K, layer):
    nc = K.nc
    name = f"moe{layer}"
    n0 = START[name]
    s_ = lambda s: K.sem(f"{name}_{s}")
    small_in, logits_made, exp_ready, exp_made, weights_ready, weights_turned, diag_ready = (
        s_(s) for s in ("small_in", "logits", "exp_ready", "exp_made", "weights", "weights_turned", "diag"))
    spread, spread_copied, silu_done, prod_done, hidden_done, chain = (
        s_(s) for s in ("spread", "spread_copied", "silu", "prod", "hidden", "dve"))
    with ExitStack() as stage:
        sb = lambda n, s, dt=F32: stage.enter_context(nc.sbuf_tensor(f"{name}_{n}", s, dt))
        hidden = sb("hid", [P, 2, 4, T])
        late = stage.enter_context(ExitStack())
        sb = lambda n, s, dt=F32: late.enter_context(nc.sbuf_tensor(f"{name}_{n}", s, dt))
        w_all = sb("w_all", [P, EXPERTS, T])
        gated = sb("gated", [P, 2, 512])
        prod = sb("prod", [P, 4, T])
        router = sb("router", [P, KD, EXPERTS])
        router_b = sb("router_b", [P, EXPERTS])
        diag = sb("w_diag", [P, EXPERTS, T])
        lg, pr, ex = (sb(n, [P, TT, EXPERTS]) for n in ("lg", "pr", "ex"))
        pairs = sb("pairs", [P, TT * GROUPS, 6])
        col = sb("col", [P, 8, TT])
        grp = sb("grp", [P, 4, TT, GROUPS])
        rank = sb("rank", [P, GROUPS])
        top = sb("top", [P, TT, 8])
        top_i = sb("top_i", [P, TT, 8], U32)
        top_f = sb("top_f", [P, TT, 8])
        pick = sb("pick", [P, 2, EXPERTS])
        comb = sb("comb", [P, TT, P])

        def down(pe, slot, land, e_parity, start, stop):
            pe.wait_ge(K.landed[slot], land)
            w = K.ring[:, slot, :].rearrange("p (k c) -> p k c", k=4)
            for tt in range(TT):
                for k in range(4):
                    for dh in range(2):
                        last = pe.matmul(K.bank[:, 2 * tt + dh, :], hidden[:, e_parity, k, tt * P:(tt + 1) * P],
                                         w[:, k, dh * 512:(dh + 1) * 512], start=(start and k == 0),
                                         stop=(stop and k == 3))
            last.then_inc(K.chunk_used, 1)

        def silu_gate(act, e, gate_chunks):
            act.wait_ge(K.chunk_used, gate_chunks)
            for j in range(2):
                if not (isinstance(e, int) and e == 0):
                    act.wait_ge(prod_done, 2 * e - 1 + j)
                act.activation(gated[:, j, :], K.bank[:, 4 + j, :], ACT.Silu).then_inc(silu_done, 1)

        def make_hidden(dve, e, parity, up_chunks):
            dve.wait_ge(K.chunk_used, up_chunks)
            if not (isinstance(e, int) and e == 0):
                dve.wait_ge(hidden_done, e)
            for j in range(2):
                dve.wait_ge(silu_done, 2 * e + j + 1)
                dve.tensor_tensor(prod[:, 2 * j:2 * j + 2, :], gated[:, j, :].rearrange("p (c t) -> p c t", c=2),
                                  K.bank[:, 6 + j, :].rearrange("p (c t) -> p c t", c=2), ALU.mult).then_inc(prod_done, 1)
            if isinstance(e, int) and e == 0:
                dve.wait_ge(spread_copied, 8)
            dve.wait_ge(prod_done, 2 * e + 2)
            w = w_all[:, e, :] if isinstance(e, int) else w_all[:, bass.ds(e, 1), :].rearrange("p o t -> p (o t)")
            dve.tensor_tensor(hidden[:, parity, :, :], prod[:], w.unsqueeze(1).to_broadcast([P, 4, T]),
                              ALU.mult).then_inc(hidden_done, 1)

        LOOPS = (EXPERTS - 2) // 2
        with nc.Block() as block:
            @block.sync
            def _(sp):
                sp.dma_start(router[:], K.A["router_w"]).then_inc(small_in, 16)
                sp.dma_start(router_b[:], K.A["router_b"].to_broadcast([P, EXPERTS])).then_inc(small_in, 16)
                assert K.fetched == n0 + RING
                with sp.Fori(0, LOOPS) as i:
                    for j in range(RING):
                        slot = (n0 + j) % RING
                        sp.wait_ge(K.chunk_used, 6 * i + (n0 + j + 1))
                        sp.dma_start(K.ring[:, slot, :], K.A["stream"][6 * i + (n0 + RING + j)]).then_inc(K.landed[slot], 16)
                K.fetched = n0 + RING + 6 * LOOPS
                fetch_chunks(sp, K, next_start(name) - 1 + RING)

            @block.tensor
            def _(pe):
                pe.wait_ge(small_in, 32)
                for tt in range(TT):
                    for k in range(KD):
                        last = pe.matmul(K.bank[:, 0, tt * EXPERTS:(tt + 1) * EXPERTS], K.hT[:, k, tt * P:(tt + 1) * P],
                                         router[:, k, :], start=(k == 0), stop=(k == KD - 1))
                last.then_inc(logits_made, 1)
                feature_product(pe, K, n0, K.hT, 4)
                feature_product(pe, K, n0 + 1, K.hT, 6)
                for tt in range(TT):
                    pe.wait_ge(weights_ready, tt + 1)
                    last = pe.transpose(K.bank[:, 1, tt * P:(tt + 1) * P], comb[:, tt, :], K.ident)
                last.then_inc(weights_turned, 1)
                pe.wait_ge(diag_ready, 1)
                for n in range(EXPERTS // 2):
                    if n >= 4:
                        pe.wait_ge(spread_copied, n - 3)
                    pe.matmul(K.bank[:, n % 4, :], K.ones_neg, diag[:, 2 * n:2 * n + 2, :], start=True,
                              stop=True).then_inc(spread, 1)
                pe.wait_ge(silu_done, 2)
                feature_product(pe, K, n0 + 2, K.hT, 4)
                pe.wait_ge(prod_done, 2)
                feature_product(pe, K, n0 + 3, K.hT, 6)
                pe.wait_ge(hidden_done, 1)
                pe.wait_ge(spread_copied, 8)
                down(pe, (n0 + 4) % RING, 16 * ((n0 + 4) // RING + 1), 0, True, False)
                with pe.Fori(0, LOOPS) as i:
                    for r in range(2):
                        c = n0 + 5 + 3 * r
                        slots = [(c + m) % RING for m in range(3)]
                        land = [16 * i + 16 * ((c + m) // RING + 1) for m in range(3)]
                        pe.wait_ge(silu_done, 4 * i + (4 + 2 * r))
                        feature_product(pe, K, None, K.hT, 4, slots[0], land[0])
                        pe.wait_ge(prod_done, 4 * i + (4 + 2 * r))
                        feature_product(pe, K, None, K.hT, 6, slots[1], land[1])
                        pe.wait_ge(hidden_done, 2 * i + (2 + r))
                        down(pe, slots[2], land[2], 1 - r, False, False)

            @block.scalar
            def _(act):
                act.wait_ge(exp_ready, 1)
                act.activation(ex[:], pr[:], ACT.Exp).then_inc(exp_made, 1)
                act.wait_ge(exp_ready, 2)
                act.activation(col[:, 5, :], col[:, 4, :], ACT.Exp).then_inc(exp_made, 1)
                silu_gate(act, 0, n0 + 1)
                for n in range(EXPERTS // 2):
                    act.wait_ge(spread, n + 1)
                    act.activation(w_all[:, 2 * n:2 * n + 2, :], K.bank[:, n % 4, :].rearrange("p (e t) -> p e t", e=2),
                                   ACT.Copy, scale=-1.0).then_inc(spread_copied, 1)
                silu_gate(act, 1, n0 + 3)
                with act.Fori(0, LOOPS) as i:
                    for r in range(2):
                        silu_gate(act, 2 * i + (2 + r), 6 * i + (n0 + 6 + 3 * r))

            @block.vector
            def _(dve):
                c = Chain(dve, chain)
                bc = lambda a, n: a.unsqueeze(2).to_broadcast([P, TT, n])
                c.step(dve.memset(comb[:], 0.0))
                c.step(dve.tensor_scalar(rank[:], K.iota[:, 0:GROUPS], -1.0, float(GROUPS), ALU.mult, ALU.add))
                dve.wait_ge(logits_made, 1)
                c.do(dve.tensor_tensor(lg[:], K.bank[:, 0, 0:TT * EXPERTS].rearrange("p (t e) -> p t e", t=TT),
                                       router_b[:].unsqueeze(1).to_broadcast([P, TT, EXPERTS]), ALU.add))
                c.do(dve.tensor_reduce(col[:, 0, :], lg[:], AX.X, ALU.max))
                dve.tensor_tensor(pr[:], lg[:], bc(col[:, 0, :], EXPERTS), ALU.subtract).then_inc(exp_ready, 1)
                dve.wait_ge(exp_made, 1)
                c.do(dve.tensor_reduce(col[:, 1, :], ex[:], AX.X, ALU.add))
                c.do(dve.reciprocal(col[:, 1, :], col[:, 1, :]))
                c.do(dve.tensor_tensor(pr[:], ex[:], bc(col[:, 1, :], EXPERTS), ALU.mult))
                g4 = pr[:].rearrange("p t (g e) -> p (t g) e", e=PER_GROUP)
                c.step(dve.tensor_tensor(pairs[:, :, 0:3], g4[:, :, 0:3], g4[:, :, 1:4], ALU.add))
                c.step(dve.tensor_tensor(pairs[:, :, 3:5], g4[:, :, 0:2], g4[:, :, 2:4], ALU.add))
                c.do(dve.tensor_tensor(pairs[:, :, 5:6], g4[:, :, 0:1], g4[:, :, 3:4], ALU.add))
                c.do(dve.tensor_reduce(grp[:, 0, :, :].rearrange("p t g -> p (t g)"), pairs[:], AX.X, ALU.max))
                c.do(dve.tensor_reduce(col[:, 2, :], grp[:, 0, :, :], AX.X, ALU.max))
                c.do(dve.tensor_tensor(grp[:, 1, :, :], grp[:, 0, :, :], bc(col[:, 2, :], GROUPS), ALU.is_ge))
                c.do(dve.tensor_tensor(grp[:, 2, :, :], grp[:, 1, :, :], rank[:].unsqueeze(1).to_broadcast([P, TT, GROUPS]),
                                       ALU.mult))
                c.do(dve.tensor_reduce(col[:, 3, :], grp[:, 2, :, :], AX.X, ALU.max))
                c.do(dve.tensor_tensor(grp[:, 3, :, :], grp[:, 2, :, :], bc(col[:, 3, :], GROUPS), ALU.is_equal))
                chosen = grp[:, 3, :, :].rearrange("p t g -> p (t g)").unsqueeze(2).to_broadcast([P, TT * GROUPS, PER_GROUP])
                lg4 = lg[:].rearrange("p t (g e) -> p (t g) e", e=PER_GROUP)
                pr4 = pr[:].rearrange("p t (g e) -> p (t g) e", e=PER_GROUP)
                c.do(dve.tensor_scalar(pr4, chosen, -NEG, NEG, ALU.mult, ALU.add))
                c.do(dve.tensor_tensor(lg4, lg4, chosen, ALU.mult))
                c.do(dve.tensor_tensor(lg[:], lg[:], pr[:], ALU.add))
                for tt in range(TT):
                    c.do(dve.max(top[:, tt, :], lg[:, tt, :]))
                    c.step(dve.max_index(top_i[:, tt, :], top[:, tt, :], lg[:, tt, :]))
                c.settle()
                c.do(dve.tensor_copy(top_f[:], top_i[:]))
                dve.tensor_tensor(col[:, 4, :], top[:, :, 1], top[:, :, 0], ALU.subtract).then_inc(exp_ready, 1)
                dve.wait_ge(exp_made, 2)
                c.do(dve.tensor_scalar(col[:, 6, :], col[:, 5, :], 1.0, None, ALU.add))
                c.do(dve.reciprocal(col[:, 6, :], col[:, 6, :]))
                c.do(dve.tensor_tensor(col[:, 7, :], col[:, 5, :], col[:, 6, :], ALU.mult))
                for tt in range(TT):
                    for m in range(2):
                        c.do(dve.tensor_scalar(pick[:, m, :], K.iota[:, 0:EXPERTS], top_f[:, tt, m:m + 1],
                                               col[:, 6 + m, tt:tt + 1], ALU.is_equal, ALU.mult))
                    dve.tensor_tensor(comb[:, tt, 0:EXPERTS], pick[:, 0, :], pick[:, 1, :], ALU.add).then_inc(weights_ready, 1)
                    dve.wait_ge(weights_ready, tt + 1)
                dve.wait_ge(weights_turned, 1)
                dve.tensor_tensor(diag[:], K.bank[:, 1, 0:T].unsqueeze(1).to_broadcast([P, EXPERTS, T]),
                                  K.ident[:, 0:EXPERTS].unsqueeze(2).to_broadcast([P, EXPERTS, T]),
                                  ALU.mult).then_inc(diag_ready, 1)
                make_hidden(dve, 0, 0, n0 + 2)
                make_hidden(dve, 1, 1, n0 + 4)
                with dve.Fori(0, LOOPS) as i:
                    for r in range(2):
                        make_hidden(dve, 2 * i + (2 + r), r, 6 * i + (n0 + 7 + 3 * r))
        late.close()

        def last_down(pe):
            n = next_start(name) - 1
            down(pe, n % RING, 16 * (n // RING + 1), 1, False, True)

        layer_norm_stage(K, name, 2 * layer + 1, last_down)



def sine_tables(dve, c, turns, scratch, cos_in, sin_in):
    c.do(dve.tensor_scalar(scratch, turns, ROUND, -ROUND, ALU.add, ALU.add))
    c.step(dve.tensor_tensor(sin_in, turns, scratch, ALU.subtract))
    c.do(dve.tensor_scalar(cos_in, turns, 0.25, None, ALU.add))
    c.do(dve.tensor_scalar(scratch, cos_in, ROUND, -ROUND, ALU.add, ALU.add))
    return dve.tensor_tensor(cos_in, cos_in, scratch, ALU.subtract)


def retention_stage(K):
    nc = K.nc
    n0 = START["ret_in"]
    s_ = lambda s: K.sem(f"ret_{s}")
    small_in, pos_in, turns_ready, trig_ready, chain = (s_(s) for s in ("small_in", "pos_in", "turns", "trig", "dve"))
    act_done, dve_done, swapped, rotated = (s_(s) for s in ("act_done", "dve_done", "swapped", "rotated"))
    s_made, decayed, o_made, o_copied, gn_in = (s_(s) for s in ("s_made", "decayed", "o_made", "o_copied", "gn_in"))
    var_ready, std_ready, out_ready, turned, oT_ready, gate_ready = (
        s_(s) for s in ("var", "std", "out", "turned", "oT", "gate"))
    with ExitStack() as stage:
        sb = lambda n, s, dt=F32: stage.enter_context(nc.sbuf_tensor(f"ret_{n}", s, dt))
        qkT = sb("qkT", [P, 2 * KD, T])
        heads = stage.enter_context(ExitStack())
        sb = lambda n, s, dt=F32: heads.enter_context(nc.sbuf_tensor(f"ret_{n}", s, dt))
        gate = sb("gate", [P, TT, 2 * D])
        v = sb("v", [P, TT, 2 * D])
        o = sb("o", [P, TT, 2 * D])
        decay = sb("decay", [P, RET_HEADS, 2 * P])
        scr = K.mod[:, 0:1024].rearrange("p (n c) -> p n c", n=2)
        trig = K.mod[:, 1024:1024 + 2 * T].rearrange("p (n t) -> p n t", n=2)
        freq = sb("freq", [P, 1])
        stats, mv, std = sb("stats", [P, RET_HEADS, TT, 6]), sb("mv", [P, RET_HEADS, TT, 2]), sb("std", [P, RET_HEADS, TT])
        eps = sb("eps", [P, 1])

        with nc.Block() as block:
            pos = o[:, 0, 0:T].bitcast(I32)
            ang = o[:, 0, T:2 * T]

            @block.sync
            def _(sp):
                sp.dma_start(pos, K.A["positions"].to_broadcast([P, T])).then_inc(pos_in, 16)
                sp.dma_start(freq[:], K.A["inv_freq"]).then_inc(pos_in, 16)
                sp.dma_start(decay[:], K.A["decay"]).then_inc(small_in, 16)
                sp.dma_start(o[:, 1, :], K.A["ret_gn_g"].to_broadcast([P, 2 * D])).then_inc(gn_in, 16)
                fetch_chunks(sp, K, START["ret_out"] + RING)

            @block.tensor
            def _(pe):
                for j in range(12):
                    b = 2 * j % 6
                    if j >= 3:
                        pe.wait_ge(act_done, j - 2)
                        pe.wait_ge(dve_done, j - 2)
                    if j < 4:
                        feature_product(pe, K, n0 + j, K.hT, b)
                    else:
                        token_product(pe, K, n0 + j, K.hT, [K.bank[:, b + tt, :] for tt in range(TT)])
                    if 1 <= j <= 4:
                        for i in range(2):
                            n = 2 * (j - 1) + i
                            pe.wait_ge(act_done if i == 0 else dve_done, j)
                            if n >= 2:
                                pe.wait_ge(rotated, n - 1)
                            pe.matmul(K.bank[:, 6 + n % 2, :], K.swap128, qkT[:, 2 * n:2 * n + 2, :], start=True,
                                      stop=True).then_inc(swapped, 1)

            def source(j, i):
                return K.bank[:, 2 * j % 6 + i, :]

            @block.scalar
            def _(act):
                act.wait_ge(turns_ready, 1)
                act.activation(trig, trig, ACT.Sin, scale=TWO_PI).then_inc(trig_ready, 1)
                for j in range(12):
                    act.wait_ge(K.chunk_used, n0 + j + 1)
                    if j < 4:
                        act.activation(qkT[:, 4 * j:4 * j + 2, :], source(j, 0).rearrange("p (c t) -> p c t", c=2),
                                       ACT.Copy, scale=1.0 if j < 2 else P ** -0.5).then_inc(act_done, 1)
                    elif j < 8:
                        act.activation(v[:, 0, (j - 4) * 512:(j - 3) * 512], source(j, 0), ACT.Copy).then_inc(act_done, 1)
                    else:
                        for i in range(TT):
                            last = act.activation(gate[:, i, (j - 8) * 512:(j - 7) * 512], source(j, i), ACT.Silu)
                        last.then_inc(act_done, 1)

            @block.vector
            def _(dve):
                c = Chain(dve, chain)
                c.step(dve.memset(eps[:], LN_EPS))
                dve.wait_ge(pos_in, 32)
                c.do(dve.tensor_copy(ang, pos))
                c.do(dve.tensor_scalar(ang, ang, freq[:, 0:1], 1.0 / (2.0 * np.pi), ALU.mult, ALU.mult))
                sine_tables(dve, c, ang, scr[:, 0, 0:T], trig[:, 0, :], trig[:, 1, :]).then_inc(turns_ready, 1)

                def rotate(n):
                    x = qkT[:, 2 * n:2 * n + 2, :]
                    two = lambda r: trig[:, r, :].unsqueeze(1).to_broadcast([P, 2, T])
                    s2 = scr[:, n % 2, :].rearrange("p (c t) -> p c t", c=2)
                    dve.wait_ge(swapped, n + 1)
                    c.step(dve.tensor_tensor(s2, K.bank[:, 6 + n % 2, :].rearrange("p (c t) -> p c t", c=2), two(1), ALU.mult))
                    c.do(dve.tensor_tensor(x, x, two(0), ALU.mult))
                    dve.tensor_tensor(x, x, s2, ALU.add).then_inc(rotated, 1)

                for j in range(12):
                    if j == 1:
                        dve.wait_ge(trig_ready, 1)
                    dve.wait_ge(K.chunk_used, n0 + j + 1)
                    if j < 4:
                        dve.tensor_scalar(qkT[:, 4 * j + 2:4 * j + 4, :], source(j, 1).rearrange("p (c t) -> p c t", c=2),
                                          1.0 if j < 2 else P ** -0.5, None, ALU.mult).then_inc(dve_done, 1)
                    elif j < 8:
                        dve.tensor_copy(v[:, 1, (j - 4) * 512:(j - 3) * 512], source(j, 1)).then_inc(dve_done, 1)
                    else:
                        dve.wait_ge(act_done, j + 1)
                        dve.wait_ge(gn_in, 16)
                        cols = slice((j - 8) * 512, (j - 7) * 512)
                        dve.tensor_tensor(gate[:, :, cols], gate[:, :, cols],
                                          o[:, 1, cols].unsqueeze(1).to_broadcast([P, TT, 512]), ALU.mult).then_inc(dve_done, 1)
                    if 1 <= j <= 4:
                        rotate(2 * (j - 1))
                        rotate(2 * (j - 1) + 1)

        W = T + P
        with nc.Block() as block:
            sbank = lambda h: K.bank[:, h % 2, 0:W]
            obank = lambda h: K.bank[:, 2 + h % 2, :]
            s_b = scr[:, :, 0:W]

            @block.tensor
            def _(pe):
                for i in range(RET_HEADS + 1):
                    if i < RET_HEADS:
                        if i >= 2:
                            pe.wait_ge(decayed, i - 1)
                        qT, kT = qkT[:, i, :], qkT[:, KD + i, :]
                        pe.matmul(sbank(i)[:, 0:T], kT[:, 0:P], qT, start=True, stop=True)
                        pe.matmul(sbank(i)[:, T:W], kT[:, P:T], qT[:, P:T], start=True, stop=True).then_inc(s_made, 1)
                    h = i - 1
                    if h >= 0:
                        if h >= 2:
                            pe.wait_ge(o_copied, h - 1)
                        pe.wait_ge(decayed, h + 1)
                        s, vh = s_b[:, h % 2, :], v[:, :, h * RET_V:(h + 1) * RET_V]
                        pe.matmul(obank(h)[:, 0:RET_V], s[:, 0:P], vh[:, 0, :], start=True, stop=True)
                        pe.matmul(obank(h)[:, RET_V:], s[:, P:T], vh[:, 0, :], start=True, stop=False)
                        pe.matmul(obank(h)[:, RET_V:], s[:, T:W], vh[:, 1, :], start=False, stop=True).then_inc(o_made, 1)

            @block.scalar
            def _(act):
                for h in range(RET_HEADS):
                    act.wait_ge(o_made, h + 1)
                    act.activation(o[:, :, h * RET_V:(h + 1) * RET_V], obank(h).rearrange("p (t e) -> p t e", t=TT),
                                   ACT.Copy).then_inc(o_copied, 1)
                act.wait_ge(var_ready, 1)
                act.activation(std[:], mv[:, :, :, 1], ACT.Sqrt, bias=eps[:]).then_inc(std_ready, 1)

            @block.vector
            def _(dve):
                c = Chain(dve, K.sem("ret_dve2"))
                dve.wait_ge(small_in, 16)
                for i in range(RET_HEADS + 1):
                    if i < RET_HEADS:
                        dve.wait_ge(s_made, i + 1)
                        if i >= 2:
                            dve.wait_ge(o_made, i - 1)
                        s = s_b[:, i % 2, :]
                        dve.tensor_tensor(s[:, 0:T], sbank(i)[:, 0:T], decay[:, i, :], ALU.mult)
                        dve.tensor_tensor(s[:, T:W], sbank(i)[:, T:W], decay[:, i, 0:P], ALU.mult).then_inc(decayed, 1)
                    h = i - 1
                    if h >= 0:
                        dve.wait_ge(o_copied, h + 1)
                        for tt in range(TT):
                            c.step(dve.bn_stats(stats[:, h, tt, :], o[:, tt, h * RET_V:(h + 1) * RET_V]))
                c.settle()
                for h in range(RET_HEADS):
                    for tt in range(TT):
                        last = c.step(dve.bn_aggr(mv[:, h, tt, :], stats[:, h, tt, :]))
                c.settle()
                dve.sem_inc(var_ready, 1)
                dve.wait_ge(std_ready, 1)
                c.do(dve.reciprocal(std[:], std[:]))
                for h in range(RET_HEADS):
                    cols = slice(h * RET_V, (h + 1) * RET_V)
                    for tt in range(TT):
                        c.step(dve.tensor_scalar(o[:, tt, cols], o[:, tt, cols], mv[:, h, tt, 0:1], std[:, h, tt:tt + 1],
                                                 ALU.subtract, ALU.mult))
                    c.settle()
                    dve.tensor_tensor(o[:, :, cols], o[:, :, cols], gate[:, :, cols], ALU.mult).then_inc(out_ready, 1)

        with nc.Block() as block:
            @block.tensor
            def _(pe):
                for k in range(2 * KD):
                    if k >= 16:
                        pe.wait_ge(oT_ready, k // 2 - 7)
                    for tt in range(TT):
                        out = K.bank[:, k // 2 % 8, (k % 2) * T + tt * P:(k % 2) * T + (tt + 1) * P]
                        last = pe.transpose(out, o[:, tt, k * P:(k + 1) * P], K.ident)
                    if k % 2:
                        last.then_inc(turned, 1)

            @block.scalar
            def _(act):
                for b in range(0, 8, 2):
                    act.wait_ge(turned, b + 1)
                    act.activation(qkT[:, 2 * b:2 * b + 2, :], K.bank[:, b, :].rearrange("p (k t) -> p k t", k=2), ACT.Copy)

            @block.vector
            def _(dve):
                for b in range(1, 8, 2):
                    dve.wait_ge(turned, b + 1)
                    dve.tensor_copy(qkT[:, 2 * b:2 * b + 2, :], K.bank[:, b, :].rearrange("p (k t) -> p k t", k=2))
        heads.close()

        def project(pe):
            for dh in range(2):
                for r in range(2):
                    token_product(pe, K, START["ret_out"] + 2 * dh + r, qkT[:, r * KD:(r + 1) * KD, :],
                                  [K.bank[:, 2 * tt + dh, :] for tt in range(TT)], start=(r == 0), stop=(r == 1))
        layer_norm_stage(K, "ret_out", 2, project)



def rms_norm_turn_stage(K, name, gain, before=None, keep=None, out=None):
    nc = K.nc
    row_in, chain, ss_ready, std_ready, h_ready, turned, evac = (
        K.sem(f"{name}_{s}") for s in ("row_in", "dve", "ss", "std", "h", "turned", "evac"))
    with ExitStack() as stage, nc.Block() as block:
        sb = lambda n, s: stage.enter_context(nc.sbuf_tensor(f"{name}_{n}", s, F32))
        g_row, h = sb("g", [P, D]), sb("hbuf", [P, TT, D])
        ss, eps = sb("ss", [P, TT]), sb("eps", [P, 1])

        @block.sync
        def _(sp):
            sp.dma_start(g_row[:], K.A[gain].to_broadcast([P, D])).then_inc(row_in, 16)
            if out is not None:
                sp.wait_ge(h_ready, TT)
                sp.dma_start(out, h[:]).then_inc(K.stored, 16)
                sp.wait_ge(K.stored, 16)

        @block.scalar
        def _(act):
            for tt in range(TT):
                act.wait_ge(ss_ready, tt + 1)
                act.activation(h[:, tt, :], K.x[:, tt, :], ACT.Square, accum_out=ss[:, tt:tt + 1]).then_inc(std_ready, 1)
            act.wait_ge(std_ready, TT)
            act.activation(ss[:], ss[:], ACT.Sqrt, bias=eps[:], scale=1.0 / D).then_inc(std_ready, 1)
            if out is None:
                evacuate_turned(act, K, turned, evac)

        if out is None:
            @block.tensor
            def _(pe):
                turn_tokens(pe, K, h, h_ready, turned)

        @block.vector
        def _(dve):
            c = Chain(dve, chain)
            c.do(dve.memset(eps[:], RMS_EPS))
            for tt in range(TT):
                if before is not None:
                    before(dve, c, tt)
                    c.settle()
                dve.sem_inc(ss_ready, 1)
            dve.wait_ge(std_ready, TT + 1)
            c.do(dve.reciprocal(ss[:], ss[:]))
            dve.wait_ge(row_in, 16)
            for tt in range(TT):
                dve.scalar_tensor_tensor(h[:, tt, :], K.x[:, tt, :], ss[:, tt:tt + 1], g_row[:], ALU.mult,
                                         ALU.mult).then_inc(h_ready, 1)


def second_projection_stage(K, S):
    nc = K.nc
    n0 = START["in2"]
    act_done, dve_done, swapped, rotated, rope_in, zeroed, chain = (
        K.sem(f"in2_{s}") for s in ("act_done", "dve_done", "swapped", "rotated", "rope_in", "zeroed", "dve"))
    with ExitStack() as stage, nc.Block() as block:
        sb = lambda n, s: stage.enter_context(nc.sbuf_tensor(f"in2_{n}", s, F32))
        rope = sb("rope", [P, 2, 2, T])
        kT = sb("kT", [P, 2, T])
        scr = sb("scr", [P, 2, 2, T])

        @block.sync
        def _(sp):
            sp.dma_start(rope[:, 0, :, :], K.A["rope64"]).then_inc(rope_in, 16)
            sp.dma_start(rope[:, 1, :, :], K.A["rope32"]).then_inc(rope_in, 16)
            fetch_chunks(sp, K, next_start("in2") + RING)

        @block.gpsimd
        def _(pool):
            pool.memset(S.kz[:], 0.0).then_inc(zeroed, 1)
            pool.memset(S.kiz[:], 0.0).then_inc(zeroed, 1)
            pool.memset(S.vz[:], 0.0).then_inc(zeroed, 1)

        def pair(n):
            return [S.qT[:, 0:2, :], S.qT[:, 2:4, :], kT[:], S.qiT[:]][n]

        @block.tensor
        def _(pe):
            def swap(n, wait, count):
                pe.wait_ge(wait, count)
                if n >= 2:
                    pe.wait_ge(rotated, n - 1)
                out = K.bank[:, 6 + n % 2, :]
                if n == 2:
                    pe.matmul(out[:, 0:T], K.swap64, kT[:, 0, :], start=True, stop=True)
                    pe.matmul(out[:, T:], K.swap32, kT[:, 1, :], start=True, stop=True).then_inc(swapped, 1)
                else:
                    pe.matmul(out, K.swap32 if n == 3 else K.swap64, pair(n), start=True, stop=True).then_inc(swapped, 1)

            for j in range(8):
                b = 2 * j % 6
                if j >= 3:
                    pe.wait_ge(act_done, j - 2)
                    pe.wait_ge(dve_done, j - 2)
                if j < 3:
                    feature_product(pe, K, n0 + j, K.hT, b)
                else:
                    cols = 136 if j == 3 else COLS
                    token_product(pe, K, n0 + j, K.hT, [K.bank[:, b + tt, 0:cols] for tt in range(TT)], cols=cols)
                if j == 2:
                    swap(0, act_done, 2)
                    swap(1, dve_done, 2)
                if j == 3:
                    pe.wait_ge(act_done, 3)
                    swap(2, dve_done, 3)
                    swap(3, dve_done, 3)

        def source(j, i):
            return K.bank[:, 2 * j % 6 + i, :]

        tiles = lambda a: a.rearrange("p (c t) -> p c t", c=2)

        @block.scalar
        def _(act):
            for j in range(8):
                act.wait_ge(K.chunk_used, n0 + j + 1)
                if j < 2:
                    dst = S.uT[:, 0:2, :] if j == 0 else S.qT[:, 0:2, :]
                    act.activation(dst, tiles(source(j, 0)), ACT.Copy).then_inc(act_done, 1)
                elif j == 2:
                    act.activation(kT[:, 0, :], source(j, 0)[:, 0:T], ACT.Copy)
                    act.activation(S.qiT[:, 0, :], source(j, 0)[:, T:], ACT.Copy).then_inc(act_done, 1)
                elif j == 3:
                    act.wait_ge(zeroed, 3)
                    v = source(j, 0)
                    act.activation(S.vz[:, 0, 0, 0:64], v[:, 0:64], ACT.Copy)
                    act.activation(S.vz[:, 1, 0, 64:P], v[:, 64:P], ACT.Copy)
                    act.activation(S.wi[:, 0, :], v[:, P:136], ACT.Copy, scale=IDX_SCALE).then_inc(act_done, 1)
                else:
                    gate = S.gates[:, (j - 4) // 2, :, (j % 2) * COLS:(j % 2 + 1) * COLS]
                    for i in range(TT):
                        last = act.activation(gate[:, i, :], source(j, i), ACT.Sigmoid)
                    last.then_inc(act_done, 1)

        @block.vector
        def _(dve):
            c = Chain(dve, chain)

            def rotate(n):
                x, s2 = pair(n), scr[:, n % 2, :, :]
                which = rope[:, 1 if n == 3 else 0, :, :]
                two = lambda r: which[:, r, :].unsqueeze(1).to_broadcast([P, 2, T])
                if n == 2:
                    two = lambda r: rope[:, :, r, :]
                dve.wait_ge(swapped, n + 1)
                c.step(dve.tensor_tensor(s2, tiles(K.bank[:, 6 + n % 2, :]), two(1), ALU.mult))
                c.do(dve.tensor_tensor(x, x, two(0), ALU.mult))
                if n != 2:
                    dve.tensor_tensor(x, x, s2, ALU.add).then_inc(rotated, 1)
                    return
                dve.wait_ge(zeroed, 3)
                for h in range(2):
                    r = slice(64 * h, 64 * h + 64)
                    c.step(dve.tensor_tensor(S.kz[r, h, :], kT[r, 0, :], s2[r, 0, :], ALU.add))
                for h in range(4):
                    r = slice(32 * h, 32 * h + 32)
                    last = dve.tensor_tensor(S.kiz[r, h, :], kT[r, 1, :], s2[r, 1, :], ALU.add)
                last.then_inc(rotated, 1)

            dve.wait_ge(rope_in, 32)
            for j in range(8):
                dve.wait_ge(K.chunk_used, n0 + j + 1)
                if j < 2:
                    dst = S.uT[:, 2:4, :] if j == 0 else S.qT[:, 2:4, :]
                    dve.tensor_copy(dst, tiles(source(j, 1))).then_inc(dve_done, 1)
                elif j == 2:
                    c.step(dve.tensor_copy(S.qiT[:, 1, :], source(j, 1)[:, 0:T]))
                    dve.tensor_copy(kT[:, 1, :], source(j, 1)[:, T:]).then_inc(dve_done, 1)
                elif j == 3:
                    dve.wait_ge(zeroed, 3)
                    v = source(j, 1)
                    c.step(dve.tensor_copy(S.vz[:, 0, 1, 0:64], v[:, 0:64]))
                    c.step(dve.tensor_copy(S.vz[:, 1, 1, 64:P], v[:, 64:P]))
                    dve.tensor_scalar(S.wi[:, 1, :], v[:, P:136], IDX_SCALE, None, ALU.mult).then_inc(dve_done, 1)
                    for n in range(4):
                        rotate(n)
                else:
                    dve.sem_inc(dve_done, 1)



S5_TILES = 16


def s5_stage(K, S):
    nc = K.nc
    s_ = lambda s: K.sem(f"s5_{s}")
    small_in, chain, trig_ready, trig_done, b_ready, turned, b_copied = (
        s_(s) for s in ("small_in", "dve", "trig_ready", "trig_done", "b_ready", "turned", "b_copied"))
    bu_made, w_used, s_ready, y_made, y_taken, tab_ready, tab_done = (
        s_(s) for s in ("bu_made", "w_used", "s_ready", "y_made", "y_taken", "tab_ready", "tab_done"))
    NT = S5_TILES
    with ExitStack() as stage, nc.Block() as block:
        sb = lambda n, s: stage.enter_context(nc.sbuf_tensor(f"s5_{n}", s, F32))
        par = sb("par", [P, 3, NT])
        col = sb("col", [P, 16, NT])
        b_in = sb("b_in", [P, 2, NT, 16])
        b_bar = sb("b_bar", [P, 2, NT, 16])
        b_pad = sb("b_pad", [P, 2, P])
        bT = sb("bT", [P, 2, 2, P])
        cz = sb("cz", [P, 2, NT, P])
        d_skip = sb("d_skip", [P, 4])
        tab = sb("tab", [P, 2, 2, T])
        turns = sb("turns", [P, 2, T])
        w, m, st = (K.mod[:, i * D:(i + 1) * D].rearrange("p (a b t) -> p a b t", a=2, b=2) for i in range(3))
        y = S.yT

        @block.sync
        def _(sp):
            for i, n in enumerate(("a_re", "a_im", "log_dt")):
                sp.dma_start(par[:, i, :], K.A[n]).then_inc(small_in, 16)
            sp.dma_start(b_in[:, 0, :, :], K.A["b_re"]).then_inc(small_in, 16)
            sp.dma_start(b_in[:, 1, :, :], K.A["b_im"]).then_inc(small_in, 16)
            sp.dma_start(d_skip[:], K.A["d_skip"]).then_inc(small_in, 16)
            sp.dma_start(cz[:, 0, :, :], K.A["c_re"]).then_inc(small_in, 16)
            sp.dma_start(cz[:, 1, :, :], K.A["c_im"]).then_inc(small_in, 16)

        @block.scalar
        def _(act):
            act.wait_ge(trig_ready, 1)
            act.activation(col[:, 0, :], par[:, 2, :], ACT.Exp).then_inc(trig_done, 1)
            act.wait_ge(trig_ready, 2)
            act.activation(col[:, 2, :], col[:, 1, :], ACT.Exp).then_inc(trig_done, 1)
            act.activation(col[:, 12:14, :], col[:, 6:8, :], ACT.Sin, scale=TWO_PI).then_inc(trig_done, 1)
            for j in range(NT):
                act.wait_ge(tab_ready, j + 1)
                act.activation(tab[:, j % 2, :, :], tab[:, j % 2, :, :], ACT.Sin, scale=TWO_PI).then_inc(tab_done, 1)
                act.wait_ge(turned, j + 1)
                if j >= 2:
                    act.wait_ge(bu_made, j - 1)
                act.activation(bT[:, j % 2, :, :], K.bank[:, j % 2, 0:2 * P].rearrange("p (r s) -> p r s", r=2),
                               ACT.Copy).then_inc(b_copied, 1)

        def outputs(pe, j):
            pe.wait_ge(s_ready, j + 1)
            if j % 4 == 0 and j >= 8:
                pe.wait_ge(y_taken, j // 4 - 1)
            out = K.bank[:, 4 + j // 4 % 2, 0:T]
            pe.matmul(out, cz[:, 0, j, :], st[:, j % 2, 0, :], start=(j % 4 == 0), stop=False)
            pe.matmul(out, cz[:, 1, j, :], st[:, j % 2, 1, :], start=False, stop=(j % 4 == 3)).then_inc(y_made, 1)

        @block.tensor
        def _(pe):
            for j in range(NT):
                pe.wait_ge(b_ready, j + 1)
                if j >= 2:
                    pe.wait_ge(b_copied, j - 1)
                for r in range(2):
                    last = pe.transpose(K.bank[:, j % 2, r * P:(r + 1) * P], b_pad[:, r, :], K.ident)
                last.then_inc(turned, 1)
                pe.wait_ge(b_copied, j + 1)
                if j >= 2:
                    pe.wait_ge(w_used, j - 1)
                for r in range(2):
                    last = pe.matmul(K.bank[:, 2 + j % 2, r * T:(r + 1) * T], bT[:, j % 2, r, :], S.uT[:, j // 4, :],
                                     start=True, stop=True)
                last.then_inc(bu_made, 1)
                if j >= 1:
                    outputs(pe, j - 1)
            outputs(pe, NT - 1)

        def take(dve, c, n):
            dve.wait_ge(y_made, 4 * n + 4)
            dve.scalar_tensor_tensor(y[:, n, :], S.uT[:, n, :], d_skip[:, n:n + 1], K.bank[:, 4 + n % 2, 0:T],
                                     ALU.mult, ALU.add).then_inc(y_taken, 1)

        @block.vector
        def _(dve):
            c = Chain(dve, chain)
            C = lambda i: col[:, i, :]
            tt = lambda out, a, b, op: c.do(dve.tensor_tensor(out, a, b, op))
            dve.wait_ge(small_in, 16 * 8)
            dve.sem_inc(trig_ready, 1)
            dve.wait_ge(trig_done, 1)
            tt(C(1), par[:, 0, :], C(0), ALU.mult)
            tt(C(3), par[:, 1, :], C(0), ALU.mult)
            c.do(dve.tensor_scalar(C(3), C(3), 1.0 / (2.0 * np.pi), None, ALU.mult))
            sine_tables(dve, c, C(3), C(4), C(6), C(7)).then_inc(trig_ready, 1)
            dve.wait_ge(trig_ready, 2)
            theta = col[:, 7, :]
            c.step(dve.memset(b_pad[:], 0.0))
            dve.wait_ge(trig_done, 3)
            tt(C(12), C(12), C(2), ALU.mult)
            tt(C(13), C(13), C(2), ALU.mult)
            c.do(dve.tensor_scalar(C(12), C(12), -1.0, None, ALU.add))
            tt(C(8), par[:, 0, :], par[:, 0, :], ALU.mult)
            tt(C(9), par[:, 1, :], par[:, 1, :], ALU.mult)
            tt(C(8), C(8), C(9), ALU.add)
            c.do(dve.reciprocal(C(8), C(8)))
            tt(C(9), C(12), par[:, 0, :], ALU.mult)
            tt(C(10), C(13), par[:, 1, :], ALU.mult)
            tt(C(9), C(9), C(10), ALU.add)
            tt(C(10), C(13), par[:, 0, :], ALU.mult)
            tt(C(11), C(12), par[:, 1, :], ALU.mult)
            tt(C(10), C(10), C(11), ALU.subtract)
            tt(C(9), C(9), C(8), ALU.mult)
            tt(C(10), C(10), C(8), ALU.mult)
            wide = lambda i: C(i).unsqueeze(2).to_broadcast([P, NT, 16])
            scratch = m[:, 0, 0, :].rearrange("p (j n) -> p j n", j=NT)
            for out, a, b, op in ((0, 9, 10, ALU.subtract), (1, 10, 9, ALU.add)):
                tt(b_bar[:, out, :, :], b_in[:, 0, :, :], wide(a), ALU.mult)
                tt(scratch, b_in[:, 1, :, :], wide(b), ALU.mult)
                tt(b_bar[:, out, :, :], b_bar[:, out, :, :], scratch, op)
            c.do(dve.tensor_scalar(cz[:, 1, :, :], cz[:, 1, :, :], -1.0, None, ALU.mult))

            def table(j):
                if j >= 2:
                    c.settle()
                c.do(dve.tensor_scalar(turns[:, 0, 0:P], K.iota, theta[:, j:j + 1], None, ALU.mult))
                c.do(dve.tensor_scalar(turns[:, 0, P:T], K.iota, float(P), theta[:, j:j + 1], ALU.add, ALU.mult))
                sine_tables(dve, c, turns[:, 0, :], turns[:, 1, :], tab[:, j % 2, 0, :], tab[:, j % 2, 1, :]).then_inc(tab_ready, 1)
                dve.wait_ge(tab_ready, j + 1)

            def pad_b(j):
                if j >= 1:
                    dve.wait_ge(turned, j)
                    old = 32 * ((j - 1) % 4)
                    c.do(dve.memset(b_pad[:, :, old:old + 32], 0.0))
                at = 32 * (j % 4)
                for half in range(2):
                    r = slice(64 * half, 64 * half + 64)
                    last = dve.tensor_copy(b_pad[r, :, at + 16 * half:at + 16 * half + 16], b_bar[r, :, j, :])
                    if half == 0:
                        c.step(last)
                last.then_inc(b_ready, 1)
                dve.wait_ge(b_ready, j + 1)

            table(0)
            pad_b(0)
            for j in range(NT):
                if j + 1 < NT:
                    pad_b(j + 1)
                    table(j + 1)
                dve.wait_ge(bu_made, j + 1)
                dve.wait_ge(tab_done, j + 1)
                bu = K.bank[:, 2 + j % 2, :].rearrange("p (r t) -> p r t", r=2)
                two = lambda i: tab[:, j % 2, i, :].unsqueeze(1).to_broadcast([P, 2, T])
                c.step(dve.tensor_tensor(w[:, 0, :, :], bu, two(0), ALU.mult))
                dve.tensor_tensor(m[:, 0, :, :], bu, two(1), ALU.mult).then_inc(w_used, 1)
                c.settle()
                dve.wait_ge(w_used, j + 1)
                c.step(dve.tensor_tensor(w[:, 0, 0, :], w[:, 0, 0, :], m[:, 0, 1, :], ALU.add))
                c.do(dve.tensor_tensor(w[:, 0, 1, :], w[:, 0, 1, :], m[:, 0, 0, :], ALU.subtract))
                decay = col[:, 2, j:j + 1].to_broadcast([P, T])
                for r in range(2):
                    c.step(dve.tensor_tensor_scan(w[:, 1, r, :], decay, w[:, 0, r, :], 0.0, ALU.mult, ALU.add))
                c.settle()
                c.step(dve.tensor_tensor(m[:, 0, :, :], w[:, 1, :, :], two(0), ALU.mult))
                c.do(dve.tensor_tensor(m[:, 1, :, :], w[:, 1, :, :], two(1), ALU.mult))
                if j >= 2:
                    dve.wait_ge(y_made, j - 1)
                c.step(dve.tensor_tensor(st[:, j % 2, 0, :], m[:, 0, 0, :], m[:, 1, 1, :], ALU.subtract))
                c.settle()
                dve.tensor_tensor(st[:, j % 2, 1, :], m[:, 0, 1, :], m[:, 1, 0, :], ALU.add).then_inc(s_ready, 1)
                dve.wait_ge(s_ready, j + 1)
                if j % 4 == 3 and j >= 7:
                    take(dve, c, j // 4 - 1)
            take(dve, c, 3)



SEL = 64
TAKEN = -3e38


def sparse_attention_stage(K, S):
    nc = K.nc
    s_ = lambda s: K.sem(f"dsa_{s}")
    idx_made, relu_done, score_ready, score_masked, pick_ready, pick_masked, chain = (
        s_(s) for s in ("idx_made", "relu", "score", "score_masked", "pick", "pick_masked", "dve"))
    l_made, l_used, max_ready, exp_done, p_ready, turned, pT_ready, o_made, o_copied = (
        s_(s) for s in ("l_made", "l_used", "max", "exp", "p", "turned", "pT", "o_made", "o_copied"))
    with ExitStack() as stage, nc.Block() as block:
        sb = lambda n, s, dt=F32: stage.enter_context(nc.sbuf_tensor(f"dsa_{n}", s, dt))
        rel = sb("rel", [P, 2, 2, T])
        score = sb("score", [P, TT, T])
        work = sb("work", [P, T])
        top = sb("top", [P, 8])
        bias = sb("bias", [P, TT, T])
        lg = sb("lg", [P, 2, 2, T])
        mx, total = sb("mx", [P, 2, 2]), sb("total", [P, 2, 2])
        pT = sb("pT", [P, 2, 4, P])
        units = [(tt, j) for tt in range(TT) for j in range(4)]

        @block.tensor
        def _(pe):
            n = 0
            for tt in range(TT):
                for pair in range(4):
                    if n >= 2:
                        pe.wait_ge(relu_done, n - 1)
                    for r in range(2):
                        h = 2 * pair + r
                        last = pe.matmul(K.bank[:, 6 + n % 2, r * T:r * T + (tt + 1) * P],
                                         S.qiT[:, h // 4, tt * P:(tt + 1) * P], S.kiz[:, h % 4, 0:(tt + 1) * P],
                                         start=True, stop=True)
                    last.then_inc(idx_made, 1)
                    n += 1

            def logits(n):
                tt, j = units[n]
                if n >= 2:
                    pe.wait_ge(l_used, n - 1)
                for h in range(2):
                    last = pe.matmul(K.bank[:, n % 2, h * T:h * T + (tt + 1) * P], S.qT[:, j, tt * P:(tt + 1) * P],
                                     S.kz[:, h, 0:(tt + 1) * P], start=True, stop=True)
                last.then_inc(l_made, 1)

            def turn(n):
                tt, j = units[n]
                pe.wait_ge(p_ready, n + 1)
                if n >= 2:
                    pe.wait_ge(pT_ready, n - 1)
                for h in range(2):
                    for kt in range(tt + 1):
                        m = h * (tt + 1) + kt
                        last = pe.transpose(K.bank[:, 2 + n % 2, m * P:(m + 1) * P], lg[:, n % 2, h, kt * P:(kt + 1) * P],
                                            K.ident)
                last.then_inc(turned, 1)

            def values(n):
                tt, j = units[n]
                pe.wait_ge(pT_ready, n + 1)
                if n >= 2:
                    pe.wait_ge(o_copied, n - 1)
                parts = [(h, kt) for h in range(2) for kt in range(tt + 1)]
                for m, (h, kt) in enumerate(parts):
                    last = pe.matmul(K.bank[:, 4 + n % 2, 0:P], S.vz[:, h, kt, :], pT[:, n % 2, m, :],
                                     start=(m == 0), stop=(m == len(parts) - 1))
                last.then_inc(o_made, 1)

            for i in range(len(units) + 2):
                if i < len(units):
                    logits(i)
                if 1 <= i <= len(units):
                    turn(i - 1)
                if i >= 2:
                    values(i - 2)

        @block.scalar
        def _(act):
            n = 0
            for tt in range(TT):
                for pair in range(4):
                    act.wait_ge(idx_made, n + 1)
                    if n >= 2:
                        act.wait_ge(score_ready, n - 1)
                    w = (tt + 1) * P
                    act.activation(rel[:, n % 2, :, 0:w], K.bank[:, 6 + n % 2, :].rearrange("p (h s) -> p h s", h=2)[:, :, 0:w],
                                   ACT.Relu).then_inc(relu_done, 1)
                    n += 1
            for n, (tt, j) in enumerate(units):
                act.wait_ge(max_ready, n + 1)
                w = (tt + 1) * P
                for h in range(2):
                    last = act.activation(lg[:, n % 2, h, 0:w], lg[:, n % 2, h, 0:w], ACT.Exp, bias=mx[:, n % 2, h:h + 1],
                                          accum_out=total[:, n % 2, h:h + 1])
                    if h == 0:
                        last.then_inc(exp_done, 1)
                last.then_inc(exp_done, 1)
                act.wait_ge(turned, n + 1)
                if n >= 2:
                    act.wait_ge(o_made, n - 1)
                act.activation(pT[:, n % 2, 0:2 * (tt + 1), :],
                               K.bank[:, 2 + n % 2, 0:2 * w].rearrange("p (m t) -> p m t", t=P), ACT.Copy).then_inc(pT_ready, 1)

        @block.gpsimd
        def _(pool):
            for tt in range(TT):
                own = slice(tt * P, (tt + 1) * P)
                pool.wait_ge(score_ready, 4 * (tt + 1))
                pool.affine_select(out=score[:, tt, own], in_=score[:, tt, own], compare_op=ALU.is_ge, fill=NEG, base=0,
                                   pattern=[[-1, P]], channel_multiplier=1).then_inc(score_masked, 1)
                pool.wait_ge(pick_ready, tt + 1)
                pool.affine_select(out=bias[:, tt, own], in_=bias[:, tt, own], compare_op=ALU.is_ge, fill=NEG, base=0,
                                   pattern=[[-1, P]], channel_multiplier=1).then_inc(pick_masked, 1)

        @block.vector
        def _(dve):
            c = Chain(dve, chain)
            n = 0
            for tt in range(TT):
                w = (tt + 1) * P
                for pair in range(4):
                    dve.wait_ge(relu_done, n + 1)
                    for r in range(2):
                        h = 2 * pair + r
                        x, wi = rel[:, n % 2, r, 0:w], S.wi[:, tt, h:h + 1]
                        if h == 0:
                            c.do(dve.tensor_scalar(score[:, tt, 0:w], x, wi, None, ALU.mult))
                            continue
                        last = dve.scalar_tensor_tensor(score[:, tt, 0:w], x, wi, score[:, tt, 0:w], ALU.mult, ALU.add)
                        if r == 0:
                            c.do(last)
                    last.then_inc(score_ready, 1)
                    dve.wait_ge(score_ready, n + 1)
                    n += 1
            for tt in range(TT):
                w = (tt + 1) * P
                dve.wait_ge(score_masked, tt + 1)
                src = score[:, tt, 0:w]
                for r in range(SEL // 8):
                    c.do(dve.max(top[:], src))
                    c.do(dve.match_replace(work[:, 0:w], top[:], src, TAKEN))
                    src = work[:, 0:w]
                c.do(dve.tensor_scalar(work[:, 0:w], work[:, 0:w], 0.5 * TAKEN, -NEG, ALU.is_lt, ALU.mult))
                dve.tensor_scalar(bias[:, tt, 0:w], work[:, 0:w], NEG, None, ALU.add).then_inc(pick_ready, 1)
                dve.wait_ge(pick_ready, tt + 1)

            def scores(n):
                tt, j = units[n]
                w = (tt + 1) * P
                if j == 0:
                    dve.wait_ge(pick_masked, tt + 1)
                dve.wait_ge(l_made, n + 1)
                if n >= 2:
                    dve.wait_ge(turned, n - 1)
                x = lg[:, n % 2, :, 0:w]
                dve.scalar_tensor_tensor(x, K.bank[:, n % 2, :].rearrange("p (h s) -> p h s", h=2)[:, :, 0:w], 0.125,
                                         bias[:, tt, 0:w].unsqueeze(1).to_broadcast([P, 2, w]), ALU.mult,
                                         ALU.add).then_inc(l_used, 1)
                dve.wait_ge(l_used, n + 1)
                c.do(dve.tensor_reduce(mx[:, n % 2, :], x, AX.X, ALU.max))
                dve.tensor_scalar(mx[:, n % 2, :], mx[:, n % 2, :], -1.0, None, ALU.mult).then_inc(max_ready, 1)

            def divide(n):
                tt, j = units[n]
                w = (tt + 1) * P
                dve.wait_ge(exp_done, 2 * n + 2)
                c.do(dve.reciprocal(total[:, n % 2, :], total[:, n % 2, :]))
                x = lg[:, n % 2, :, 0:w]
                dve.tensor_tensor(x, x, total[:, n % 2, :].unsqueeze(2).to_broadcast([P, 2, w]), ALU.mult).then_inc(p_ready, 1)

            def take(n):
                tt, j = units[n]
                dve.wait_ge(o_made, n + 1)
                dve.tensor_copy(S.yaT[:, j, tt * P:(tt + 1) * P], K.bank[:, 4 + n % 2, 0:P]).then_inc(o_copied, 1)

            for i in range(len(units) + 2):
                if i < len(units):
                    scores(i)
                if 1 <= i <= len(units):
                    divide(i - 1)
                if i >= 2:
                    take(i - 2)



def join_stage(K, S):
    nc = K.nc
    s_ = lambda s: K.sem(f"join_{s}")
    gelu_done, sig_done, y_ready, chain, m_ready, turned, evac = (
        s_(s) for s in ("gelu", "sig", "y", "dve", "m", "turned", "evac"))
    with ExitStack() as stage, nc.Block() as block:
        sig = stage.enter_context(nc.sbuf_tensor("join_sig", [P, 4, T], F32))
        n_glu, n_ssm, n_attn, n_out = (START[n] for n in ("w_glu", "ssm_up", "attn_up", "w_out2"))

        @block.sync
        def _(sp):
            fetch_chunks(sp, K, next_start("w_out2") + RING)

        @block.scalar
        def _(act):
            act.activation(S.yT[:], S.yT[:], ACT.Gelu_apprx_tanh).then_inc(gelu_done, 1)
            act.wait_ge(K.chunk_used, n_glu + 1)
            act.activation(sig[:], K.bank[:, 0:2, :].rearrange("p b (c t) -> p (b c) t", c=2), ACT.Sigmoid).then_inc(sig_done, 1)
            evacuate_turned(act, K, turned, evac)

        @block.tensor
        def _(pe):
            pe.wait_ge(gelu_done, 1)
            wait_chunk(pe, K, n_glu)
            w = K.ring[:, n_glu % RING, 0:4 * 512].rearrange("p (k c) -> p k c", k=4)
            for i in range(4):
                for k in range(4):
                    last = pe.matmul(K.bank[:, i // 2, (i % 2) * T:(i % 2 + 1) * T], w[:, k, i * P:(i + 1) * P],
                                     S.yT[:, k, :], start=(k == 0), stop=(k == 3))
            last.then_inc(K.chunk_used, 1)
            pe.wait_ge(y_ready, 1)
            for n, xT, b in ((n_ssm, S.yT, 0), (n_attn, S.yaT, 4)):
                wait_chunk(pe, K, n)
                w = K.ring[:, n % RING, :].rearrange("p (k c) -> p k c", k=4)
                for tt in range(TT):
                    for dh in range(2):
                        for k in range(4):
                            last = pe.matmul(K.bank[:, b + 2 * tt + dh, :], xT[:, k, tt * P:(tt + 1) * P],
                                             w[:, k, dh * 512:(dh + 1) * 512], start=(k == 0), stop=(k == 3))
                last.then_inc(K.chunk_used, 1)
            turn_tokens(pe, K, S.gates[:, 0, :, :], m_ready, turned)
            pe.wait_ge(evac, 4)
            for dh in range(2):
                token_product(pe, K, n_out + dh, K.hT, [K.bank[:, 2 * tt + dh, :] for tt in range(TT)])

        @block.vector
        def _(dve):
            c = Chain(dve, chain)
            dve.wait_ge(sig_done, 1)
            dve.tensor_tensor(S.yT[:], S.yT[:], sig[:], ALU.mult).then_inc(y_ready, 1)
            gs, ga = S.gates[:, 0, :, :], S.gates[:, 1, :, :]
            product = lambda b: K.bank[:, b:b + 4, :].rearrange("p (t b) c -> p t (b c)", t=TT)
            dve.wait_ge(K.chunk_used, n_ssm + 1)
            c.step(dve.tensor_tensor(gs, gs, product(0), ALU.mult))
            dve.wait_ge(K.chunk_used, n_attn + 1)
            c.do(dve.tensor_tensor(ga, ga, product(4), ALU.mult))
            dve.tensor_tensor(gs, gs, ga, ALU.add).then_inc(m_ready, TT)


def add_banks(K):
    def add(dve, c, tt):
        x = K.x[:, tt, :]
        c.do(dve.tensor_tensor(x, x, K.bank[:, 2 * tt:2 * tt + 2, :].rearrange("p b c -> p (b c)"), ALU.add))
    return add


class Second:

    def __init__(self, nc, scope):
        sb = lambda n, s: scope.enter_context(nc.sbuf_tensor(n, s, F32))
        self.uT = sb("uT", [P, 4, T])
        self.qT = sb("qT", [P, 4, T])
        self.qiT = sb("qiT", [P, 2, T])
        self.kz = sb("kz", [P, 2, T])
        self.kiz = sb("kiz", [P, 4, T])
        self.vz = sb("vz", [P, 2, TT, P])
        self.wi = sb("wi", [P, TT, 8])
        self.gates = sb("gates", [P, 2, TT, D])
        self.yT = sb("ysT", [P, 4, T])
        self.yaT = sb("yaT", [P, 4, T])



PK_HEADS = 8
PK = 128
TOP = 16
U_SLOTS = 4
V_SLOTS = 6


def peer_query_stage(K, scores):
    nc = K.nc
    n_wq, n_keys = START["peer_wq"], START["peer_keys"]
    act_done, dve_done, s_made = (K.sem(f"peerq_{s}") for s in ("act_done", "dve_done", "s_made"))
    with ExitStack() as stage, nc.Block() as block:
        qT = stage.enter_context(nc.sbuf_tensor("peer_qT", [P, 2 * PK_HEADS, T], F32))

        @block.tensor
        def _(pe):
            for j in range(4):
                feature_product(pe, K, n_wq + j, K.hT, 2 * j)
            wait_chunk(pe, K, n_keys)
            keys = K.ring[:, n_keys % RING, 0:2048].rearrange("p (m n) -> p m n", n=PK)
            for n in range(8):
                tt, g = n // 4, n % 4
                for done in (act_done, dve_done):
                    done_to = max(g, n // 2) + 1
                    pe.wait_ge(done, done_to)
                for i in range(4):
                    m = 4 * g + i
                    last = pe.matmul(K.bank[:, n, i * PK:(i + 1) * PK], qT[:, m, tt * P:(tt + 1) * P], keys[:, m, :],
                                     start=True, stop=True)
                last.then_inc(s_made, 1)

        tiles = lambda b: K.bank[:, b, :].rearrange("p (c t) -> p c t", c=2)

        @block.scalar
        def _(act):
            for j in range(4):
                act.wait_ge(K.chunk_used, n_wq + j + 1)
                act.activation(qT[:, 4 * j:4 * j + 2, :], tiles(2 * j), ACT.Copy).then_inc(act_done, 1)
            for n in range(0, 8, 2):
                act.wait_ge(s_made, n + 1)
                act.activation(scores[:, n // 4, n % 4 * 512:(n % 4 + 1) * 512], K.bank[:, n, :], ACT.Copy)

        @block.vector
        def _(dve):
            for j in range(4):
                dve.wait_ge(K.chunk_used, n_wq + j + 1)
                dve.tensor_copy(qT[:, 4 * j + 2:4 * j + 4, :], tiles(2 * j + 1)).then_inc(dve_done, 1)
            for n in range(1, 8, 2):
                dve.wait_ge(s_made, n + 1)
                dve.tensor_copy(scores[:, n // 4, n % 4 * 512:(n % 4 + 1) * 512], K.bank[:, n, :])


def top_sixteen(dve, c, values, index, src):
    c.do(dve.max(values[:, 0:8], src))
    c.do(dve.max_index(index[:, 0:8], values[:, 0:8], src))
    c.do(dve.match_replace(src, values[:, 0:8], src, TAKEN))
    c.do(dve.max(values[:, 8:TOP], src))
    c.step(dve.max_index(index[:, 8:TOP], values[:, 8:TOP], src))


def peer_stage(K, scores, scores_scope):
    nc = K.nc
    s_ = lambda s: K.sem(f"peer_{s}")
    u_in = [s_(f"u_in{i}") for i in range(U_SLOTS)]
    v_in = [s_(f"v_in{i}") for i in range(V_SLOTS)]
    u_used, gelu_done, chain, sel_ready, exp_ready, exp_done = (
        s_(s) for s in ("u_used", "gelu", "dve", "sel", "exp_ready", "exp_done"))
    with ExitStack() as stage:
        H = stage.enter_context(nc.sbuf_tensor("H", [P, PK, T], F32))
        sel = stage.enter_context(nc.sbuf_tensor("sel", [P, 3, TT, P], F32))
        route = stage.enter_context(ExitStack())
        sb = lambda n, s, dt=F32: route.enter_context(nc.sbuf_tensor(f"peer_{n}", s, dt))
        u = sb("u", [P, U_SLOTS, KD, PK])
        val = sb("val", [P, 2, TOP])
        idx = sb("idx", [P, 2, TOP], U32)
        idx_f = sb("idx_f", [P, PK_HEADS, 2, TOP])
        cand = sb("cand", [P, 2 * P])
        best = sb("best", [P, PK_HEADS, TOP])
        pos = sb("pos", [P, PK_HEADS, TOP], U32)
        part = sb("part", [P, 2, PK_HEADS, TOP], U32)
        part_f = sb("part_f", [P, 2, PK_HEADS, TOP])
        hot = sb("hot", [P, TOP, TOP])
        col = sb("col", [P, 2, PK_HEADS])

        with nc.Block() as block:
            @block.sync
            def _(sp):
                for i in range(U_SLOTS):
                    sp.dma_start(u[:, i, :, :], K.A["peer_u"][i]).then_inc(u_in[i], 16)
                with sp.Fori(0, PK // U_SLOTS - 1) as g:
                    for i in range(U_SLOTS):
                        sp.wait_ge(u_used, g * U_SLOTS + (i + 1))
                        sp.dma_start(u[:, i, :, :], K.A["peer_u"][g * U_SLOTS + (U_SLOTS + i)]).then_inc(u_in[i], 16)

            def tile(pe, i, land):
                pe.wait_ge(u_in[i], land)
                for k in range(KD):
                    last = pe.matmul(K.bank[:, i // 2, (i % 2) * T:(i % 2 + 1) * T], u[:, i, k, :], K.hT[:, k, :],
                                     start=(k == 0), stop=(k == KD - 1))
                last.then_inc(u_used, 1)

            @block.tensor
            def _(pe):
                for i in range(U_SLOTS):
                    tile(pe, i, 16)
                with pe.Fori(1, PK // U_SLOTS) as g:
                    for i in range(U_SLOTS):
                        if i % 2 == 0:
                            pe.wait_ge(gelu_done, 2 * g + (i // 2 - 1))
                        tile(pe, i, 16 * g + 16)

            @block.scalar
            def _(act):
                def gelu(b, g):
                    act.wait_ge(u_used, g * U_SLOTS + 2 * (b + 1))
                    act.activation(H[:, bass.ds(g * U_SLOTS + 2 * b, 2), :],
                                   K.bank[:, b, :].rearrange("p (i t) -> p i t", i=2), ACT.Gelu_apprx_tanh).then_inc(gelu_done, 1)

                with act.Fori(0, PK // U_SLOTS) as g:
                    for b in range(2):
                        gelu(b, g)
                for tt in range(TT):
                    act.wait_ge(exp_ready, tt + 1)
                    act.activation(sel[:, 2, tt, :], sel[:, 2, tt, :], ACT.Exp).then_inc(exp_done, 1)

            @block.vector
            def _(dve):
                c = Chain(dve, chain)
                wide = lambda a: a.unsqueeze(2).to_broadcast([P, PK_HEADS, TOP])
                flat = lambda a: a.rearrange("p h k -> p (h k)")
                for tt in range(TT):
                    for h in range(PK_HEADS):
                        for half in range(2):
                            m = 2 * h + half
                            top_sixteen(dve, c, val[:, half, :], idx[:, half, :], scores[:, tt, m * PK:(m + 1) * PK])
                        c.settle()
                        c.step(dve.tensor_copy(idx_f[:, h, :, :], idx[:]))
                        c.do(dve.tensor_tensor(cand[:].rearrange("p (a b) -> p a b", a=TOP),
                                               val[:, 0, :].unsqueeze(2).to_broadcast([P, TOP, TOP]),
                                               val[:, 1, :].unsqueeze(1).to_broadcast([P, TOP, TOP]), ALU.add))
                        top_sixteen(dve, c, best[:, h, :], pos[:, h, :], cand[:])
                        c.settle()
                    c.step(dve.tensor_scalar(part[:, 0, :, :], pos[:], 4, None, ALU.logical_shift_right))
                    c.do(dve.tensor_scalar(part[:, 1, :, :], pos[:], TOP - 1, None, ALU.bitwise_and))
                    c.do(dve.tensor_copy(part_f[:], part[:]))
                    for half in range(2):
                        for h in range(PK_HEADS):
                            c.do(dve.tensor_tensor(hot[:], part_f[:, half, h, :].unsqueeze(2).to_broadcast([P, TOP, TOP]),
                                                   K.iota[:, 0:TOP].unsqueeze(1).to_broadcast([P, TOP, TOP]), ALU.is_equal))
                            c.do(dve.tensor_tensor(hot[:], hot[:], idx_f[:, h, half, :].unsqueeze(1).to_broadcast([P, TOP, TOP]),
                                                   ALU.mult))
                            c.do(dve.tensor_reduce(sel[:, half, tt, h * TOP:(h + 1) * TOP], hot[:], AX.X, ALU.add))
                    gate = sel[:, 2, tt, :].rearrange("p (h k) -> p h k", k=TOP)
                    dve.tensor_tensor(gate, best[:], wide(best[:, :, 0]), ALU.subtract).then_inc(exp_ready, 1)
                    dve.wait_ge(exp_ready, tt + 1)
                for tt in range(TT):
                    gate = sel[:, 2, tt, :].rearrange("p (h k) -> p h k", k=TOP)
                    dve.wait_ge(exp_done, tt + 1)
                    c.do(dve.tensor_reduce(col[:, tt, :], gate, AX.X, ALU.add))
                    c.do(dve.reciprocal(col[:, tt, :], col[:, tt, :]))
                    c.do(dve.tensor_tensor(gate, gate, wide(col[:, tt, :]), ALU.mult))
        route.close()
        scores_scope.close()

        v = stage.enter_context(nc.sbuf_tensor("peer_v", [P, V_SLOTS, D], F32))
        hots = stage.enter_context(ExitStack())
        sb = lambda n, s, dt=F32: hots.enter_context(nc.sbuf_tensor(f"peer_{n}", s, dt))
        selT = sb("selT", [P, 3, T])
        QT = 4
        a_hot = sb("a_hot", [P, 2, QT, P])
        b_hot = sb("b_hot", [P, 2, QT, P])
        turned, selT_done, hot_ready, g_made, g_used = (s_(s) for s in ("turned", "selT", "hot", "g_made", "g_used"))
        with nc.Block() as block:
            @block.sync
            def _(sp):
                for i in range(V_SLOTS):
                    sp.dma_start(v[:, i, :], K.A["peer_v"][i]).then_inc(v_in[i], 16)

            @block.tensor
            def _(pe):
                for r in range(3):
                    for tt in range(TT):
                        last = pe.transpose(K.bank[:, r, tt * P:(tt + 1) * P], sel[:, r, tt, :], K.ident)
                last.then_inc(turned, 1)
                with pe.Fori(0, T // (2 * QT)) as g:
                    for b in range(2):
                        pe.wait_ge(hot_ready, 2 * g + (b + 1))
                        pe.wait_ge(g_used, 2 * g + (b + 1))
                        for q in range(QT):
                            last = pe.matmul(K.bank[:, 3 + b, q * P:(q + 1) * P], a_hot[:, b, q, :], b_hot[:, b, q, :],
                                             start=True, stop=True)
                        last.then_inc(g_made, 1)

            @block.vector
            def _(dve):
                dve.sem_inc(g_used, 2)
                dve.wait_ge(turned, 1)
                dve.tensor_copy(selT[:], K.bank[:, 0:3, 0:T]).then_inc(selT_done, 1)
                dve.wait_ge(selT_done, 1)

                def one_hots(g, b, ahead):
                    for q in range(QT):
                        at = bass.ds(g * 2 * QT + (ahead + q), 1) if not isinstance(g, int) else slice(ahead + q, ahead + q + 1)
                        dve.tensor_scalar(a_hot[:, b, q, :], K.iota, selT[:, 1, at], selT[:, 2, at], ALU.is_equal, ALU.mult)
                        last = dve.tensor_scalar(b_hot[:, b, q, :], K.iota, selT[:, 0, at], None, ALU.is_equal)
                    last.then_inc(hot_ready, 1)

                def gate_h(g, b, count):
                    dve.wait_ge(g_made, count)
                    h = H[:, :, bass.ds(g * 2 * QT + b * QT, QT)]
                    dve.tensor_tensor(h, h, K.bank[:, 3 + b, :].rearrange("p (q i) -> p i q", q=QT),
                                      ALU.mult).then_inc(g_used, 1)

                one_hots(0, 0, 0)
                one_hots(0, 1, QT)
                with dve.Fori(0, T // (2 * QT) - 1) as g:
                    for b in range(2):
                        gate_h(g, b, 2 * g + (b + 1))
                        one_hots(g, b, 2 * QT + b * QT)
                g = T // (2 * QT) - 1
                for b in range(2):
                    dve.wait_ge(g_made, 2 * g + b + 1)
                    h = H[:, :, 2 * QT * g + b * QT:2 * QT * g + (b + 1) * QT]
                    dve.tensor_tensor(h, h, K.bank[:, 3 + b, :].rearrange("p (q i) -> p i q", q=QT), ALU.mult).then_inc(g_used, 1)
        hots.close()

        v_used, y_made, y_done, y_turned = (s_(s) for s in ("v_used", "y_made", "y_done", "y_turned"))
        with nc.Block() as block:
            LOOPS = (PK - 2) // V_SLOTS

            @block.sync
            def _(sp):
                with sp.Fori(0, (PK - V_SLOTS) // V_SLOTS) as g:
                    for i in range(V_SLOTS):
                        sp.wait_ge(v_used, g * V_SLOTS + (i + 1))
                        sp.dma_start(v[:, i, :], K.A["peer_v"][g * V_SLOTS + (V_SLOTS + i)]).then_inc(v_in[i], 16)
                for n in range((PK - V_SLOTS) // V_SLOTS * V_SLOTS + V_SLOTS, PK):
                    sp.wait_ge(v_used, n - V_SLOTS + 1)
                    sp.dma_start(v[:, n % V_SLOTS, :], K.A["peer_v"][n]).then_inc(v_in[n % V_SLOTS], 16)

            @block.tensor
            def _(pe):
                def tile(i, land, h, start, stop):
                    pe.wait_ge(v_in[i], land)
                    for d in range(KD):
                        last = pe.matmul(K.bank[:, d, 0:T], v[:, i, d * P:(d + 1) * P], h, start=start, stop=stop)
                    last.then_inc(v_used, 1)

                tile(0, 16, H[:, 0, :], True, False)
                with pe.Fori(0, LOOPS) as g:
                    for i in range(V_SLOTS):
                        slot = (1 + i) % V_SLOTS
                        h = H[:, bass.ds(g * V_SLOTS + (1 + i), 1), :].rearrange("p o t -> p (o t)")
                        tile(slot, 16 * g + 16 * ((1 + i) // V_SLOTS + 1), h, False, False)
                n = PK - 1
                tile(n % V_SLOTS, 16 * (n // V_SLOTS + 1), H[:, n, :], False, True)
                pe.wait_ge(y_done, 2)
                for tt in range(TT):
                    for k in range(KD):
                        last = pe.transpose(K.bank[:, 2 * tt + k // 4, (k % 4) * P:(k % 4 + 1) * P],
                                            K.hT[:, k, tt * P:(tt + 1) * P], K.ident)
                last.then_inc(y_turned, 1)

            @block.scalar
            def _(act):
                act.wait_ge(v_used, PK)
                act.activation(K.hT[:, 0:4, :], K.bank[:, 0:4, 0:T], ACT.Copy).then_inc(y_done, 1)

            @block.vector
            def _(dve):
                dve.wait_ge(v_used, PK)
                dve.tensor_copy(K.hT[:, 4:8, :], K.bank[:, 4:8, 0:T]).then_inc(y_done, 1)



def program(nc, inputs, out):
    with ExitStack() as ctx:
        K = Core(nc, ctx, inputs)
        with ExitStack() as scope:
            load_stage(K, scope)
            ada_stage(K, "ada00", 0)
            stick_breaking_stage(K)
            ada_stage(K, "ada01", 1)
            moe_stage(K, 0)
            K.recycle_sems()
            ada_stage(K, "ada10", 2)
            retention_stage(K)
            ada_stage(K, "ada11", 3)
            moe_stage(K, 1)
            rms_norm_turn_stage(K, "norm1", "norm1_g")
            with ExitStack() as second:
                S = Second(nc, second)
                second_projection_stage(K, S)
                s5_stage(K, S)
                sparse_attention_stage(K, S)
                join_stage(K, S)
            K.recycle_sems()
            rms_norm_turn_stage(K, "norm2", "norm2_g", before=add_banks(K))
            scores_scope = ctx.enter_context(ExitStack())
            scores = scores_scope.enter_context(nc.sbuf_tensor("peer_scores", [P, TT, 2048], F32, side="right"))
            peer_query_stage(K, scores)
        peer_stage(K, scores, scores_scope)
        rms_norm_turn_stage(K, "norm_f", "norm_f_g", before=add_banks(K),
                            out=out[0].rearrange("(t p) d -> p t d", p=P))



def _chunks(w):
    rows, cols = w.shape
    kt = rows // P
    c = CHUNK // kt
    return w.reshape(kt, P, cols // c, c).transpose(2, 1, 0, 3).reshape(cols // c, P, CHUNK)


def _short(w):
    rows, cols = w.shape
    out = np.zeros((1, P, CHUNK), w.dtype)
    out[0, :, 0:rows // P * cols] = w.reshape(rows // P, P, cols).transpose(1, 0, 2).reshape(P, -1)
    return out


def _experts(gate, up, down):
    parts = []
    for e in range(EXPERTS):
        parts += [_chunks(gate[e]), _chunks(up[e])]
        if e:
            parts.append(_chunks(down[e - 1]))
    return parts + [_chunks(down[EXPERTS - 1])]


def _swap(dim):
    m = np.zeros((P, P), np.float32)
    for base in range(0, P, dim):
        for i in range(dim // 2):
            m[base + dim // 2 + i, base + i] = -1.0
            m[base + i, base + dim // 2 + i] = 1.0
    return m


def _rope_rows(dim):
    inv = (np.float32(10000.0) ** (-np.arange(0, dim, 2, dtype=np.float32) / np.float32(dim))).astype(np.float32)
    ang = np.arange(T, dtype=np.float32)[None, :] * inv[np.arange(P) % (dim // 2)][:, None]
    return np.stack([np.cos(ang), np.sin(ang)], 1).astype(np.float32)


def _retention_decay():
    h = np.arange(RET_HEADS, dtype=np.float32)
    lg = np.log(np.float32(1.0) - np.exp2(np.float32(-5.0) - h)).astype(np.float64)
    m, n = np.arange(P)[:, None, None], np.arange(P)[None, None, :]
    lg = lg[None, :, None]
    own = np.where(n >= m, np.exp(np.maximum(n - m, 0) * lg), 0.0)
    before = np.exp((n + 1.0 + P - 1.0 - m) * lg)
    return np.concatenate([own, before], 2).astype(np.float32)


def layout(a):
    eye = np.eye(P, dtype=np.float32)
    tri = -np.tril(np.ones((P, P), np.float32))
    w2 = a["w_in_2"][0]
    u, q, k, v, qi, ki, wi, gs, ga = np.split(w2, np.cumsum([512, 512, 128, 128, 256, 32, 8, 1024])[:8], axis=1)
    pair = np.concatenate([np.concatenate([np.arange(64 * j, 64 * j + 64), np.arange(64 * (j + 4), 64 * (j + 4) + 64)])
                           for j in range(4)])
    stream = []
    for i in range(DEPTH):
        stream += [_chunks(a["ada_w"][i, 0])]
        stream += [_chunks(a["sb_w_in"][0]), _chunks(a["sb_w_out"][0])] if i == 0 else [
            _chunks(a["ret_w_in"][0])] + [_chunks(a["ret_w_out"][0][r:r + D, c:c + COLS])
                                          for c in (0, COLS) for r in (0, D)]
        stream += [_chunks(a["ada_w"][i, 1])]
        stream += _experts(a["moe_w_gate"][i], a["moe_w_up"][i], a["moe_w_down"][i])
    stream += [_chunks(u), _chunks(q[:, pair]), _chunks(np.concatenate([k, qi, ki, ki, ki, ki], 1)),
               _short(np.concatenate([v, wi], 1)), _chunks(gs), _chunks(ga), _short(a["w_glu_2"][0]),
               _chunks(a["w_ssm_up_2"][0]), _chunks(a["w_attn_up_2"][0][pair]), _chunks(a["w_out_2"][0]),
               _chunks(a["peer_wq_2"][0])]
    keys = np.stack([a["peer_k1_2"][0], a["peer_k2_2"][0]], 1)
    stream += [_short(keys.reshape(-1, P).T)]
    stream = np.concatenate(stream)
    assert stream.shape == (CHUNKS, P, CHUNK)
    states = lambda s: s[0].reshape(16, P).T
    cz = np.zeros((2, 16, P, P), np.float32)
    for n, c in enumerate((a["c_re_2"][0], a["c_im_2"][0])):
        for g in range(32):
            col = 16 * (g % 8)
            cz[n, g // 2, 64 * (g % 2):64 * (g % 2) + 64, col:col + 16] = c[g].T
    out = {
        "stream": stream,
        "x_tokens": a["x"][0].reshape(TT, P, D).transpose(1, 0, 2),
        "c_cols": a["c"].reshape(KD, P).T,
        "ada_b": a["ada_b"].reshape(4, 3 * D),
        "ln_g": a["ln_g"].reshape(4, D),
        "ln_b": a["ln_b"].reshape(4, D),
        "consts": np.stack([eye, tri, -np.ones((P, P), np.float32), _swap(128), _swap(64), _swap(32),
                            np.tile(np.arange(P, dtype=np.float32), (P, 1))], 1),
        "router_w": a["router_w"].reshape(KD, P, EXPERTS).transpose(1, 0, 2),
        "router_b": a["router_b"].reshape(1, EXPERTS),
        "positions": a["positions"].reshape(1, T),
        "inv_freq": (np.float32(1.0) / (np.float32(10000.0) ** (np.arange(0, 128, 2, dtype=np.float32) / np.float32(128)))
                     ).astype(np.float32)[np.arange(P) % 64].reshape(P, 1),
        "decay": _retention_decay(),
        "ret_gn_g": a["ret_gn_g"].reshape(1, 2 * D),
        "rope64": _rope_rows(64),
        "rope32": _rope_rows(32),
        "norm1_g": a["norm1_g_2"].reshape(1, D),
        "norm2_g": a["norm2_g_2"].reshape(1, D),
        "norm_f_g": a["norm_f_g_2"].reshape(1, D),
        "a_re": states(a["a_re_2"]),
        "a_im": states(a["a_im_2"]),
        "log_dt": np.repeat(a["log_dt_2"][0], 64).reshape(16, P).T,
        "b_re": a["b_re_2"][0].reshape(16, P, 16).transpose(1, 0, 2),
        "b_im": a["b_im_2"][0].reshape(16, P, 16).transpose(1, 0, 2),
        "c_re": cz[0].transpose(1, 0, 2),
        "c_im": cz[1].transpose(1, 0, 2),
        "d_skip": a["d_skip_2"].reshape(4, P).T,
        "peer_u": a["peer_u_2"][0].reshape(P, P, KD, P).transpose(0, 3, 2, 1).reshape(P, P, KD * P),
        "peer_v": a["peer_v_2"][0].reshape(P, P, D),
    }
    return {k: np.ascontiguousarray(v) for k, v in out.items()}


def kernel(**inputs):
    from concourse import bacc
    from concourse.bass_utils import run_bass_kernel_spmd

    nc = bacc.Bacc("TRN2", target_bir_lowering=False, num_devices=1)
    arrays = layout({k: np.asarray(v) for k, v in inputs.items()})
    aps = {k: nc.dram_tensor(f"in_{k}", v.shape, mybir.dt.from_np(v.dtype), kind="ExternalInput").ap()
           for k, v in arrays.items()}
    out = nc.dram_tensor("out", (1, T, D), F32, kind="ExternalOutput").ap()
    program(nc, aps, out)
    result = run_bass_kernel_spmd(nc, [{f"in_{k}": v for k, v in arrays.items()}], core_ids=[0])
    return result.results[0]["out"]
```

```python
from contextlib import ExitStack

import concourse.bass as bass
import numpy as np
from concourse import mybir
from concourse.alu_op_type import AluOpType as ALU

F32 = mybir.dt.float32
I32 = mybir.dt.int32
BF16 = mybir.dt.bfloat16
F32R = mybir.dt.float32r
U32 = mybir.dt.uint32
ACT = mybir.ActivationFunctionType
AX = mybir.AxisListType

P = 128
T = 256
TT = T // P
D = 1024
KD = D // P
CHUNK = 4096
COLS = CHUNK // KD
RING = 6
DEPTH = 2
ALPHA = float((2 * DEPTH) ** 0.25)
LN_EPS = 1e-5
RMS_EPS = 1e-6
SB_HEADS = 16
SB_DIM = D // SB_HEADS
RET_HEADS = 8
RET_V = 2 * D // RET_HEADS
EXPERTS = 16
GROUPS = 4
PER_GROUP = EXPERTS // GROUPS
IDX_SCALE = 1.0 / 16.0
NEG = -1e30
TWO_PI = float(np.float32(6.283185))
ROUND = 12582912.0

STREAM = [("ada00", 6), ("sb_in", 6), ("sb_out", 2),
          ("ada01", 6), ("moe0", 3 * EXPERTS),
          ("ada10", 6), ("ret_in", 12), ("ret_out", 4),
          ("ada11", 6), ("moe1", 3 * EXPERTS),
          ("in2", 8), ("w_glu", 1), ("ssm_up", 1), ("attn_up", 1), ("w_out2", 2), ("peer_wq", 4), ("peer_keys", 1)]
START = {}
_n = 0
for _name, _count in STREAM:
    START[_name] = _n
    _n += _count
CHUNKS = _n
ADA_ROW = {"ada00": 0, "ada01": 1, "ada10": 2, "ada11": 3}
SHORT = {START["in2"] + 3: KD * 136, START["w_glu"]: 4 * 512, START["peer_keys"]: 2048}


def next_start(name):
    order = [n for n, _ in STREAM]
    i = order.index(name)
    return START[order[i + 1]] if i + 1 < len(order) else CHUNKS


class Core:

    def __init__(self, nc, ctx, inputs):
        self.nc = nc
        self.ctx = ctx
        self.A = inputs
        self.fetched = 0
        self.bank = ctx.enter_context(nc.psum_tensor("bank", [P, 8, 512], F32))
        self.consts = self.sb("consts", [P, 7, P])
        self.ident = self.consts[:, 0, :]
        self.tri_neg = self.consts[:, 1, :]
        self.ones_neg = self.consts[:, 2, :]
        self.swap128 = self.consts[:, 3, :]
        self.swap64 = self.consts[:, 4, :]
        self.swap32 = self.consts[:, 5, :]
        self.iota = self.consts[:, 6, :]
        self.x = self.sb("x", [P, TT, D])
        self.hT = self.sb("hT", [P, KD, T])
        self.mod = self.sb("mod", [P, 3 * D])
        self.landed = [nc.alloc_semaphore(f"landed{s}") for s in range(RING)]
        self.chunk_used = nc.alloc_semaphore("chunk_used")
        self.stored = nc.alloc_semaphore("stored")
        self.stage_sems = []
        self.loaded = nc.alloc_semaphore("consts_loaded")

    def sb(self, name, shape, dt=F32):
        return self.ctx.enter_context(self.nc.sbuf_tensor(name, shape, dt))

    def sem(self, name):
        self.stage_sems.append(self.nc.alloc_semaphore(name))
        return self.stage_sems[-1]

    def recycle_sems(self):
        self.nc.clear_and_free_semaphores(self.stage_sems)
        self.nc.all_engine_barrier()
        self.stage_sems = []


class Chain:

    def __init__(self, eng, sem):
        self.eng, self.sem, self.n = eng, sem, 0

    def step(self, ins):
        self.n += 1
        ins.then_inc(self.sem, 1)
        return ins

    def settle(self):
        self.eng.wait_ge(self.sem, self.n)

    def do(self, ins):
        self.step(ins)
        self.settle()



def fetch_chunks(sp, K, upto):
    upto = min(upto, CHUNKS)
    for n in range(K.fetched, upto):
        if n >= RING:
            sp.wait_ge(K.chunk_used, n - RING + 1)
        size = SHORT.get(n, CHUNK)
        sp.dma_start(K.ring[:, n % RING, 0:size], K.A["stream"][n, :, 0:size]).then_inc(K.landed[n % RING], 16)
    K.fetched = max(K.fetched, upto)


def wait_chunk(pe, K, n):
    pe.wait_ge(K.landed[n % RING], 16 * (n // RING + 1))


def feature_product(pe, K, n, xT, bank0, slot=None, land=None):
    if n is not None:
        slot, land = n % RING, 16 * (n // RING + 1)
    pe.wait_ge(K.landed[slot], land)
    w = K.ring[:, slot, :].rearrange("p (k c) -> p k c", k=KD)
    for c in range(4):
        out = K.bank[:, bank0 + c // 2, (c % 2) * T:(c % 2 + 1) * T]
        for k in range(KD):
            last = pe.matmul(out, w[:, k, c * P:(c + 1) * P], xT[:, k, :], start=(k == 0), stop=(k == KD - 1))
    last.then_inc(K.chunk_used, 1)


def token_product(pe, K, n, xT, banks, cols=COLS, kt=KD, start=True, stop=True):
    wait_chunk(pe, K, n)
    w = K.ring[:, n % RING, 0:kt * cols].rearrange("p (k c) -> p k c", k=kt)
    for tt in range(TT):
        for k in range(kt):
            last = pe.matmul(banks[tt], xT[:, k, tt * P:(tt + 1) * P], w[:, k, :],
                             start=(start and k == 0), stop=(stop and k == kt - 1))
    last.then_inc(K.chunk_used, 1)



def load_stage(K, scope):
    nc = K.nc
    K.ring = scope.enter_context(nc.sbuf_tensor("ring", [P, RING, CHUNK], F32))
    K.silu_c = scope.enter_context(nc.sbuf_tensor("silu_c", [P, KD], F32))
    K.c_wide = scope.enter_context(nc.sbuf_tensor("c_wide", [P, KD, P], F32))
    c_in, act_done, wide_done = K.sem("c_in"), K.sem("silu_c_done"), K.sem("c_wide_done")
    with nc.Block() as block:
        @block.sync
        def _(sp):
            sp.dma_start(K.silu_c[:], K.A["c_cols"]).then_inc(c_in, 16)
            fetch_chunks(sp, K, RING)

        @block.scalar
        def _(act):
            act.dma_start(K.consts[:], K.A["consts"]).then_inc(K.loaded, 16)
            act.dma_start(K.x[:], K.A["x_tokens"]).then_inc(K.loaded, 16)
            act.wait_ge(c_in, 16)
            act.activation(K.silu_c[:], K.silu_c[:], ACT.Silu).then_inc(act_done, 1)

        @block.vector
        def _(dve):
            dve.wait_ge(act_done, 1)
            dve.tensor_copy(K.c_wide[:], K.silu_c[:].unsqueeze(2).to_broadcast([P, KD, P])).then_inc(wide_done, 1)
            dve.wait_ge(wide_done, 1)



class AdaLN:

    def __init__(self, K, name):
        self.K, self.name, self.row = K, name, ADA_ROW[name]
        self.bias_in, self.h_ready, self.turned, self.evac = (
            K.sem(f"{name}_{s}") for s in ("bias_in", "h", "turned", "evac"))
        self.h_scope = ExitStack()
        self.h = self.h_scope.enter_context(K.nc.sbuf_tensor(f"{name}_hbuf", [P, TT, D], F32, side="right"))

    def bias(self, eng, cols):
        row = self.K.A["ada_b"][self.row:self.row + 1, cols]
        eng.dma_start(self.K.mod[:, cols], row.to_broadcast([P, cols.stop - cols.start])).then_inc(self.bias_in, 16)

    def tensor(self, pe, y_read=None):
        K, n0 = self.K, START[self.name]
        for j in range(6):
            wait_chunk(pe, K, n0 + j)
            if j == 4 and y_read is not None:
                pe.wait_ge(y_read, 1)
            w = K.ring[:, (n0 + j) % RING, :].rearrange("p (k c) -> p k c", k=KD)
            for k in range(KD):
                last = pe.matmul(K.bank[:, (4 + j) % 8, :], K.c_wide[:, k, :], w[:, k, :], start=(k == 0), stop=(k == KD - 1))
            last.then_inc(K.chunk_used, 1)
        pe.wait_ge(K.loaded, 32)
        turn_tokens(pe, K, self.h, self.h_ready, self.turned)

    def vector(self, dve, c, biases):
        K, n0 = self.K, START[self.name]
        dve.wait_ge(self.bias_in, 16 * biases)
        dve.wait_ge(K.loaded, 32)
        for j in range(6):
            dve.wait_ge(K.chunk_used, n0 + j + 1)
            part = K.mod[:, j * COLS:(j + 1) * COLS]
            c.step(dve.scalar_tensor_tensor(part, K.bank[:, (4 + j) % 8, :], 0.0 if j < 2 else 1.0, part, ALU.add, ALU.add))
        for tt in range(TT):
            c.settle()
            c.do(dve.tensor_tensor(self.h[:, tt, :], K.x[:, tt, :], K.mod[:, D:2 * D], ALU.mult))
            dve.tensor_tensor(self.h[:, tt, :], self.h[:, tt, :], K.mod[:, 0:D], ALU.add).then_inc(self.h_ready, 1)


def ada_stage(K, name):
    nc = K.nc
    ada = AdaLN(K, name)
    with nc.Block() as block:
        @block.sync
        def _(sp):
            fetch_chunks(sp, K, next_start(name) + RING)

        @block.scalar
        def _(act):
            ada.bias(act, slice(0, 3 * D))
            evacuate_turned(act, K, ada.turned, ada.evac)

        @block.tensor
        def _(pe):
            ada.tensor(pe)

        @block.vector
        def _(dve):
            ada.vector(dve, Chain(dve, K.sem(f"{name}_dve")), 1)
    ada.h_scope.close()


def turn_tokens(pe, K, h, h_ready, turned):
    for tt in range(TT):
        pe.wait_ge(h_ready, tt + 1)
        for k in range(KD):
            out = K.bank[:, (6 + k // 2) % 8, (k % 2) * T + tt * P:(k % 2) * T + (tt + 1) * P]
            last = pe.transpose(out, h[:, tt, k * P:(k + 1) * P], K.ident)
    last.then_inc(turned, 1)


def evacuate_turned(act, K, turned, evac):
    act.wait_ge(turned, 1)
    for b in range(4):
        act.activation(K.hT[:, 2 * b:2 * b + 2, :], K.bank[:, (6 + b) % 8, :].rearrange("p (k t) -> p k t", k=2),
                       ACT.Copy).then_inc(evac, 1)



def layer_norm_stage(K, name, row, project, following=None):
    nc = K.nc
    rows_in, chain, y_read, var_ready, rstd_ready = (
        K.sem(f"{name}_norm_{s}") for s in ("rows_in", "dve", "y_read", "var", "std"))
    ada = AdaLN(K, following) if following else None
    with ExitStack() as stage, nc.Block() as block:
        sb = lambda n, s: stage.enter_context(nc.sbuf_tensor(f"{name}_{n}", s, F32))
        g_row, b_row = sb("g", [P, D]), sb("b", [P, D])
        s = sb("s", [P, TT, D])
        stats, mv, std = sb("stats", [P, TT, 2, 6]), sb("mv", [P, TT, 2]), sb("std", [P, TT])
        eps = sb("eps", [P, 1])

        @block.sync
        def _(sp):
            sp.dma_start(g_row[:], K.A["ln_g"][row:row + 1, :].to_broadcast([P, D])).then_inc(rows_in, 16)
            sp.dma_start(b_row[:], K.A["ln_b"][row:row + 1, :].to_broadcast([P, D])).then_inc(rows_in, 16)
            if ada:
                fetch_chunks(sp, K, next_start(following) + RING)

        @block.tensor
        def _(pe):
            if project is not None:
                project(pe)
            if ada:
                ada.tensor(pe, y_read)

        @block.scalar
        def _(act):
            if ada:
                ada.bias(act, slice(0, 2 * D))
            act.wait_ge(var_ready, 1)
            act.activation(std[:], mv[:, :, 1], ACT.Sqrt, bias=eps[:]).then_inc(rstd_ready, 1)
            if ada:
                act.wait_ge(y_read, TT)
                ada.bias(act, slice(2 * D, 3 * D))
                evacuate_turned(act, K, ada.turned, ada.evac)

        @block.vector
        def _(dve):
            c = Chain(dve, chain)
            c.step(dve.memset(eps[:], LN_EPS))
            dve.wait_ge(K.chunk_used, next_start(name))
            for tt in range(TT):
                y = K.bank[:, 2 * tt:2 * tt + 2, :].rearrange("p b c -> p (b c)")
                dve.tensor_tensor(s[:, tt, :], y, K.mod[:, 2 * D:3 * D], ALU.mult).then_inc(y_read, 1)
            for tt in range(TT):
                dve.wait_ge(y_read, tt + 1)
                c.do(dve.scalar_tensor_tensor(s[:, tt, :], K.x[:, tt, :], ALPHA, s[:, tt, :], ALU.mult, ALU.add))
                for j in range(2):
                    c.step(dve.bn_stats(stats[:, tt, j, :], s[:, tt, j * 512:(j + 1) * 512]))
                c.settle()
                last = dve.bn_aggr(mv[:, tt, :], stats[:, tt, :, :])
                if tt == 0:
                    c.step(last)
            last.then_inc(var_ready, 1)
            dve.wait_ge(rstd_ready, 1)
            c.do(dve.reciprocal(std[:], std[:]))
            dve.wait_ge(rows_in, 32)
            for tt in range(TT):
                c.do(dve.tensor_scalar(s[:, tt, :], s[:, tt, :], mv[:, tt, 0:1], std[:, tt:tt + 1], ALU.subtract, ALU.mult))
                c.do(dve.tensor_tensor(s[:, tt, :], s[:, tt, :], g_row[:], ALU.mult))
                c.step(dve.tensor_tensor(K.x[:, tt, :], s[:, tt, :], b_row[:], ALU.add))
            c.settle()
            if ada:
                ada.vector(dve, c, 2)
    return ada



def stick_breaking_stage(K):
    nc = K.nc
    n0 = START["sb_in"]
    W = T + P
    act_done, dve_done, q_zeroed, zeroed = (K.sem(f"sb_{s}") for s in ("act_done", "dve_done", "q_zeroed", "v_zeroed"))
    with ExitStack() as stage:
        sb = lambda n, s: stage.enter_context(nc.sbuf_tensor(f"sb_{n}", s, F32))
        oT = sb("oT", [P, KD, T])
        heads = stage.enter_context(ExitStack())
        sb = lambda n, s: heads.enter_context(nc.sbuf_tensor(f"sb_{n}", s, F32))
        qz = sb("qz", [P, SB_HEADS, T])
        kT = sb("kT", [P, KD, T])
        vz = sb("vz", [P, TT, SB_HEADS, P])

        with nc.Block() as block:
            @block.sync
            def _(sp):
                fetch_chunks(sp, K, START["sb_out"] + RING)

            @block.gpsimd
            def _(pool):
                pool.memset(vz[:], 0.0).then_inc(zeroed, 1)

            @block.tensor
            def _(pe):
                for j in range(6):
                    b = 2 * j % 8
                    if j >= 4:
                        pe.wait_ge(act_done, j - 3)
                        pe.wait_ge(dve_done, j - 3)
                    if j < 4:
                        feature_product(pe, K, n0 + j, K.hT, b)
                    else:
                        token_product(pe, K, n0 + j, K.hT, [K.bank[:, b + tt, :] for tt in range(TT)])

            def empty(eng, i, done):
                def scaled(out, src, scale):
                    if i == 0:
                        return eng.activation(out, src, ACT.Copy, scale=scale)
                    return eng.tensor_scalar(out, src, scale, None, ALU.mult)

                eng.wait_ge(q_zeroed, 1)
                for j in range(6):
                    if j == 4:
                        eng.wait_ge(zeroed, 1)
                    src = K.bank[:, 2 * j % 8 + i, :]
                    eng.wait_ge(K.chunk_used, n0 + j + 1)
                    if 2 <= j < 4:
                        c = 4 * (j - 2) + 2 * i
                        scaled(kT[:, c:c + 2, :], src.rearrange("p (c t) -> p c t", c=2), 1.0).then_inc(done, 1)
                        continue
                    for half in range(2):
                        lo = half * SB_DIM
                        if j < 2:
                            head = 8 * j + 4 * i + half
                            last = scaled(qz[lo:lo + SB_DIM, head:head + 3:2, :],
                                          src[lo:lo + SB_DIM, :].rearrange("p (c t) -> p c t", c=2), SB_DIM ** -0.5)
                        else:
                            head = 8 * (j - 4) + half
                            heads_v = src.rearrange("p (h two d) -> p h two d", two=2, d=SB_DIM)
                            last = scaled(vz[:, i, head:head + 7:2, lo:lo + SB_DIM], heads_v[:, :, half, :], 1.0)
                    last.then_inc(done, 1)

            @block.scalar
            def _(act):
                empty(act, 0, act_done)

            @block.vector
            def _(dve):
                dve.memset(qz[:], 0.0).then_inc(q_zeroed, 1)
                empty(dve, 1, dve_done)

        z_made, z_abs, soft, sp_made, sp_masked, s_made, a_made, a_masked, o_made, o_done = (
            K.sem(f"sb_{s}") for s in ("z_made", "z_abs", "soft", "sp_made", "sp_masked", "s_made", "a_made",
                                       "a_masked", "o_made", "o_done"))
        act_chain = K.sem("sb_act")
        with nc.Block() as block:
            NB = 3
            zabs, soft_b, sp_b, a_b = (sb(n, [P, NB, W]) for n in ("zabs", "softb", "spb", "ab"))
            zbank = lambda h: K.bank[:, h % 2, 0:W]
            sbank = lambda h: K.bank[:, 2 + h % 2, 0:W]

            def diagonal(buf):
                return buf.rearrange("p (b q) -> p b q", q=P)[:, 0:3:2, :]

            @block.tensor
            def _(pe):
                def scores(h, out, tile, stop):
                    if tile == 0:
                        return pe.matmul(out[:, 0:T], kT[:, h // 2, 0:P], qz[:, h, :], start=True, stop=stop)
                    return pe.matmul(out[:, T:W], kT[:, h // 2, P:T], qz[:, h, P:T], start=True, stop=stop)

                for i in range(SB_HEADS + 3):
                    if i < SB_HEADS:
                        if i >= 2:
                            pe.wait_ge(sp_made, i - 1)
                        scores(i, zbank(i), 0, True)
                        scores(i, zbank(i), 1, True).then_inc(z_made, 1)
                    h = i - 1
                    if 0 <= h < SB_HEADS:
                        if h >= 2:
                            pe.wait_ge(a_made, h - 1)
                        scores(h, sbank(h), 0, False)
                        pe.wait_ge(sp_masked, h + 1)
                        sp = sp_b[:, h % NB, :]
                        pe.matmul(sbank(h)[:, P:T], K.ones_neg, sp[:, T:W], start=False, stop=False)
                        pe.matmul(sbank(h)[:, 0:T], K.tri_neg, sp[:, 0:T], start=False, stop=True)
                        scores(h, sbank(h), 1, False)
                        pe.matmul(sbank(h)[:, T:W], K.tri_neg, sp[:, T:W], start=False, stop=True).then_inc(s_made, 1)
                    h = i - 3
                    if h >= 0:
                        pair, a = h // 2, a_b[:, h % NB, :]
                        out = K.bank[:, 4 + pair % 2, 0:T]
                        if h % 2 == 0 and pair >= 2:
                            pe.wait_ge(o_done, pair - 1)
                        pe.wait_ge(a_masked, h + 1)
                        parts = [(out, vz[:, 0, h, :], a[:, 0:T]), (out[:, P:T], vz[:, 1, h, :], a[:, T:W])]
                        for n, (o, v, prob) in enumerate(parts if h % 2 == 0 else parts[::-1]):
                            last = pe.matmul(o, v, prob, start=(h % 2 == 0 and n == 0), stop=(h % 2 == 1 and n == 1),
                                             skip_group_check=True)
                        last.then_inc(o_made, 1)

            @block.vector
            def _(dve):
                for i in range(SB_HEADS + 4):
                    h = i - 1
                    if 0 <= h < SB_HEADS:
                        dve.wait_ge(soft, 2 * h + 2)
                        if h >= NB:
                            dve.wait_ge(s_made, h - NB + 1)
                        dve.scalar_tensor_tensor(sp_b[:, h % NB, :], zbank(h), 0.0, soft_b[:, h % NB, :], ALU.max,
                                                 ALU.add).then_inc(sp_made, 1)
                    h = i - 4
                    if h >= 0 and h % 2 == 1:
                        dve.wait_ge(o_made, h + 1)
                        dve.tensor_copy(oT[:, h // 2, :], K.bank[:, 4 + h // 2 % 2, 0:T]).then_inc(o_done, 1)

            @block.scalar
            def _(act):
                act.preload_act_table_set("natural_log_exp_and_others")
                for i in range(SB_HEADS + 1):
                    if i < SB_HEADS:
                        act.wait_ge(z_made, i + 1)
                        act.activation(zabs[:, i % NB, :], zbank(i), ACT.Abs).then_inc(z_abs, 1)
                        act.wait_ge(z_abs, i + 1)
                        if i >= NB:
                            act.wait_ge(sp_made, i - NB + 1)
                        act.activation(zabs[:, i % NB, :], zabs[:, i % NB, :], ACT.Exp, scale=-1.0).then_inc(soft, 1)
                        act.wait_ge(soft, 2 * i + 1)
                        act.activation(soft_b[:, i % NB, :], zabs[:, i % NB, :], ACT.Ln, bias=1.0).then_inc(soft, 1)
                    h = i - 1
                    if h >= 0:
                        act.wait_ge(s_made, h + 1)
                        if h >= NB:
                            act.wait_ge(o_made, h - NB + 1)
                        act.activation(a_b[:, h % NB, :], sbank(h), ACT.Exp).then_inc(a_made, 1)

            @block.gpsimd
            def _(pool):
                mask = dict(compare_op=ALU.is_gt, fill=0.0, base=0, pattern=[[0, 2], [1, P]], channel_multiplier=-1)
                for i in range(SB_HEADS + 1):
                    if i < SB_HEADS:
                        pool.wait_ge(sp_made, i + 1)
                        d = diagonal(sp_b[:, i % NB, :])
                        pool.affine_select(out=d, in_=d, **mask).then_inc(sp_masked, 1)
                    if i >= 1:
                        pool.wait_ge(a_made, i)
                        d = diagonal(a_b[:, (i - 1) % NB, :])
                        pool.affine_select(out=d, in_=d, **mask).then_inc(a_masked, 1)

        heads.close()

        def project(pe):
            for dh in range(2):
                token_product(pe, K, START["sb_out"] + dh, oT, [K.bank[:, 2 * tt + dh, :] for tt in range(TT)])
        return layer_norm_stage(K, "sb_out", 0, project, "ada01")



def moe_stage(K, layer, ada, following=None):
    nc = K.nc
    h = ada.h
    name = f"moe{layer}"
    n0, n_end = START[name], next_start(name)
    s_ = lambda s: K.sem(f"{name}_{s}")
    small_in, logits_made, exp_ready, exp_made, group_ready, ranks_made, weights_ready, flag_ready = (
        s_(s) for s in ("small_in", "logits", "exp_ready", "exp_made", "group", "ranks", "weights", "flag"))
    silu_done, prod_done, hidden_done, chain, spread, copied = (
        s_(s) for s in ("silu", "prod", "hidden", "dve", "spread", "copied"))
    with ExitStack() as stage:
        sb = lambda n, s, dt=F32: stage.enter_context(nc.sbuf_tensor(f"{name}_{n}", s, dt))
        tokens = sb("tokens", [P, EXPERTS * T])
        wide = sb("wide", [P, EXPERTS * T])
        weights = sb("slot_w", [P, EXPERTS, P])
        hid = sb("hid", [P, 2, 4, T])
        hot = sb("hot", [P, TT, GROUPS, P])
        hotT = sb("hotT", [P, GROUPS, T])
        eq = sb("eq", [P, TT, P])
        zero = sb("zero", [P, COLS], BF16)
        router = sb("router", [P, KD, EXPERTS])
        router_b = sb("router_b", [P, EXPERTS])
        lg, pr, ex = (sb(n, [P, TT, EXPERTS]) for n in ("lg", "pr", "ex"))
        pairs = sb("pairs", [P, TT * GROUPS, 6])
        col = sb("col", [P, 9, TT])
        grp = sb("grp", [P, 4, TT, GROUPS])
        group = sb("group", [P, TT, GROUPS])
        rank_in = sb("rank_in", [P, TT, GROUPS])
        order = sb("order", [P, GROUPS])
        flag = sb("flag", [P, 1], I32)
        top = sb("top", [P, TT, 8])
        top_i = sb("top_i", [P, TT, 8], U32)
        top_f = sb("top_f", [P, TT, 8])
        pick = sb("pick", [P, 2, EXPERTS])
        comb = sb("comb", [P, TT, P])

        def route(dve, c):
            bc = lambda a, n: a.unsqueeze(2).to_broadcast([P, TT, n])
            c.step(dve.memset(comb[:], 0.0))
            c.step(dve.memset(zero[:], 0.0))
            c.step(dve.tensor_scalar(order[:], K.iota[:, 0:GROUPS], -1.0, float(GROUPS), ALU.mult, ALU.add))
            dve.wait_ge(logits_made, 1)
            c.do(dve.tensor_tensor(lg[:], K.bank[:, 0, 0:TT * EXPERTS].rearrange("p (t e) -> p t e", t=TT),
                                   router_b[:].unsqueeze(1).to_broadcast([P, TT, EXPERTS]), ALU.add))
            c.do(dve.tensor_reduce(col[:, 0, :], lg[:], AX.X, ALU.max))
            dve.tensor_tensor(pr[:], lg[:], bc(col[:, 0, :], EXPERTS), ALU.subtract).then_inc(exp_ready, 1)
            dve.wait_ge(exp_made, 1)
            c.do(dve.tensor_reduce(col[:, 1, :], ex[:], AX.X, ALU.add))
            c.do(dve.reciprocal(col[:, 1, :], col[:, 1, :]))
            c.do(dve.tensor_tensor(pr[:], ex[:], bc(col[:, 1, :], EXPERTS), ALU.mult))
            g4 = pr[:].rearrange("p t (g e) -> p (t g) e", e=PER_GROUP)
            c.step(dve.tensor_tensor(pairs[:, :, 0:3], g4[:, :, 0:3], g4[:, :, 1:4], ALU.add))
            c.step(dve.tensor_tensor(pairs[:, :, 3:5], g4[:, :, 0:2], g4[:, :, 2:4], ALU.add))
            c.do(dve.tensor_tensor(pairs[:, :, 5:6], g4[:, :, 0:1], g4[:, :, 3:4], ALU.add))
            c.do(dve.tensor_reduce(grp[:, 0, :, :].rearrange("p t g -> p (t g)"), pairs[:], AX.X, ALU.max))
            c.do(dve.tensor_reduce(col[:, 2, :], grp[:, 0, :, :], AX.X, ALU.max))
            c.do(dve.tensor_tensor(grp[:, 1, :, :], grp[:, 0, :, :], bc(col[:, 2, :], GROUPS), ALU.is_ge))
            c.do(dve.tensor_tensor(grp[:, 2, :, :], grp[:, 1, :, :], order[:].unsqueeze(1).to_broadcast([P, TT, GROUPS]),
                                   ALU.mult))
            c.do(dve.tensor_reduce(col[:, 3, :], grp[:, 2, :, :], AX.X, ALU.max))
            dve.tensor_tensor(group[:], grp[:, 2, :, :], bc(col[:, 3, :], GROUPS), ALU.is_equal).then_inc(group_ready, 1)
            dve.wait_ge(group_ready, 1)
            chosen = group[:].rearrange("p t g -> p (t g)").unsqueeze(2).to_broadcast([P, TT * GROUPS, PER_GROUP])
            lg4 = lg[:].rearrange("p t (g e) -> p (t g) e", e=PER_GROUP)
            pr4 = pr[:].rearrange("p t (g e) -> p (t g) e", e=PER_GROUP)
            c.step(dve.tensor_scalar(pr4, chosen, -NEG, NEG, ALU.mult, ALU.add))
            c.do(dve.tensor_tensor(lg4, lg4, chosen, ALU.mult))
            c.do(dve.tensor_tensor(lg[:], lg[:], pr[:], ALU.add))
            for tt in range(TT):
                c.step(dve.max(top[:, tt, :], lg[:, tt, :]))
            c.settle()
            for tt in range(TT):
                c.step(dve.max_index(top_i[:, tt, :], top[:, tt, :], lg[:, tt, :]))
            dve.tensor_tensor(col[:, 4, :], top[:, :, 1], top[:, :, 0], ALU.subtract).then_inc(exp_ready, 1)
            c.settle()
            c.do(dve.tensor_copy(top_f[:], top_i[:]))
            dve.wait_ge(ranks_made, 1)
            c.step(dve.tensor_reduce(col[:, 7, 0:1], K.bank[:, 3, 0:GROUPS], AX.X, ALU.min))
            c.do(dve.tensor_tensor(rank_in[:], K.bank[:, 1:1 + TT, 0:GROUPS], group[:], ALU.mult))
            dve.tensor_scalar(flag[:], col[:, 7, 0:1], -float(P), None, ALU.is_lt).then_inc(flag_ready, 1)
            c.do(dve.tensor_reduce(col[:, 8, :], rank_in[:], AX.X, ALU.add))
            c.do(dve.tensor_scalar(col[:, 8, :], col[:, 8, :], -1.0, -1.0, ALU.mult, ALU.add))
            for tt in range(TT):
                c.step(dve.tensor_scalar(eq[:, tt, :], K.iota, col[:, 8, tt:tt + 1], None, ALU.is_equal))
            dve.wait_ge(flag_ready, 1)
            dve.wait_ge(exp_made, 2)
            c.do(dve.tensor_scalar(col[:, 6, :], col[:, 5, :], 1.0, None, ALU.add))
            c.do(dve.reciprocal(col[:, 6, :], col[:, 6, :]))
            c.do(dve.tensor_tensor(col[:, 7, :], col[:, 5, :], col[:, 6, :], ALU.mult))

        def combine(dve, c):
            for tt in range(TT):
                for m in range(2):
                    c.step(dve.tensor_scalar(pick[:, m, :], K.iota[:, 0:EXPERTS], top_f[:, tt, m:m + 1],
                                             col[:, 6 + m, tt:tt + 1], ALU.is_equal, ALU.mult))
                c.settle()
                c.do(dve.tensor_tensor(comb[:, tt, 0:EXPERTS], pick[:, 0, :], pick[:, 1, :], ALU.add))
            dve.sem_inc(weights_ready, 1)

        made, scattered, hot_ready, wide_ready, taken = (s_(s) for s in ("made", "scattered", "hot_ready", "wide", "taken"))
        slots = tokens[:].rearrange("p (k g s) -> p k g s", k=KD, g=GROUPS)
        slot_comb = wide[:].rearrange("p (t e s) -> p t e s", t=TT, e=EXPERTS)
        y_g, hotT_g = wide[:, 0:D], wide[:, D:D + T]
        gated_s, prod_s = hid[:, 1, 0:2, :].rearrange("p a b -> p (a b)"), hid[:, 1, 2:4, :].rearrange("p a b -> p (a b)")
        hid_s = hid[:, 0, :, :].rearrange("p (a b) (c s) -> p a (b c) s", a=2, s=P)
        FIRST = 14

        def place(i, r, m):
            c = n0 + max(3 * r - 1, 0) + m if i is None else n0 + 3 * (PER_GROUP + r) - 1 + m
            land = 16 * (c // RING + 1)
            return c % RING, land if i is None else 3 * PER_GROUP // RING * 16 * i + land

        def expert(i, r):
            return r if i is None else PER_GROUP * i + (PER_GROUP + r)

        def tensor_gathered(pe):
            pe.sem_inc(scattered, 1)
            pe.wait_ge(hot_ready, TT)
            for g in range(GROUPS):
                for tt in range(TT):
                    last = pe.transpose(K.bank[:, g // 2, (g % 2) * T + tt * P:(g % 2) * T + (tt + 1) * P],
                                        hot[:, tt, g, :], K.ident)
                if g % 2:
                    last.then_inc(made, 1)
            for k in range(KD):
                if k >= 6:
                    pe.wait_ge(copied, k - 5)
                for tt in range(TT):
                    last = pe.matmul(K.bank[:, (2 + k) % 8, :], h[:, tt, k * P:(k + 1) * P],
                                     hot[:, tt, :, :].rearrange("p g s -> p (g s)"), start=(tt == 0), stop=(tt == 1))
                last.then_inc(made, 1)
            for n in range(4):
                pe.wait_ge(copied, 3 + n)
                for tt in range(TT):
                    pe.wait_ge(wide_ready, tt + 1)
                    last = pe.matmul(K.bank[:, 2 + n, :], K.ones_neg, slot_comb[:, tt, 4 * n:4 * n + 4, :],
                                     start=(tt == 0), stop=(tt == 1))
                last.then_inc(made, 1)
            pe.wait_ge(copied, FIRST)
            for b in range(4):
                pe.matmul(K.bank[:, b, :], zero[:, 0:P], zero[:], start=True, stop=False)

            def up_product(i, r, m):
                slot, land = place(i, r, m)
                pe.wait_ge(K.landed[slot], land)
                w = K.ring[:, slot, :].rearrange("p (k c) -> p k c", k=KD)
                for c in range(4):
                    for k in range(KD):
                        x = slots[:, k, 0, :] if i is None else slots[:, k, bass.ds(i + 1, 1), :].rearrange("p o s -> p (o s)")
                        last = pe.matmul(K.bank[:, 4 + m, c * P:(c + 1) * P], w[:, k, c * P:(c + 1) * P], x,
                                         start=(k == 0), stop=(k == KD - 1))
                last.then_inc(K.chunk_used, 1)

            def down_product(slot, land, r):
                pe.wait_ge(K.landed[slot], land)
                w = K.ring[:, slot, :].rearrange("p (k c) -> p k c", k=4)
                for k in range(4):
                    for dh in range(2):
                        last = pe.matmul(K.bank[:, 6 + dh, :], hid_s[:, r % 2, k, :], w[:, k, dh * 512:(dh + 1) * 512],
                                         start=(r == 0 and k == 0), stop=(r == PER_GROUP - 1 and k == 3))
                last.then_inc(K.chunk_used, 1)

            def scatter(count, stop):
                pe.wait_ge(taken, count)
                for tt in range(TT):
                    for dh in range(2):
                        last = pe.matmul(K.bank[:, 2 * tt + dh, :], hotT_g[:, tt * P:(tt + 1) * P],
                                         y_g[:, dh * 512:(dh + 1) * 512], start=False, stop=stop)
                last.then_inc(scattered, 1)

            def experts(i):
                for r in range(PER_GROUP):
                    first = i is None and r == 0
                    e = expert(i, r)
                    if not first:
                        pe.wait_ge(silu_done, e)
                    up_product(i, r, 0)
                    if not first:
                        pe.wait_ge(prod_done, e)
                    up_product(i, r, 1)
                    if i is not None and r == 1:
                        scatter(i + 1, False)
                    if not first:
                        pe.wait_ge(hidden_done, e)
                        down_product(*place(i, r, 2), (r - 1) % PER_GROUP)

            experts(None)
            with pe.Fori(0, GROUPS - 1) as i:
                experts(i)
            pe.wait_ge(hidden_done, EXPERTS)
            down_product((n_end - 1) % RING, 16 * ((n_end - 1) // RING + 1), PER_GROUP - 1)
            scatter(GROUPS, True)

        def scalar_gathered(act):
            outs = [hotT[:, 0:2, :], hotT[:, 2:4, :]] + [slots[:, k, :, :] for k in range(KD)]
            for n, out in enumerate(outs):
                act.wait_ge(made, n + 1)
                act.activation(out, K.bank[:, n % 8, :].rearrange("p (a b) -> p a b", a=out.shape[1]), ACT.Copy).then_inc(copied, 1)
            for n in range(4):
                act.wait_ge(made, len(outs) + n + 1)
                act.activation(weights[:, 4 * n:4 * n + 4, :], K.bank[:, 2 + n, :].rearrange("p (e s) -> p e s", e=4),
                               ACT.Copy, scale=-1.0).then_inc(copied, 1)

            def take(g, used):
                act.wait_ge(K.chunk_used, used)
                act.wait_ge(scattered, g + 1)
                source = hotT[:, g, :] if isinstance(g, int) else hotT[:, bass.ds(g, 1), :].rearrange("p o t -> p (o t)")
                act.activation(hotT_g, source, ACT.Copy)
                act.activation(y_g, K.bank[:, 6:8, :].rearrange("p b c -> p (b c)"), ACT.Copy).then_inc(taken, 1)

            def experts(i):
                for r in range(PER_GROUP):
                    first = i is None and r == 0
                    e = expert(i, r)
                    act.wait_ge(K.chunk_used, n0 + 1 if first else 3 * e + n0)
                    if not first:
                        act.wait_ge(prod_done, e)
                    act.activation(gated_s, K.bank[:, 4, :], ACT.Silu).then_inc(silu_done, 1)
                    if i is not None and r == 0:
                        take(i, 3 * PER_GROUP * i + (n0 + 3 * PER_GROUP + 2))

            experts(None)
            with act.Fori(0, GROUPS - 1) as i:
                experts(i)
            take(GROUPS - 1, n_end)

        def vector_gathered(dve, c):
            for tt in range(TT):
                dve.tensor_tensor(hot[:, tt, :, :], eq[:, tt, :].unsqueeze(1).to_broadcast([P, GROUPS, P]),
                                  group[:, tt, :].unsqueeze(2).to_broadcast([P, GROUPS, P]), ALU.mult).then_inc(hot_ready, 1)
            combine(dve, c)
            for tt in range(TT):
                dve.tensor_tensor(slot_comb[:, tt, :, :], eq[:, tt, :].unsqueeze(1).to_broadcast([P, EXPERTS, P]),
                                  comb[:, tt, 0:EXPERTS].unsqueeze(2).to_broadcast([P, EXPERTS, P]), ALU.mult).then_inc(wide_ready, 1)

            def experts(i):
                for r in range(PER_GROUP):
                    first = i is None and r == 0
                    e = expert(i, r)
                    dve.wait_ge(K.chunk_used, n0 + 2 if first else 3 * e + (n0 + 1))
                    dve.wait_ge(silu_done, e + 1)
                    if not first:
                        dve.wait_ge(hidden_done, e)
                    dve.tensor_tensor(prod_s, gated_s, K.bank[:, 5, :], ALU.mult).then_inc(prod_done, 1)
                    dve.wait_ge(prod_done, e + 1)
                    if first:
                        dve.wait_ge(copied, FIRST)
                    w = weights[:, e, :] if i is None else weights[:, bass.ds(e, 1), :].rearrange("p o s -> p (o s)")
                    dve.tensor_tensor(hid_s[:, r % 2, :, :], prod_s.rearrange("p (c s) -> p c s", c=4),
                                      w.unsqueeze(1).to_broadcast([P, 4, P]), ALU.mult).then_inc(hidden_done, 1)

            experts(None)
            with dve.Fori(0, GROUPS - 1) as i:
                experts(i)

        w_all = tokens[:].rearrange("p (e t) -> p e t", e=EXPERTS)
        diag = wide[:].rearrange("p (e t) -> p e t", e=EXPERTS)
        room = weights[:].rearrange("p e s -> p (e s)")
        gated, prod = room[:, 0:1024].rearrange("p (j c) -> p j c", j=2), room[:, 1024:2048].rearrange("p (c t) -> p c t", c=4)
        LOOPS = (EXPERTS - 2) // 2

        def tensor_dense(pe):
            def down(slot, land, e_parity, start, stop):
                pe.wait_ge(K.landed[slot], land)
                w = K.ring[:, slot, :].rearrange("p (k c) -> p k c", k=4)
                for tt in range(TT):
                    for k in range(4):
                        for dh in range(2):
                            last = pe.matmul(K.bank[:, 2 * tt + dh, :], hid[:, e_parity, k, tt * P:(tt + 1) * P],
                                             w[:, k, dh * 512:(dh + 1) * 512], start=(start and k == 0),
                                             stop=(stop and k == 3))
                last.then_inc(K.chunk_used, 1)

            pe.wait_ge(weights_ready, 1)
            for tt in range(TT):
                last = pe.transpose(K.bank[:, 1, tt * P:(tt + 1) * P], comb[:, tt, :], K.ident)
            last.then_inc(made, 1)
            pe.wait_ge(wide_ready, 1)
            for n in range(EXPERTS // 2):
                if n >= 4:
                    pe.wait_ge(copied, n - 3)
                pe.matmul(K.bank[:, n % 4, :], K.ones_neg, diag[:, 2 * n:2 * n + 2, :], start=True,
                          stop=True).then_inc(spread, 1)
            feature_product(pe, K, n0, K.hT, 4)
            feature_product(pe, K, n0 + 1, K.hT, 6)
            pe.wait_ge(silu_done, 2)
            feature_product(pe, K, n0 + 2, K.hT, 4)
            pe.wait_ge(prod_done, 2)
            feature_product(pe, K, n0 + 3, K.hT, 6)
            pe.wait_ge(hidden_done, 1)
            pe.wait_ge(copied, 8)
            down((n0 + 4) % RING, 16 * ((n0 + 4) // RING + 1), 0, True, False)
            with pe.Fori(0, LOOPS) as i:
                for r in range(2):
                    c = n0 + 5 + 3 * r
                    slot = [(c + m) % RING for m in range(3)]
                    land = [16 * i + 16 * ((c + m) // RING + 1) for m in range(3)]
                    pe.wait_ge(silu_done, 4 * i + (4 + 2 * r))
                    feature_product(pe, K, None, K.hT, 4, slot[0], land[0])
                    pe.wait_ge(prod_done, 4 * i + (4 + 2 * r))
                    feature_product(pe, K, None, K.hT, 6, slot[1], land[1])
                    pe.wait_ge(hidden_done, 2 * i + (2 + r))
                    down(slot[2], land[2], 1 - r, False, False)
            pe.wait_ge(hidden_done, EXPERTS)
            down((n_end - 1) % RING, 16 * ((n_end - 1) // RING + 1), 1, False, True)

        def scalar_dense(act):
            def silu_gate(e, gate_chunks):
                act.wait_ge(K.chunk_used, gate_chunks)
                for j in range(2):
                    if not (isinstance(e, int) and e == 0):
                        act.wait_ge(prod_done, 2 * e - 1 + j)
                    act.activation(gated[:, j, :], K.bank[:, 4 + j, :], ACT.Silu).then_inc(silu_done, 1)

            for n in range(EXPERTS // 2):
                act.wait_ge(spread, n + 1)
                act.activation(w_all[:, 2 * n:2 * n + 2, :], K.bank[:, n % 4, :].rearrange("p (e t) -> p e t", e=2),
                               ACT.Copy, scale=-1.0).then_inc(copied, 1)
            silu_gate(0, n0 + 1)
            silu_gate(1, n0 + 3)
            with act.Fori(0, LOOPS) as i:
                for r in range(2):
                    silu_gate(2 * i + (2 + r), 6 * i + (n0 + 6 + 3 * r))

        def vector_dense(dve, c):
            def make_hidden(e, parity, up_chunks):
                dve.wait_ge(K.chunk_used, up_chunks)
                if not (isinstance(e, int) and e == 0):
                    dve.wait_ge(hidden_done, e)
                for j in range(2):
                    dve.wait_ge(silu_done, 2 * e + j + 1)
                    dve.tensor_tensor(prod[:, 2 * j:2 * j + 2, :], gated[:, j, :].rearrange("p (c t) -> p c t", c=2),
                                      K.bank[:, 6 + j, :].rearrange("p (c t) -> p c t", c=2), ALU.mult).then_inc(prod_done, 1)
                if isinstance(e, int) and e == 0:
                    dve.wait_ge(copied, 8)
                dve.wait_ge(prod_done, 2 * e + 2)
                w = w_all[:, e, :] if isinstance(e, int) else w_all[:, bass.ds(e, 1), :].rearrange("p o t -> p (o t)")
                dve.tensor_tensor(hid[:, parity, :, :], prod[:], w.unsqueeze(1).to_broadcast([P, 4, T]),
                                  ALU.mult).then_inc(hidden_done, 1)

            combine(dve, c)
            dve.wait_ge(made, 1)
            dve.tensor_tensor(diag[:], K.bank[:, 1, 0:T].unsqueeze(1).to_broadcast([P, EXPERTS, T]),
                              K.ident[:, 0:EXPERTS].unsqueeze(2).to_broadcast([P, EXPERTS, T]),
                              ALU.mult).then_inc(wide_ready, 1)
            make_hidden(0, 0, n0 + 2)
            make_hidden(1, 1, n0 + 4)
            with dve.Fori(0, LOOPS) as i:
                for r in range(2):
                    make_hidden(2 * i + (2 + r), r, 6 * i + (n0 + 7 + 3 * r))

        with nc.Block() as block:
            @block.sync
            def _(sp):
                sp.dma_start(router[:], K.A["router_w"]).then_inc(small_in, 16)
                sp.dma_start(router_b[:], K.A["router_b"].to_broadcast([P, EXPERTS])).then_inc(small_in, 16)
                LOOPS = (n_end - n0 - RING) // RING
                assert K.fetched == n0 + RING and (n_end - n0) % RING == 0
                with sp.Fori(0, LOOPS) as i:
                    for j in range(RING):
                        slot = (n0 + j) % RING
                        sp.wait_ge(K.chunk_used, 6 * i + (n0 + j + 1))
                        sp.dma_start(K.ring[:, slot, :], K.A["stream"][6 * i + (n0 + RING + j)]).then_inc(K.landed[slot], 16)
                K.fetched = n_end
                fetch_chunks(sp, K, n_end + RING)

            @block.tensor
            def _(pe):
                pe.wait_ge(small_in, 32)
                for tt in range(TT):
                    for k in range(KD):
                        last = pe.matmul(K.bank[:, 0, tt * EXPERTS:(tt + 1) * EXPERTS], K.hT[:, k, tt * P:(tt + 1) * P],
                                         router[:, k, :], start=(k == 0), stop=(k == KD - 1))
                last.then_inc(logits_made, 1)
                pe.wait_ge(group_ready, 1)
                pe.matmul(K.bank[:, 1, 0:GROUPS], K.tri_neg, group[:, 0, :], start=True, stop=False)
                pe.matmul(K.bank[:, 1, 0:GROUPS], K.ones_neg, group[:, 1, :], start=False, stop=True)
                pe.matmul(K.bank[:, 2, 0:GROUPS], K.tri_neg, group[:, 1, :], start=True, stop=True)
                pe.matmul(K.bank[:, 3, 0:GROUPS], K.ones_neg, group[:, 0, :], start=True, stop=False)
                pe.matmul(K.bank[:, 3, 0:GROUPS], K.ones_neg, group[:, 1, :], start=False, stop=True).then_inc(ranks_made, 1)
                pe.wait_ge(flag_ready, 1)
                crowded = pe.value_load(flag[0:1, 0:1])
                with pe.If(crowded):
                    tensor_dense(pe)
                with pe.Else():
                    tensor_gathered(pe)

            @block.scalar
            def _(act):
                act.wait_ge(exp_ready, 1)
                act.activation(ex[:], pr[:], ACT.Exp).then_inc(exp_made, 1)
                act.wait_ge(exp_ready, 2)
                act.activation(col[:, 5, :], col[:, 4, :], ACT.Exp).then_inc(exp_made, 1)
                act.wait_ge(flag_ready, 1)
                crowded = act.value_load(flag[0:1, 0:1])
                with act.If(crowded):
                    scalar_dense(act)
                with act.Else():
                    scalar_gathered(act)

            @block.vector
            def _(dve):
                c = Chain(dve, chain)
                route(dve, c)
                crowded = dve.value_load(flag[0:1, 0:1])
                steps = c.n
                with dve.If(crowded):
                    vector_dense(dve, c)
                with dve.Else():
                    c.n = steps
                    vector_gathered(dve, c)
    ada.h_scope.close()
    return layer_norm_stage(K, name, 2 * layer + 1, None, following)



def sine_tables(dve, c, turns, scratch, cos_in, sin_in):
    c.do(dve.tensor_scalar(scratch, turns, ROUND, -ROUND, ALU.add, ALU.add))
    c.step(dve.tensor_tensor(sin_in, turns, scratch, ALU.subtract))
    c.do(dve.tensor_scalar(cos_in, turns, 0.25, None, ALU.add))
    c.do(dve.tensor_scalar(scratch, cos_in, ROUND, -ROUND, ALU.add, ALU.add))
    return dve.tensor_tensor(cos_in, cos_in, scratch, ALU.subtract)


def retention_stage(K):
    nc = K.nc
    n0 = START["ret_in"]
    s_ = lambda s: K.sem(f"ret_{s}")
    small_in, pos_in, turns_ready, trig_ready, chain = (s_(s) for s in ("small_in", "pos_in", "turns", "trig", "dve"))
    act_done, dve_done, swapped, rotated = (s_(s) for s in ("act_done", "dve_done", "swapped", "rotated"))
    s_made, decayed, o_made, o_copied, gn_in = (s_(s) for s in ("s_made", "decayed", "o_made", "o_copied", "gn_in"))
    var_ready, std_ready, out_ready, turned, oT_ready, gate_ready = (
        s_(s) for s in ("var", "std", "out", "turned", "oT", "gate"))
    with ExitStack() as stage:
        sb = lambda n, s, dt=F32: stage.enter_context(nc.sbuf_tensor(f"ret_{n}", s, dt))
        qkT = sb("qkT", [P, 2 * KD, T])
        heads = stage.enter_context(ExitStack())
        sb = lambda n, s, dt=F32: heads.enter_context(nc.sbuf_tensor(f"ret_{n}", s, dt))
        gate = sb("gate", [P, TT, 2 * D])
        v = sb("v", [P, TT, 2 * D])
        o = sb("o", [P, TT, 2 * D])
        decay = sb("decay", [P, RET_HEADS, 2 * P])
        scr = K.mod[:, 0:1024].rearrange("p (n c) -> p n c", n=2)
        trig = K.mod[:, 1024:1024 + 2 * T].rearrange("p (n t) -> p n t", n=2)
        freq = sb("freq", [P, 1])
        stats, mv, std = sb("stats", [P, RET_HEADS, TT, 6]), sb("mv", [P, RET_HEADS, TT, 2]), sb("std", [P, RET_HEADS, TT])
        eps = sb("eps", [P, 1])

        with nc.Block() as block:
            pos = o[:, 0, 0:T].bitcast(I32)
            ang = o[:, 0, T:2 * T]

            @block.sync
            def _(sp):
                sp.dma_start(pos, K.A["positions"].to_broadcast([P, T])).then_inc(pos_in, 16)
                sp.dma_start(freq[:], K.A["inv_freq"]).then_inc(pos_in, 16)
                sp.dma_start(decay[:], K.A["decay"]).then_inc(small_in, 16)
                sp.dma_start(o[:, 1, :], K.A["ret_gn_g"].to_broadcast([P, 2 * D])).then_inc(gn_in, 16)
                fetch_chunks(sp, K, START["ret_out"] + RING)

            @block.tensor
            def _(pe):
                for j in range(12):
                    b = 2 * j % 6
                    if j >= 3:
                        pe.wait_ge(act_done, j - 2)
                        pe.wait_ge(dve_done, j - 2)
                    if j < 4:
                        feature_product(pe, K, n0 + j, K.hT, b)
                    else:
                        token_product(pe, K, n0 + j, K.hT, [K.bank[:, b + tt, :] for tt in range(TT)])
                    if 1 <= j <= 4:
                        for i in range(2):
                            n = 2 * (j - 1) + i
                            pe.wait_ge(act_done if i == 0 else dve_done, j)
                            if n >= 2:
                                pe.wait_ge(rotated, n - 1)
                            pe.matmul(K.bank[:, 6 + n % 2, :], K.swap128, qkT[:, 2 * n:2 * n + 2, :], start=True,
                                      stop=True).then_inc(swapped, 1)

            def source(j, i):
                return K.bank[:, 2 * j % 6 + i, :]

            @block.scalar
            def _(act):
                act.wait_ge(turns_ready, 1)
                act.activation(trig, trig, ACT.Sin, scale=TWO_PI).then_inc(trig_ready, 1)
                for j in range(12):
                    act.wait_ge(K.chunk_used, n0 + j + 1)
                    if j < 4:
                        act.activation(qkT[:, 4 * j:4 * j + 2, :], source(j, 0).rearrange("p (c t) -> p c t", c=2),
                                       ACT.Copy, scale=1.0 if j < 2 else P ** -0.5).then_inc(act_done, 1)
                    elif j < 8:
                        act.activation(v[:, 0, (j - 4) * 512:(j - 3) * 512], source(j, 0), ACT.Copy).then_inc(act_done, 1)
                    else:
                        for i in range(TT):
                            last = act.activation(gate[:, i, (j - 8) * 512:(j - 7) * 512], source(j, i), ACT.Silu)
                        last.then_inc(act_done, 1)

            @block.vector
            def _(dve):
                c = Chain(dve, chain)
                c.step(dve.memset(eps[:], LN_EPS))
                dve.wait_ge(pos_in, 32)
                c.do(dve.tensor_copy(ang, pos))
                c.do(dve.tensor_scalar(ang, ang, freq[:, 0:1], 1.0 / (2.0 * np.pi), ALU.mult, ALU.mult))
                sine_tables(dve, c, ang, scr[:, 0, 0:T], trig[:, 0, :], trig[:, 1, :]).then_inc(turns_ready, 1)

                def rotate(n):
                    x = qkT[:, 2 * n:2 * n + 2, :]
                    two = lambda r: trig[:, r, :].unsqueeze(1).to_broadcast([P, 2, T])
                    s2 = scr[:, n % 2, :].rearrange("p (c t) -> p c t", c=2)
                    dve.wait_ge(swapped, n + 1)
                    c.step(dve.tensor_tensor(s2, K.bank[:, 6 + n % 2, :].rearrange("p (c t) -> p c t", c=2), two(1), ALU.mult))
                    c.do(dve.tensor_tensor(x, x, two(0), ALU.mult))
                    dve.tensor_tensor(x, x, s2, ALU.add).then_inc(rotated, 1)

                for j in range(12):
                    if j == 1:
                        dve.wait_ge(trig_ready, 1)
                    dve.wait_ge(K.chunk_used, n0 + j + 1)
                    if j < 4:
                        dve.tensor_scalar(qkT[:, 4 * j + 2:4 * j + 4, :], source(j, 1).rearrange("p (c t) -> p c t", c=2),
                                          1.0 if j < 2 else P ** -0.5, None, ALU.mult).then_inc(dve_done, 1)
                    elif j < 8:
                        dve.tensor_copy(v[:, 1, (j - 4) * 512:(j - 3) * 512], source(j, 1)).then_inc(dve_done, 1)
                    else:
                        dve.wait_ge(act_done, j + 1)
                        dve.wait_ge(gn_in, 16)
                        cols = slice((j - 8) * 512, (j - 7) * 512)
                        dve.tensor_tensor(gate[:, :, cols], gate[:, :, cols],
                                          o[:, 1, cols].unsqueeze(1).to_broadcast([P, TT, 512]), ALU.mult).then_inc(dve_done, 1)
                    if 1 <= j <= 4:
                        rotate(2 * (j - 1))
                        rotate(2 * (j - 1) + 1)

        W = T + P
        with nc.Block() as block:
            sbank = lambda h: K.bank[:, h % 2, 0:W]
            obank = lambda h: K.bank[:, 2 + h % 2, :]
            s_b = scr[:, :, 0:W]

            @block.tensor
            def _(pe):
                for i in range(RET_HEADS + 1):
                    if i < RET_HEADS:
                        if i >= 2:
                            pe.wait_ge(decayed, i - 1)
                        qT, kT = qkT[:, i, :], qkT[:, KD + i, :]
                        pe.matmul(sbank(i)[:, 0:T], kT[:, 0:P], qT, start=True, stop=True)
                        pe.matmul(sbank(i)[:, T:W], kT[:, P:T], qT[:, P:T], start=True, stop=True).then_inc(s_made, 1)
                    h = i - 1
                    if h >= 0:
                        if h >= 2:
                            pe.wait_ge(o_copied, h - 1)
                        pe.wait_ge(decayed, h + 1)
                        s, vh = s_b[:, h % 2, :], v[:, :, h * RET_V:(h + 1) * RET_V]
                        pe.matmul(obank(h)[:, 0:RET_V], s[:, 0:P], vh[:, 0, :], start=True, stop=True)
                        pe.matmul(obank(h)[:, RET_V:], s[:, P:T], vh[:, 0, :], start=True, stop=False)
                        pe.matmul(obank(h)[:, RET_V:], s[:, T:W], vh[:, 1, :], start=False, stop=True).then_inc(o_made, 1)

            @block.scalar
            def _(act):
                for h in range(RET_HEADS):
                    act.wait_ge(o_made, h + 1)
                    act.activation(o[:, :, h * RET_V:(h + 1) * RET_V], obank(h).rearrange("p (t e) -> p t e", t=TT),
                                   ACT.Copy).then_inc(o_copied, 1)
                act.wait_ge(var_ready, 1)
                act.activation(std[:], mv[:, :, :, 1], ACT.Sqrt, bias=eps[:]).then_inc(std_ready, 1)

            @block.vector
            def _(dve):
                c = Chain(dve, K.sem("ret_dve2"))
                dve.wait_ge(small_in, 16)
                for i in range(RET_HEADS + 1):
                    if i < RET_HEADS:
                        dve.wait_ge(s_made, i + 1)
                        if i >= 2:
                            dve.wait_ge(o_made, i - 1)
                        s = s_b[:, i % 2, :]
                        dve.tensor_tensor(s[:, 0:T], sbank(i)[:, 0:T], decay[:, i, :], ALU.mult)
                        dve.tensor_tensor(s[:, T:W], sbank(i)[:, T:W], decay[:, i, 0:P], ALU.mult).then_inc(decayed, 1)
                    h = i - 1
                    if h >= 0:
                        dve.wait_ge(o_copied, h + 1)
                        for tt in range(TT):
                            c.step(dve.bn_stats(stats[:, h, tt, :], o[:, tt, h * RET_V:(h + 1) * RET_V]))
                c.settle()
                for h in range(RET_HEADS):
                    for tt in range(TT):
                        last = c.step(dve.bn_aggr(mv[:, h, tt, :], stats[:, h, tt, :]))
                c.settle()
                dve.sem_inc(var_ready, 1)
                dve.wait_ge(std_ready, 1)
                c.do(dve.reciprocal(std[:], std[:]))
                for h in range(RET_HEADS):
                    cols = slice(h * RET_V, (h + 1) * RET_V)
                    for tt in range(TT):
                        c.step(dve.tensor_scalar(o[:, tt, cols], o[:, tt, cols], mv[:, h, tt, 0:1], std[:, h, tt:tt + 1],
                                                 ALU.subtract, ALU.mult))
                    c.settle()
                    dve.tensor_tensor(o[:, :, cols], o[:, :, cols], gate[:, :, cols], ALU.mult).then_inc(out_ready, 1)

        with nc.Block() as block:
            @block.tensor
            def _(pe):
                for k in range(2 * KD):
                    if k >= 16:
                        pe.wait_ge(oT_ready, k // 2 - 7)
                    for tt in range(TT):
                        out = K.bank[:, k // 2 % 8, (k % 2) * T + tt * P:(k % 2) * T + (tt + 1) * P]
                        last = pe.transpose(out, o[:, tt, k * P:(k + 1) * P], K.ident)
                    if k % 2:
                        last.then_inc(turned, 1)

            @block.scalar
            def _(act):
                for b in range(0, 8, 2):
                    act.wait_ge(turned, b + 1)
                    act.activation(qkT[:, 2 * b:2 * b + 2, :], K.bank[:, b, :].rearrange("p (k t) -> p k t", k=2), ACT.Copy)

            @block.vector
            def _(dve):
                for b in range(1, 8, 2):
                    dve.wait_ge(turned, b + 1)
                    dve.tensor_copy(qkT[:, 2 * b:2 * b + 2, :], K.bank[:, b, :].rearrange("p (k t) -> p k t", k=2))
        heads.close()

        def project(pe):
            for dh in range(2):
                for r in range(2):
                    token_product(pe, K, START["ret_out"] + 2 * dh + r, qkT[:, r * KD:(r + 1) * KD, :],
                                  [K.bank[:, 2 * tt + dh, :] for tt in range(TT)], start=(r == 0), stop=(r == 1))
        return layer_norm_stage(K, "ret_out", 2, project, "ada11")



def rms_norm_turn_stage(K, name, gain, before=None, keep=None, out=None):
    nc = K.nc
    row_in, chain, ss_ready, std_ready, h_ready, turned, evac = (
        K.sem(f"{name}_{s}") for s in ("row_in", "dve", "ss", "std", "h", "turned", "evac"))
    with ExitStack() as stage, nc.Block() as block:
        sb = lambda n, s: stage.enter_context(nc.sbuf_tensor(f"{name}_{n}", s, F32))
        g_row, h = sb("g", [P, D]), sb("hbuf", [P, TT, D])
        ss, eps = sb("ss", [P, TT]), sb("eps", [P, 1])

        @block.sync
        def _(sp):
            sp.dma_start(g_row[:], K.A[gain].to_broadcast([P, D])).then_inc(row_in, 16)
            if out is not None:
                sp.wait_ge(h_ready, TT)
                sp.dma_start(out, h[:]).then_inc(K.stored, 16)
                sp.wait_ge(K.stored, 16)

        @block.scalar
        def _(act):
            for tt in range(TT):
                act.wait_ge(ss_ready, tt + 1)
                act.activation(h[:, tt, :], K.x[:, tt, :], ACT.Square, accum_out=ss[:, tt:tt + 1]).then_inc(std_ready, 1)
            act.wait_ge(std_ready, TT)
            act.activation(ss[:], ss[:], ACT.Sqrt, bias=eps[:], scale=1.0 / D).then_inc(std_ready, 1)
            if out is None:
                evacuate_turned(act, K, turned, evac)

        if out is None:
            @block.tensor
            def _(pe):
                turn_tokens(pe, K, h, h_ready, turned)

        @block.vector
        def _(dve):
            c = Chain(dve, chain)
            c.do(dve.memset(eps[:], RMS_EPS))
            for tt in range(TT):
                if before is not None:
                    before(dve, c, tt)
                    c.settle()
                dve.sem_inc(ss_ready, 1)
            dve.wait_ge(std_ready, TT + 1)
            c.do(dve.reciprocal(ss[:], ss[:]))
            dve.wait_ge(row_in, 16)
            for tt in range(TT):
                dve.scalar_tensor_tensor(h[:, tt, :], K.x[:, tt, :], ss[:, tt:tt + 1], g_row[:], ALU.mult,
                                         ALU.mult).then_inc(h_ready, 1)


S5_TILES = 16


def projection_and_s5_stage(K, S):
    nc = K.nc
    n0 = START["in2"]
    act_done, dve_done, swapped, rotated, rope_in, zeroed, chain, gates_done, pool_chain = (
        K.sem(f"in2_{s}") for s in ("act_done", "dve_done", "swapped", "rotated", "rope_in", "zeroed", "dve", "gates", "pool"))
    s_ = lambda s: K.sem(f"s5_{s}")
    small_in, trig_ready, trig_done, b_ready, turned, b_copied = (
        s_(s) for s in ("small_in", "trig_ready", "trig_done", "b_ready", "turned", "b_copied"))
    bu_made, w_used, s_ready, y_made, y_taken, tab_ready, tab_done = (
        s_(s) for s in ("bu_made", "w_used", "s_ready", "y_made", "y_taken", "tab_ready", "tab_done"))
    NT = S5_TILES
    with ExitStack() as stage, nc.Block() as block:
        rope = K.c_wide[:].rearrange("p k c -> p (k c)").rearrange("p (a b t) -> p a b t", a=2, b=2)
        kT = S.yaT[:, 0:2, :]
        scr = K.mod[:, 2 * D:3 * D].rearrange("p (a b t) -> p a b t", a=2, b=2)
        sb = lambda n, s: stage.enter_context(nc.sbuf_tensor(f"s5_{n}", s, F32))
        par = sb("par", [P, 3, NT])
        col = sb("col", [P, 16, NT])
        b_in = sb("b_in", [P, 2, NT, 16])
        b_bar = sb("b_bar", [P, 2, NT, 16])
        b_pad = sb("b_pad", [P, 2, P])
        bT = sb("bT", [P, 2, 2, P])
        cz = sb("cz", [P, 2, NT, P])
        d_skip = sb("d_skip", [P, 4])
        tab = sb("tab", [P, 2, 2, T])
        turns = sb("turns", [P, 2, T])
        w, m, st = (K.mod[:, i * D:(i + 1) * D].rearrange("p (a b t) -> p a b t", a=2, b=2) for i in range(3))
        y = S.yT

        @block.sync
        def _(sp):
            sp.dma_start(rope[:, 0, :, :], K.A["rope64"]).then_inc(rope_in, 16)
            sp.dma_start(rope[:, 1, :, :], K.A["rope32"]).then_inc(rope_in, 16)
            for i, n in enumerate(("a_re", "a_im", "log_dt")):
                sp.dma_start(par[:, i, :], K.A[n]).then_inc(small_in, 16)
            sp.dma_start(b_in[:, 0, :, :], K.A["b_re"]).then_inc(small_in, 16)
            sp.dma_start(b_in[:, 1, :, :], K.A["b_im"]).then_inc(small_in, 16)
            sp.dma_start(d_skip[:], K.A["d_skip"]).then_inc(small_in, 16)
            sp.dma_start(cz[:, 0, :, :], K.A["c_re"]).then_inc(small_in, 16)
            sp.dma_start(cz[:, 1, :, :], K.A["c_im"]).then_inc(small_in, 16)
            fetch_chunks(sp, K, next_start("in2") + RING)

        @block.gpsimd
        def _(pool):
            pool.memset(S.kz[:], 0.0).then_inc(zeroed, 1)
            pool.memset(S.kiz[:], 0.0).then_inc(zeroed, 1)
            pool.memset(S.vz[:], 0.0).then_inc(zeroed, 1)
            c = Chain(pool, pool_chain)
            theta = col[:, 7, :]
            pool.wait_ge(trig_ready, 2)
            pool.wait_ge(K.loaded, 32)
            for j in range(NT):
                if j >= 2:
                    pool.wait_ge(s_ready, j - 1)
                c.step(pool.tensor_scalar(turns[:, 0, 0:P], K.iota, theta[:, j:j + 1], None, ALU.mult))
                c.do(pool.tensor_scalar(turns[:, 0, P:T], K.iota, float(P), theta[:, j:j + 1], ALU.add, ALU.mult))
                sine_tables(pool, c, turns[:, 0, :], turns[:, 1, :], tab[:, j % 2, 0, :], tab[:, j % 2, 1, :]).then_inc(tab_ready, 1)
                pool.wait_ge(tab_ready, j + 1)

        def pair(n):
            return [S.qT[:, 0:2, :], S.qT[:, 2:4, :], kT, S.qiT[:]][n]

        def project_tensor(pe):
            def swap(n, wait, count):
                pe.wait_ge(wait, count)
                if n >= 2:
                    pe.wait_ge(rotated, n - 1)
                out = K.bank[:, 6 + n % 2, :]
                if n == 2:
                    pe.matmul(out[:, 0:T], K.swap64, kT[:, 0, :], start=True, stop=True)
                    pe.matmul(out[:, T:], K.swap32, kT[:, 1, :], start=True, stop=True).then_inc(swapped, 1)
                else:
                    pe.matmul(out, K.swap32 if n == 3 else K.swap64, pair(n), start=True, stop=True).then_inc(swapped, 1)

            for j in range(4):
                b = 2 * j % 6
                if j == 3:
                    pe.wait_ge(act_done, 1)
                    pe.wait_ge(dve_done, 1)
                if j < 3:
                    feature_product(pe, K, n0 + j, K.hT, b)
                else:
                    cols = 136
                    token_product(pe, K, n0 + j, K.hT, [K.bank[:, b + tt, 0:cols] for tt in range(TT)], cols=cols)
                if j == 2:
                    swap(0, act_done, 2)
                    swap(1, dve_done, 2)
                if j == 3:
                    pe.wait_ge(act_done, 3)
                    swap(2, dve_done, 3)
                    swap(3, dve_done, 3)

        def source(j, i):
            return K.bank[:, 2 * j % 6 + i, :]

        tiles = lambda a: a.rearrange("p (c t) -> p c t", c=2)

        def project_scalar(act):
            for j in range(4):
                act.wait_ge(K.chunk_used, n0 + j + 1)
                if j < 2:
                    dst = S.uT[:, 0:2, :] if j == 0 else S.qT[:, 0:2, :]
                    act.activation(dst, tiles(source(j, 0)), ACT.Copy).then_inc(act_done, 1)
                elif j == 2:
                    act.activation(kT[:, 0, :], source(j, 0)[:, 0:T], ACT.Copy)
                    act.activation(S.qiT[:, 0, :], source(j, 0)[:, T:], ACT.Copy).then_inc(act_done, 1)
                else:
                    act.wait_ge(zeroed, 3)
                    v = source(j, 0)
                    act.activation(S.vz[:, 0, 0, 0:64], v[:, 0:64], ACT.Copy)
                    act.activation(S.vz[:, 1, 0, 64:P], v[:, 64:P], ACT.Copy)
                    act.activation(S.wi[:, 0, :], v[:, P:136], ACT.Copy, scale=IDX_SCALE).then_inc(act_done, 1)

        def gate_product(pe, j):
            n, q = n0 + 4 + j // 4, j % 4
            if q == 0:
                wait_chunk(pe, K, n)
                pe.wait_ge(rotated, 4)
                if j:
                    pe.wait_ge(gates_done, j // 4)
            w = K.ring[:, n % RING, :].rearrange("p (k c) -> p k c", k=KD)
            for k in range(4 * (q % 2), 4 * (q % 2) + 4):
                last = pe.matmul(K.bank[:, 6 + q // 2, :], K.hT[:, k, q // 2 * P:(q // 2 + 1) * P], w[:, k, :],
                                 start=(k == 0), stop=(k == KD - 1))
            if q == 3:
                last.then_inc(K.chunk_used, 1)

        def take_gate(act, n):
            act.wait_ge(K.chunk_used, n0 + 4 + n + 1)
            for i in range(TT):
                last = act.activation(S.gates[:, n // 2, i, n % 2 * COLS:(n % 2 + 1) * COLS], K.bank[:, 6 + i, :], ACT.Sigmoid)
            last.then_inc(gates_done, 1)

        def project_vector(dve, c):
            def rotate(n):
                x, s2 = pair(n), scr[:, n % 2, :, :]
                which = rope[:, 1 if n == 3 else 0, :, :]
                two = lambda r: which[:, r, :].unsqueeze(1).to_broadcast([P, 2, T])
                if n == 2:
                    two = lambda r: rope[:, :, r, :]
                dve.wait_ge(swapped, n + 1)
                c.step(dve.tensor_tensor(s2, tiles(K.bank[:, 6 + n % 2, :]), two(1), ALU.mult))
                c.do(dve.tensor_tensor(x, x, two(0), ALU.mult))
                if n != 2:
                    dve.tensor_tensor(x, x, s2, ALU.add).then_inc(rotated, 1)
                    return
                dve.wait_ge(zeroed, 3)
                for h in range(2):
                    r = slice(64 * h, 64 * h + 64)
                    c.step(dve.tensor_tensor(S.kz[r, h, :], kT[r, 0, :], s2[r, 0, :], ALU.add))
                for h in range(4):
                    r = slice(32 * h, 32 * h + 32)
                    last = dve.tensor_tensor(S.kiz[r, h, :], kT[r, 1, :], s2[r, 1, :], ALU.add)
                last.then_inc(rotated, 1)

            dve.wait_ge(rope_in, 32)
            for j in range(4):
                dve.wait_ge(K.chunk_used, n0 + j + 1)
                if j < 2:
                    dst = S.uT[:, 2:4, :] if j == 0 else S.qT[:, 2:4, :]
                    dve.tensor_copy(dst, tiles(source(j, 1))).then_inc(dve_done, 1)
                elif j == 2:
                    c.step(dve.tensor_copy(S.qiT[:, 1, :], source(j, 1)[:, 0:T]))
                    dve.tensor_copy(kT[:, 1, :], source(j, 1)[:, T:]).then_inc(dve_done, 1)
                else:
                    dve.wait_ge(zeroed, 3)
                    v = source(j, 1)
                    c.step(dve.tensor_copy(S.vz[:, 0, 1, 0:64], v[:, 0:64]))
                    c.step(dve.tensor_copy(S.vz[:, 1, 1, 64:P], v[:, 64:P]))
                    dve.tensor_scalar(S.wi[:, 1, :], v[:, P:136], IDX_SCALE, None, ALU.mult).then_inc(dve_done, 1)
                    for n in range(4):
                        rotate(n)
            dve.wait_ge(rotated, 4)

        def s5_scalar_start(act):
            act.wait_ge(trig_ready, 1)
            act.activation(col[:, 0, :], par[:, 2, :], ACT.Exp).then_inc(trig_done, 1)
            act.wait_ge(trig_ready, 2)
            act.activation(col[:, 2, :], col[:, 1, :], ACT.Exp).then_inc(trig_done, 1)
            act.activation(col[:, 12:14, :], col[:, 6:8, :], ACT.Sin, scale=TWO_PI).then_inc(trig_done, 1)

        def s5_scalar(act):
            for j in range(NT):
                if j >= 4 and j % 4 == 0:
                    take_gate(act, j // 4 - 1)
                act.wait_ge(tab_ready, j + 1)
                act.activation(tab[:, j % 2, :, :], tab[:, j % 2, :, :], ACT.Sin, scale=TWO_PI).then_inc(tab_done, 1)
                act.wait_ge(turned, j + 1)
                if j >= 2:
                    act.wait_ge(bu_made, j - 1)
                act.activation(bT[:, j % 2, :, :], K.bank[:, j % 2, 0:2 * P].rearrange("p (r s) -> p r s", r=2),
                               ACT.Copy).then_inc(b_copied, 1)
            take_gate(act, 3)

        def outputs(pe, j):
            pe.wait_ge(s_ready, j + 1)
            if j % 4 == 0 and j >= 8:
                pe.wait_ge(y_taken, j // 4 - 1)
            out = K.bank[:, 4 + j // 4 % 2, 0:T]
            pe.matmul(out, cz[:, 0, j, :], st[:, j % 2, 0, :], start=(j % 4 == 0), stop=False)
            pe.matmul(out, cz[:, 1, j, :], st[:, j % 2, 1, :], start=False, stop=(j % 4 == 3)).then_inc(y_made, 1)

        def s5_tensor(pe):
            pe.wait_ge(act_done, 4)
            pe.wait_ge(dve_done, 4)
            for j in range(NT):
                pe.wait_ge(b_ready, j + 1)
                if j >= 2:
                    pe.wait_ge(b_copied, j - 1)
                for r in range(2):
                    last = pe.transpose(K.bank[:, j % 2, r * P:(r + 1) * P], b_pad[:, r, :], K.ident)
                last.then_inc(turned, 1)
                pe.wait_ge(b_copied, j + 1)
                if j >= 2:
                    pe.wait_ge(w_used, j - 1)
                for r in range(2):
                    last = pe.matmul(K.bank[:, 2 + j % 2, r * T:(r + 1) * T], bT[:, j % 2, r, :], S.uT[:, j // 4, :],
                                     start=True, stop=True)
                last.then_inc(bu_made, 1)
                gate_product(pe, j)
                if j >= 1:
                    outputs(pe, j - 1)
            outputs(pe, NT - 1)

        def take(dve, c, n):
            dve.wait_ge(y_made, 4 * n + 4)
            dve.scalar_tensor_tensor(y[:, n, :], S.uT[:, n, :], d_skip[:, n:n + 1], K.bank[:, 4 + n % 2, 0:T],
                                     ALU.mult, ALU.add).then_inc(y_taken, 1)

        def s5_vector_start(dve, c):
            C = lambda i: col[:, i, :]
            tt = lambda out, a, b, op: c.do(dve.tensor_tensor(out, a, b, op))
            dve.wait_ge(small_in, 16 * 8)
            dve.sem_inc(trig_ready, 1)
            dve.wait_ge(trig_done, 1)
            tt(C(1), par[:, 0, :], C(0), ALU.mult)
            tt(C(3), par[:, 1, :], C(0), ALU.mult)
            c.do(dve.tensor_scalar(C(3), C(3), 1.0 / (2.0 * np.pi), None, ALU.mult))
            sine_tables(dve, c, C(3), C(4), C(6), C(7)).then_inc(trig_ready, 1)
            dve.wait_ge(trig_ready, 2)
            c.step(dve.memset(b_pad[:], 0.0))
            dve.wait_ge(trig_done, 3)
            tt(C(12), C(12), C(2), ALU.mult)
            tt(C(13), C(13), C(2), ALU.mult)
            c.do(dve.tensor_scalar(C(12), C(12), -1.0, None, ALU.add))
            tt(C(8), par[:, 0, :], par[:, 0, :], ALU.mult)
            tt(C(9), par[:, 1, :], par[:, 1, :], ALU.mult)
            tt(C(8), C(8), C(9), ALU.add)
            c.do(dve.reciprocal(C(8), C(8)))
            tt(C(9), C(12), par[:, 0, :], ALU.mult)
            tt(C(10), C(13), par[:, 1, :], ALU.mult)
            tt(C(9), C(9), C(10), ALU.add)
            tt(C(10), C(13), par[:, 0, :], ALU.mult)
            tt(C(11), C(12), par[:, 1, :], ALU.mult)
            tt(C(10), C(10), C(11), ALU.subtract)
            tt(C(9), C(9), C(8), ALU.mult)
            tt(C(10), C(10), C(8), ALU.mult)
            wide = lambda i: C(i).unsqueeze(2).to_broadcast([P, NT, 16])
            scratch = m[:, 0, 0, :].rearrange("p (j n) -> p j n", j=NT)
            for out, a, b, op in ((0, 9, 10, ALU.subtract), (1, 10, 9, ALU.add)):
                tt(b_bar[:, out, :, :], b_in[:, 0, :, :], wide(a), ALU.mult)
                tt(scratch, b_in[:, 1, :, :], wide(b), ALU.mult)
                tt(b_bar[:, out, :, :], b_bar[:, out, :, :], scratch, op)
            c.do(dve.tensor_scalar(cz[:, 1, :, :], cz[:, 1, :, :], -1.0, None, ALU.mult))

        def s5_vector(dve, c):
            def pad_b(j):
                if j >= 1:
                    dve.wait_ge(turned, j)
                    old = 32 * ((j - 1) % 4)
                    c.do(dve.memset(b_pad[:, :, old:old + 32], 0.0))
                at = 32 * (j % 4)
                for half in range(2):
                    r = slice(64 * half, 64 * half + 64)
                    last = dve.tensor_copy(b_pad[r, :, at + 16 * half:at + 16 * half + 16], b_bar[r, :, j, :])
                    if half == 0:
                        c.step(last)
                last.then_inc(b_ready, 1)
                dve.wait_ge(b_ready, j + 1)

            pad_b(0)
            for j in range(NT):
                if j + 1 < NT:
                    pad_b(j + 1)
                dve.wait_ge(bu_made, j + 1)
                dve.wait_ge(tab_done, j + 1)
                bu = K.bank[:, 2 + j % 2, :].rearrange("p (r t) -> p r t", r=2)
                two = lambda i: tab[:, j % 2, i, :].unsqueeze(1).to_broadcast([P, 2, T])
                c.step(dve.tensor_tensor(w[:, 0, :, :], bu, two(0), ALU.mult))
                dve.tensor_tensor(m[:, 0, :, :], bu, two(1), ALU.mult).then_inc(w_used, 1)
                c.settle()
                dve.wait_ge(w_used, j + 1)
                c.step(dve.tensor_tensor(w[:, 0, 0, :], w[:, 0, 0, :], m[:, 0, 1, :], ALU.add))
                c.do(dve.tensor_tensor(w[:, 0, 1, :], w[:, 0, 1, :], m[:, 0, 0, :], ALU.subtract))
                decay = col[:, 2, j:j + 1].to_broadcast([P, T])
                for r in range(2):
                    c.step(dve.tensor_tensor_scan(w[:, 1, r, :], decay, w[:, 0, r, :], 0.0, ALU.mult, ALU.add))
                c.settle()
                c.step(dve.tensor_tensor(m[:, 0, :, :], w[:, 1, :, :], two(0), ALU.mult))
                c.do(dve.tensor_tensor(m[:, 1, :, :], w[:, 1, :, :], two(1), ALU.mult))
                if j >= 2:
                    dve.wait_ge(y_made, j - 1)
                c.step(dve.tensor_tensor(st[:, j % 2, 0, :], m[:, 0, 0, :], m[:, 1, 1, :], ALU.subtract))
                c.settle()
                dve.tensor_tensor(st[:, j % 2, 1, :], m[:, 0, 1, :], m[:, 1, 0, :], ALU.add).then_inc(s_ready, 1)
                dve.wait_ge(s_ready, j + 1)
                if j % 4 == 3 and j >= 7:
                    take(dve, c, j // 4 - 1)
            take(dve, c, 3)

        @block.tensor
        def _(pe):
            project_tensor(pe)
            s5_tensor(pe)

        @block.scalar
        def _(act):
            s5_scalar_start(act)
            project_scalar(act)
            s5_scalar(act)

        @block.vector
        def _(dve):
            c = Chain(dve, chain)
            s5_vector_start(dve, c)
            project_vector(dve, c)
            s5_vector(dve, c)



SEL = 64
TAKEN = -3e38


def sparse_attention_stage(K, S):
    nc = K.nc
    s_ = lambda s: K.sem(f"dsa_{s}")
    idx_made, relu_done, score_ready, score_masked, pick_ready, pick_masked, chain = (
        s_(s) for s in ("idx_made", "relu", "score", "score_masked", "pick", "pick_masked", "dve"))
    l_made, l_used, max_ready, exp_done, p_ready, turned, pT_ready, o_made, o_copied = (
        s_(s) for s in ("l_made", "l_used", "max", "exp", "p", "turned", "pT", "o_made", "o_copied"))
    with ExitStack() as stage, nc.Block() as block:
        sb = lambda n, s, dt=F32: stage.enter_context(nc.sbuf_tensor(f"dsa_{n}", s, dt))
        rel = sb("rel", [P, 2, 2, T])
        score = sb("score", [P, TT, T])
        work = sb("work", [P, T])
        top = sb("top", [P, 8])
        bias = sb("bias", [P, TT, T])
        lg = sb("lg", [P, 2, 2, T])
        mx, total = sb("mx", [P, 2, 2]), sb("total", [P, 2, 2])
        pT = sb("pT", [P, 2, 4, P])
        units = [(tt, j) for tt in range(TT) for j in range(4)]

        @block.tensor
        def _(pe):
            n = 0
            for tt in range(TT):
                for pair in range(4):
                    if n >= 2:
                        pe.wait_ge(relu_done, n - 1)
                    for r in range(2):
                        h = 2 * pair + r
                        last = pe.matmul(K.bank[:, 6 + n % 2, r * T:r * T + (tt + 1) * P],
                                         S.qiT[:, h // 4, tt * P:(tt + 1) * P], S.kiz[:, h % 4, 0:(tt + 1) * P],
                                         start=True, stop=True)
                    last.then_inc(idx_made, 1)
                    n += 1

            def logits(n):
                tt, j = units[n]
                if n >= 2:
                    pe.wait_ge(l_used, n - 1)
                for h in range(2):
                    last = pe.matmul(K.bank[:, n % 2, h * T:h * T + (tt + 1) * P], S.qT[:, j, tt * P:(tt + 1) * P],
                                     S.kz[:, h, 0:(tt + 1) * P], start=True, stop=True)
                last.then_inc(l_made, 1)

            def turn(n):
                tt, j = units[n]
                pe.wait_ge(p_ready, n + 1)
                if n >= 2:
                    pe.wait_ge(pT_ready, n - 1)
                for h in range(2):
                    for kt in range(tt + 1):
                        m = h * (tt + 1) + kt
                        last = pe.transpose(K.bank[:, 2 + n % 2, m * P:(m + 1) * P], lg[:, n % 2, h, kt * P:(kt + 1) * P],
                                            K.ident)
                last.then_inc(turned, 1)

            def values(n):
                tt, j = units[n]
                pe.wait_ge(pT_ready, n + 1)
                if n >= 2:
                    pe.wait_ge(o_copied, n - 1)
                parts = [(h, kt) for h in range(2) for kt in range(tt + 1)]
                for m, (h, kt) in enumerate(parts):
                    last = pe.matmul(K.bank[:, 4 + n % 2, 0:P], S.vz[:, h, kt, :], pT[:, n % 2, m, :],
                                     start=(m == 0), stop=(m == len(parts) - 1))
                last.then_inc(o_made, 1)

            for i in range(len(units) + 2):
                if i < len(units):
                    logits(i)
                if 1 <= i <= len(units):
                    turn(i - 1)
                if i >= 2:
                    values(i - 2)

        @block.scalar
        def _(act):
            n = 0
            for tt in range(TT):
                for pair in range(4):
                    act.wait_ge(idx_made, n + 1)
                    if n >= 2:
                        act.wait_ge(score_ready, n - 1)
                    w = (tt + 1) * P
                    act.activation(rel[:, n % 2, :, 0:w], K.bank[:, 6 + n % 2, :].rearrange("p (h s) -> p h s", h=2)[:, :, 0:w],
                                   ACT.Relu).then_inc(relu_done, 1)
                    n += 1
            for n, (tt, j) in enumerate(units):
                act.wait_ge(max_ready, n + 1)
                w = (tt + 1) * P
                for h in range(2):
                    last = act.activation(lg[:, n % 2, h, 0:w], lg[:, n % 2, h, 0:w], ACT.Exp, bias=mx[:, n % 2, h:h + 1],
                                          accum_out=total[:, n % 2, h:h + 1])
                    if h == 0:
                        last.then_inc(exp_done, 1)
                last.then_inc(exp_done, 1)
                act.wait_ge(turned, n + 1)
                if n >= 2:
                    act.wait_ge(o_made, n - 1)
                act.activation(pT[:, n % 2, 0:2 * (tt + 1), :],
                               K.bank[:, 2 + n % 2, 0:2 * w].rearrange("p (m t) -> p m t", t=P), ACT.Copy).then_inc(pT_ready, 1)

        @block.gpsimd
        def _(pool):
            for tt in range(TT):
                own = slice(tt * P, (tt + 1) * P)
                pool.wait_ge(score_ready, 4 * (tt + 1))
                pool.affine_select(out=score[:, tt, own], in_=score[:, tt, own], compare_op=ALU.is_ge, fill=NEG, base=0,
                                   pattern=[[-1, P]], channel_multiplier=1).then_inc(score_masked, 1)
                pool.wait_ge(pick_ready, tt + 1)
                pool.affine_select(out=bias[:, tt, own], in_=bias[:, tt, own], compare_op=ALU.is_ge, fill=NEG, base=0,
                                   pattern=[[-1, P]], channel_multiplier=1).then_inc(pick_masked, 1)

        @block.vector
        def _(dve):
            c = Chain(dve, chain)
            n = 0
            for tt in range(TT):
                w = (tt + 1) * P
                for pair in range(4):
                    dve.wait_ge(relu_done, n + 1)
                    for r in range(2):
                        h = 2 * pair + r
                        x, wi = rel[:, n % 2, r, 0:w], S.wi[:, tt, h:h + 1]
                        if h == 0:
                            c.do(dve.tensor_scalar(score[:, tt, 0:w], x, wi, None, ALU.mult))
                            continue
                        last = dve.scalar_tensor_tensor(score[:, tt, 0:w], x, wi, score[:, tt, 0:w], ALU.mult, ALU.add)
                        if r == 0:
                            c.do(last)
                    last.then_inc(score_ready, 1)
                    dve.wait_ge(score_ready, n + 1)
                    n += 1
            for tt in range(TT):
                w = (tt + 1) * P
                dve.wait_ge(score_masked, tt + 1)
                src = score[:, tt, 0:w]
                for r in range(SEL // 8):
                    c.do(dve.max(top[:], src))
                    c.do(dve.match_replace(work[:, 0:w], top[:], src, TAKEN))
                    src = work[:, 0:w]
                c.do(dve.tensor_scalar(work[:, 0:w], work[:, 0:w], 0.5 * TAKEN, -NEG, ALU.is_lt, ALU.mult))
                dve.tensor_scalar(bias[:, tt, 0:w], work[:, 0:w], NEG, None, ALU.add).then_inc(pick_ready, 1)
                dve.wait_ge(pick_ready, tt + 1)

            def scores(n):
                tt, j = units[n]
                w = (tt + 1) * P
                if j == 0:
                    dve.wait_ge(pick_masked, tt + 1)
                dve.wait_ge(l_made, n + 1)
                if n >= 2:
                    dve.wait_ge(turned, n - 1)
                x = lg[:, n % 2, :, 0:w]
                dve.scalar_tensor_tensor(x, K.bank[:, n % 2, :].rearrange("p (h s) -> p h s", h=2)[:, :, 0:w], 0.125,
                                         bias[:, tt, 0:w].unsqueeze(1).to_broadcast([P, 2, w]), ALU.mult,
                                         ALU.add).then_inc(l_used, 1)
                dve.wait_ge(l_used, n + 1)
                c.do(dve.tensor_reduce(mx[:, n % 2, :], x, AX.X, ALU.max))
                dve.tensor_scalar(mx[:, n % 2, :], mx[:, n % 2, :], -1.0, None, ALU.mult).then_inc(max_ready, 1)

            def divide(n):
                tt, j = units[n]
                w = (tt + 1) * P
                dve.wait_ge(exp_done, 2 * n + 2)
                c.do(dve.reciprocal(total[:, n % 2, :], total[:, n % 2, :]))
                x = lg[:, n % 2, :, 0:w]
                dve.tensor_tensor(x, x, total[:, n % 2, :].unsqueeze(2).to_broadcast([P, 2, w]), ALU.mult).then_inc(p_ready, 1)

            def take(n):
                tt, j = units[n]
                dve.wait_ge(o_made, n + 1)
                dve.tensor_copy(S.yaT[:, j, tt * P:(tt + 1) * P], K.bank[:, 4 + n % 2, 0:P]).then_inc(o_copied, 1)

            for i in range(len(units) + 2):
                if i < len(units):
                    scores(i)
                if 1 <= i <= len(units):
                    divide(i - 1)
                if i >= 2:
                    take(i - 2)



def join_stage(K, S):
    nc = K.nc
    s_ = lambda s: K.sem(f"join_{s}")
    gelu_done, sig_done, y_ready, chain, m_ready, turned, evac = (
        s_(s) for s in ("gelu", "sig", "y", "dve", "m", "turned", "evac"))
    with ExitStack() as stage, nc.Block() as block:
        sig = stage.enter_context(nc.sbuf_tensor("join_sig", [P, 4, T], F32))
        n_glu, n_ssm, n_attn, n_out = (START[n] for n in ("w_glu", "ssm_up", "attn_up", "w_out2"))

        @block.sync
        def _(sp):
            fetch_chunks(sp, K, next_start("w_out2") + RING)

        @block.scalar
        def _(act):
            act.activation(S.yT[:], S.yT[:], ACT.Gelu_apprx_tanh).then_inc(gelu_done, 1)
            act.wait_ge(K.chunk_used, n_glu + 1)
            act.activation(sig[:], K.bank[:, 0:2, :].rearrange("p b (c t) -> p (b c) t", c=2), ACT.Sigmoid).then_inc(sig_done, 1)
            evacuate_turned(act, K, turned, evac)

        @block.tensor
        def _(pe):
            pe.wait_ge(gelu_done, 1)
            wait_chunk(pe, K, n_glu)
            w = K.ring[:, n_glu % RING, 0:4 * 512].rearrange("p (k c) -> p k c", k=4)
            for i in range(4):
                for k in range(4):
                    last = pe.matmul(K.bank[:, i // 2, (i % 2) * T:(i % 2 + 1) * T], w[:, k, i * P:(i + 1) * P],
                                     S.yT[:, k, :], start=(k == 0), stop=(k == 3))
            last.then_inc(K.chunk_used, 1)
            pe.wait_ge(y_ready, 1)
            for n, xT, b in ((n_ssm, S.yT, 0), (n_attn, S.yaT, 4)):
                wait_chunk(pe, K, n)
                w = K.ring[:, n % RING, :].rearrange("p (k c) -> p k c", k=4)
                for tt in range(TT):
                    for dh in range(2):
                        for k in range(4):
                            last = pe.matmul(K.bank[:, b + 2 * tt + dh, :], xT[:, k, tt * P:(tt + 1) * P],
                                             w[:, k, dh * 512:(dh + 1) * 512], start=(k == 0), stop=(k == 3))
                last.then_inc(K.chunk_used, 1)
            turn_tokens(pe, K, S.gates[:, 0, :, :], m_ready, turned)
            pe.wait_ge(evac, 4)
            for dh in range(2):
                token_product(pe, K, n_out + dh, K.hT, [K.bank[:, 2 * tt + dh, :] for tt in range(TT)])

        @block.vector
        def _(dve):
            c = Chain(dve, chain)
            dve.wait_ge(sig_done, 1)
            dve.tensor_tensor(S.yT[:], S.yT[:], sig[:], ALU.mult).then_inc(y_ready, 1)
            gs, ga = S.gates[:, 0, :, :], S.gates[:, 1, :, :]
            product = lambda b: K.bank[:, b:b + 4, :].rearrange("p (t b) c -> p t (b c)", t=TT)
            dve.wait_ge(K.chunk_used, n_ssm + 1)
            c.step(dve.tensor_tensor(gs, gs, product(0), ALU.mult))
            dve.wait_ge(K.chunk_used, n_attn + 1)
            c.do(dve.tensor_tensor(ga, ga, product(4), ALU.mult))
            dve.tensor_tensor(gs, gs, ga, ALU.add).then_inc(m_ready, TT)


def add_banks(K):
    def add(dve, c, tt):
        x = K.x[:, tt, :]
        c.do(dve.tensor_tensor(x, x, K.bank[:, 2 * tt:2 * tt + 2, :].rearrange("p b c -> p (b c)"), ALU.add))
    return add


class Second:

    def __init__(self, nc, scope):
        sb = lambda n, s: scope.enter_context(nc.sbuf_tensor(n, s, F32))
        self.uT = sb("uT", [P, 4, T])
        self.qT = sb("qT", [P, 4, T])
        self.qiT = sb("qiT", [P, 2, T])
        self.kz = sb("kz", [P, 2, T])
        self.kiz = sb("kiz", [P, 4, T])
        self.vz = sb("vz", [P, 2, TT, P])
        self.wi = sb("wi", [P, TT, 8])
        self.gates = sb("gates", [P, 2, TT, D])
        self.yT = sb("ysT", [P, 4, T])
        self.yaT = sb("yaT", [P, 4, T])



PK_HEADS = 8
PK = 128
TOP = 16
U_SLOTS = 4
V_SLOTS = 3


def peer_query_stage(K, scores):
    nc = K.nc
    n_wq, n_keys = START["peer_wq"], START["peer_keys"]
    act_done, dve_done, s_made = (K.sem(f"peerq_{s}") for s in ("act_done", "dve_done", "s_made"))
    with ExitStack() as stage, nc.Block() as block:
        qT = stage.enter_context(nc.sbuf_tensor("peer_qT", [P, 2 * PK_HEADS, T], F32))

        @block.tensor
        def _(pe):
            for j in range(4):
                feature_product(pe, K, n_wq + j, K.hT, 2 * j)
            wait_chunk(pe, K, n_keys)
            keys = K.ring[:, n_keys % RING, 0:2048].rearrange("p (m n) -> p m n", n=PK)
            for n in range(8):
                tt, g = n // 4, n % 4
                for done in (act_done, dve_done):
                    done_to = max(g, n // 2) + 1
                    pe.wait_ge(done, done_to)
                for i in range(4):
                    m = 4 * g + i
                    last = pe.matmul(K.bank[:, n, i * PK:(i + 1) * PK], qT[:, m, tt * P:(tt + 1) * P], keys[:, m, :],
                                     start=True, stop=True)
                last.then_inc(s_made, 1)

        tiles = lambda b: K.bank[:, b, :].rearrange("p (c t) -> p c t", c=2)

        @block.scalar
        def _(act):
            for j in range(4):
                act.wait_ge(K.chunk_used, n_wq + j + 1)
                act.activation(qT[:, 4 * j:4 * j + 2, :], tiles(2 * j), ACT.Copy).then_inc(act_done, 1)
            for n in range(0, 8, 2):
                act.wait_ge(s_made, n + 1)
                act.activation(scores[:, n // 4, n % 4 * 512:(n % 4 + 1) * 512], K.bank[:, n, :], ACT.Copy)

        @block.vector
        def _(dve):
            for j in range(4):
                dve.wait_ge(K.chunk_used, n_wq + j + 1)
                dve.tensor_copy(qT[:, 4 * j + 2:4 * j + 4, :], tiles(2 * j + 1)).then_inc(dve_done, 1)
            for n in range(1, 8, 2):
                dve.wait_ge(s_made, n + 1)
                dve.tensor_copy(scores[:, n // 4, n % 4 * 512:(n % 4 + 1) * 512], K.bank[:, n, :])


def top_sixteen(dve, c, values, index, src):
    c.do(dve.max(values[:, 0:8], src))
    c.do(dve.max_index(index[:, 0:8], values[:, 0:8], src))
    c.do(dve.match_replace(src, values[:, 0:8], src, TAKEN))
    c.do(dve.max(values[:, 8:TOP], src))
    c.step(dve.max_index(index[:, 8:TOP], values[:, 8:TOP], src))


def peer_stage(K, scores, scores_scope):
    nc = K.nc
    s_ = lambda s: K.sem(f"peer_{s}")
    u_in = [s_(f"u_in{i}") for i in range(U_SLOTS)]
    v_in = [s_(f"v_in{i}") for i in range(V_SLOTS)]
    u_used, gelu_done, chain, sel_ready, exp_ready, exp_done = (
        s_(s) for s in ("u_used", "gelu", "dve", "sel", "exp_ready", "exp_done"))
    with ExitStack() as stage:
        H = stage.enter_context(nc.sbuf_tensor("H", [P, PK, T], F32))
        sel = stage.enter_context(nc.sbuf_tensor("sel", [P, 3, TT, P], F32))
        route = stage.enter_context(ExitStack())
        sb = lambda n, s, dt=F32: route.enter_context(nc.sbuf_tensor(f"peer_{n}", s, dt))
        u = sb("u", [P, U_SLOTS, KD, PK])
        val = sb("val", [P, 2, TOP])
        idx = sb("idx", [P, 2, TOP], U32)
        idx_f = sb("idx_f", [P, PK_HEADS, 2, TOP])
        cand = sb("cand", [P, 2 * P])
        best = sb("best", [P, PK_HEADS, TOP])
        pos = sb("pos", [P, PK_HEADS, TOP], U32)
        part = sb("part", [P, 2, PK_HEADS, TOP], U32)
        part_f = sb("part_f", [P, 2, PK_HEADS, TOP])
        hot = sb("hot", [P, TOP, TOP])
        col = sb("col", [P, 2, PK_HEADS])

        with nc.Block() as block:
            @block.sync
            def _(sp):
                for i in range(U_SLOTS):
                    sp.dma_start(u[:, i, :, :], K.A["peer_u"][i]).then_inc(u_in[i], 16)
                with sp.Fori(0, PK // U_SLOTS - 1) as g:
                    for i in range(U_SLOTS):
                        sp.wait_ge(u_used, g * U_SLOTS + (i + 1))
                        sp.dma_start(u[:, i, :, :], K.A["peer_u"][g * U_SLOTS + (U_SLOTS + i)]).then_inc(u_in[i], 16)

            def tile(pe, i, land):
                pe.wait_ge(u_in[i], land)
                for k in range(KD):
                    last = pe.matmul(K.bank[:, i // 2, (i % 2) * T:(i % 2 + 1) * T], u[:, i, k, :], K.hT[:, k, :],
                                     start=(k == 0), stop=(k == KD - 1))
                last.then_inc(u_used, 1)

            @block.tensor
            def _(pe):
                for i in range(U_SLOTS):
                    tile(pe, i, 16)
                with pe.Fori(1, PK // U_SLOTS) as g:
                    for i in range(U_SLOTS):
                        if i % 2 == 0:
                            pe.wait_ge(gelu_done, 2 * g + (i // 2 - 1))
                        tile(pe, i, 16 * g + 16)

            @block.scalar
            def _(act):
                def gelu(b, g):
                    act.wait_ge(u_used, g * U_SLOTS + 2 * (b + 1))
                    act.activation(H[:, bass.ds(g * U_SLOTS + 2 * b, 2), :],
                                   K.bank[:, b, :].rearrange("p (i t) -> p i t", i=2), ACT.Gelu_apprx_tanh).then_inc(gelu_done, 1)

                with act.Fori(0, PK // U_SLOTS) as g:
                    for b in range(2):
                        gelu(b, g)
                for tt in range(TT):
                    act.wait_ge(exp_ready, tt + 1)
                    act.activation(sel[:, 2, tt, :], sel[:, 2, tt, :], ACT.Exp).then_inc(exp_done, 1)

            @block.vector
            def _(dve):
                c = Chain(dve, chain)
                wide = lambda a: a.unsqueeze(2).to_broadcast([P, PK_HEADS, TOP])
                flat = lambda a: a.rearrange("p h k -> p (h k)")
                for tt in range(TT):
                    for h in range(PK_HEADS):
                        for half in range(2):
                            m = 2 * h + half
                            top_sixteen(dve, c, val[:, half, :], idx[:, half, :], scores[:, tt, m * PK:(m + 1) * PK])
                        c.settle()
                        c.step(dve.tensor_copy(idx_f[:, h, :, :], idx[:]))
                        c.do(dve.tensor_tensor(cand[:].rearrange("p (a b) -> p a b", a=TOP),
                                               val[:, 0, :].unsqueeze(2).to_broadcast([P, TOP, TOP]),
                                               val[:, 1, :].unsqueeze(1).to_broadcast([P, TOP, TOP]), ALU.add))
                        top_sixteen(dve, c, best[:, h, :], pos[:, h, :], cand[:])
                        c.settle()
                    c.step(dve.tensor_scalar(part[:, 0, :, :], pos[:], 4, None, ALU.logical_shift_right))
                    c.do(dve.tensor_scalar(part[:, 1, :, :], pos[:], TOP - 1, None, ALU.bitwise_and))
                    c.do(dve.tensor_copy(part_f[:], part[:]))
                    for half in range(2):
                        for h in range(PK_HEADS):
                            c.do(dve.tensor_tensor(hot[:], part_f[:, half, h, :].unsqueeze(2).to_broadcast([P, TOP, TOP]),
                                                   K.iota[:, 0:TOP].unsqueeze(1).to_broadcast([P, TOP, TOP]), ALU.is_equal))
                            c.do(dve.tensor_tensor(hot[:], hot[:], idx_f[:, h, half, :].unsqueeze(1).to_broadcast([P, TOP, TOP]),
                                                   ALU.mult))
                            c.do(dve.tensor_reduce(sel[:, half, tt, h * TOP:(h + 1) * TOP], hot[:], AX.X, ALU.add))
                    gate = sel[:, 2, tt, :].rearrange("p (h k) -> p h k", k=TOP)
                    dve.tensor_tensor(gate, best[:], wide(best[:, :, 0]), ALU.subtract).then_inc(exp_ready, 1)
                    dve.wait_ge(exp_ready, tt + 1)
                for tt in range(TT):
                    gate = sel[:, 2, tt, :].rearrange("p (h k) -> p h k", k=TOP)
                    dve.wait_ge(exp_done, tt + 1)
                    c.do(dve.tensor_reduce(col[:, tt, :], gate, AX.X, ALU.add))
                    c.do(dve.reciprocal(col[:, tt, :], col[:, tt, :]))
                    c.do(dve.tensor_tensor(gate, gate, wide(col[:, tt, :]), ALU.mult))
        route.close()
        scores_scope.close()

        v = stage.enter_context(nc.sbuf_tensor("peer_v", [P, V_SLOTS, D], F32))
        hots = stage.enter_context(ExitStack())
        sb = lambda n, s, dt=F32: hots.enter_context(nc.sbuf_tensor(f"peer_{n}", s, dt))
        selT = sb("selT", [P, 2, T])
        QT = 4
        a_hot = sb("a_hot", [P, 2, QT, P])
        b_hot = sb("b_hot", [P, 2, QT, P])
        away = sb("away", [P, 2, QT, P])
        neg_i1 = sb("neg_i1", [P, T])
        turned, selT_done, hot_ready, g_made, g_used = (s_(s) for s in ("turned", "selT", "hot", "g_made", "g_used"))
        neg_ready, away_made, b_ready = (s_(s) for s in ("neg", "away", "b_ready"))
        with nc.Block() as block:
            @block.sync
            def _(sp):
                for i in range(V_SLOTS):
                    sp.dma_start(v[:, i, :], K.A["peer_v"][i]).then_inc(v_in[i], 16)

            @block.tensor
            def _(pe):
                for r in range(3):
                    for tt in range(TT):
                        last = pe.transpose(K.bank[:, r, tt * P:(tt + 1) * P], sel[:, r, tt, :], K.ident)
                last.then_inc(turned, 1)
                with pe.Fori(0, T // (2 * QT)) as g:
                    for b in range(2):
                        pe.wait_ge(hot_ready, 2 * g + (b + 1))
                        pe.wait_ge(b_ready, 2 * g + (b + 1))
                        pe.wait_ge(g_used, 2 * g + (b + 1))
                        for q in range(QT):
                            last = pe.matmul(K.bank[:, 3 + b, q * P:(q + 1) * P], a_hot[:, b, q, :], b_hot[:, b, q, :],
                                             start=True, stop=True)
                        last.then_inc(g_made, 1)

            @block.scalar
            def _(act):
                act.wait_ge(turned, 1)
                act.activation(neg_i1[:], K.bank[:, 0, 0:T], ACT.Copy, scale=-1.0).then_inc(neg_ready, 1)
                act.wait_ge(neg_ready, 1)

                def one_hot(b, first, count, used=None):
                    for q in range(QT):
                        at = bass.ds(first + q, 1) if used is not None else slice(first + q, first + q + 1)
                        last = act.activation(away[:, b, q, :], K.iota, ACT.Square, bias=neg_i1[:, at])
                    last.then_inc(away_made, 1)
                    act.wait_ge(away_made, count)
                    if used is not None:
                        act.wait_ge(g_made, used)
                    act.activation(b_hot[:, b, :, :], away[:, b, :, :], ACT.Relu, scale=-4.0, bias=1.0).then_inc(b_ready, 1)

                one_hot(0, 0, 1)
                one_hot(1, QT, 2)
                with act.Fori(0, T // (2 * QT) - 1) as g:
                    for b in range(2):
                        one_hot(b, g * 2 * QT + (2 * QT + b * QT), 2 * g + (3 + b), 2 * g + (b + 1))

            @block.vector
            def _(dve):
                dve.sem_inc(g_used, 2)
                dve.wait_ge(turned, 1)
                dve.wait_ge(neg_ready, 1)
                dve.tensor_copy(selT[:], K.bank[:, 1:3, 0:T]).then_inc(selT_done, 1)
                dve.wait_ge(selT_done, 1)

                def one_hots(g, b, ahead):
                    for q in range(QT):
                        at = bass.ds(g * 2 * QT + (ahead + q), 1) if not isinstance(g, int) else slice(ahead + q, ahead + q + 1)
                        last = dve.tensor_scalar(a_hot[:, b, q, :], K.iota, selT[:, 0, at], selT[:, 1, at],
                                                 ALU.is_equal, ALU.mult)
                    last.then_inc(hot_ready, 1)

                def gate_h(g, b, count):
                    dve.wait_ge(g_made, count)
                    h = H[:, :, bass.ds(g * 2 * QT + b * QT, QT)]
                    dve.tensor_tensor(h, h, K.bank[:, 3 + b, :].rearrange("p (q i) -> p i q", q=QT),
                                      ALU.mult).then_inc(g_used, 1)

                one_hots(0, 0, 0)
                one_hots(0, 1, QT)
                with dve.Fori(0, T // (2 * QT) - 1) as g:
                    for b in range(2):
                        gate_h(g, b, 2 * g + (b + 1))
                        one_hots(g, b, 2 * QT + b * QT)
                g = T // (2 * QT) - 1
                for b in range(2):
                    dve.wait_ge(g_made, 2 * g + b + 1)
                    h = H[:, :, 2 * QT * g + b * QT:2 * QT * g + (b + 1) * QT]
                    dve.tensor_tensor(h, h, K.bank[:, 3 + b, :].rearrange("p (q i) -> p i q", q=QT), ALU.mult).then_inc(g_used, 1)
        hots.close()

        BUFS = 3
        hi_ready, lo_ready, used = (s_(s) for s in ("hi", "lo", "used"))
        split = lambda n, shape: stage.enter_context(nc.sbuf_tensor(f"peer_{n}", [P, BUFS] + shape, F32R))
        v_hi, v_lo, h_hi, h_lo = split("v_hi", [D]), split("v_lo", [D]), split("h_hi", [T]), split("h_lo", [T])
        with nc.Block() as block:
            LOOPS = (PK - 2) // V_SLOTS

            @block.sync
            def _(sp):
                with sp.Fori(0, (PK - V_SLOTS) // V_SLOTS) as g:
                    for i in range(V_SLOTS):
                        sp.wait_ge(lo_ready, g * V_SLOTS + (i + 1))
                        sp.dma_start(v[:, i, :], K.A["peer_v"][g * V_SLOTS + (V_SLOTS + i)]).then_inc(v_in[i], 16)
                for n in range((PK - V_SLOTS) // V_SLOTS * V_SLOTS + V_SLOTS, PK):
                    sp.wait_ge(lo_ready, n - V_SLOTS + 1)
                    sp.dma_start(v[:, n % V_SLOTS, :], K.A["peer_v"][n]).then_inc(v_in[n % V_SLOTS], 16)

            def tiles(eng, step):
                with eng.Fori(0, PK // V_SLOTS) as g:
                    for i in range(V_SLOTS):
                        step(g * V_SLOTS + i, i, 16 * g + 16)
                for n in range(PK // V_SLOTS * V_SLOTS, PK):
                    step(n, n % V_SLOTS, 16 * (n // V_SLOTS + 1))

            def h_tile(n):
                return H[:, n, :] if isinstance(n, int) else H[:, bass.ds(n, 1), :].rearrange("p o t -> p (o t)")

            @block.tensor
            def _(pe):
                pe.sem_inc(used, BUFS)

                def product(n, b, start, stop):
                    pe.wait_ge(lo_ready, n + 1)
                    for tt in range(TT):
                        mine = slice(tt * P, (tt + 1) * P)
                        for h, v_part, first, last_one in ((h_hi, v_hi, True, False), (h_hi, v_lo, False, False),
                                                           (h_lo, v_hi, False, True)):
                            for dh in range(2):
                                last = pe.matmul(K.bank[:, 2 * tt + dh, :], h[:, b, mine],
                                                 v_part[:, b, dh * 512:(dh + 1) * 512], start=start and first,
                                                 stop=stop and last_one)
                    last.then_inc(used, 1)

                product(0, 0, True, False)
                with pe.Fori(0, LOOPS) as g:
                    for i in range(V_SLOTS):
                        product(g * V_SLOTS + (1 + i), (1 + i) % BUFS, False, False)
                product(PK - 1, (PK - 1) % BUFS, False, True)

            @block.scalar
            def _(act):
                def high(n, i, land):
                    act.wait_ge(v_in[i], land)
                    act.wait_ge(used, n + 1)
                    act.activation(h_hi[:, i % BUFS, :], h_tile(n), ACT.Copy)
                    act.activation(v_hi[:, i % BUFS, :], v[:, i, :], ACT.Copy).then_inc(hi_ready, 1)

                tiles(act, high)

            @block.vector
            def _(dve):
                def low(n, i, land):
                    dve.wait_ge(v_in[i], land)
                    dve.wait_ge(hi_ready, n + 1)
                    b = i % BUFS
                    dve.tensor_tensor(h_lo[:, b, :], h_tile(n), h_hi[:, b, :].bitcast(F32), ALU.subtract)
                    dve.tensor_tensor(v_lo[:, b, :], v[:, i, :], v_hi[:, b, :].bitcast(F32), ALU.subtract).then_inc(lo_ready, 1)

                tiles(dve, low)



def program(nc, inputs, out):
    with ExitStack() as ctx:
        K = Core(nc, ctx, inputs)
        with ExitStack() as scope:
            load_stage(K, scope)
            ada_stage(K, "ada00")
            ada = stick_breaking_stage(K)
            moe_stage(K, 0, ada, "ada10").h_scope.close()
            K.recycle_sems()
            ada = retention_stage(K)
            moe_stage(K, 1, ada)
            rms_norm_turn_stage(K, "norm1", "norm1_g")
            with ExitStack() as second:
                S = Second(nc, second)
                projection_and_s5_stage(K, S)
                sparse_attention_stage(K, S)
                join_stage(K, S)
            K.recycle_sems()
            rms_norm_turn_stage(K, "norm2", "norm2_g", before=add_banks(K))
            scores_scope = ctx.enter_context(ExitStack())
            scores = scores_scope.enter_context(nc.sbuf_tensor("peer_scores", [P, TT, 2048], F32, side="right"))
            peer_query_stage(K, scores)
        peer_stage(K, scores, scores_scope)
        rms_norm_turn_stage(K, "norm_f", "norm_f_g", before=add_banks(K),
                            out=out[0].rearrange("(t p) d -> p t d", p=P))



def _chunks(w):
    rows, cols = w.shape
    kt = rows // P
    c = CHUNK // kt
    return w.reshape(kt, P, cols // c, c).transpose(2, 1, 0, 3).reshape(cols // c, P, CHUNK)


def _short(w):
    rows, cols = w.shape
    out = np.zeros((1, P, CHUNK), w.dtype)
    out[0, :, 0:rows // P * cols] = w.reshape(rows // P, P, cols).transpose(1, 0, 2).reshape(P, -1)
    return out


def _experts(gate, up, down):
    parts = []
    for e in range(EXPERTS):
        parts += [_chunks(gate[e]), _chunks(up[e])]
        if e:
            parts.append(_chunks(down[e - 1]))
    return parts + [_chunks(down[EXPERTS - 1])]


def _swap(dim):
    m = np.zeros((P, P), np.float32)
    for base in range(0, P, dim):
        for i in range(dim // 2):
            m[base + dim // 2 + i, base + i] = -1.0
            m[base + i, base + dim // 2 + i] = 1.0
    return m


def _rope_rows(dim):
    inv = (np.float32(10000.0) ** (-np.arange(0, dim, 2, dtype=np.float32) / np.float32(dim))).astype(np.float32)
    ang = np.arange(T, dtype=np.float32)[None, :] * inv[np.arange(P) % (dim // 2)][:, None]
    return np.stack([np.cos(ang), np.sin(ang)], 1).astype(np.float32)


def _retention_decay():
    h = np.arange(RET_HEADS, dtype=np.float32)
    lg = np.log(np.float32(1.0) - np.exp2(np.float32(-5.0) - h)).astype(np.float64)
    m, n = np.arange(P)[:, None, None], np.arange(P)[None, None, :]
    lg = lg[None, :, None]
    own = np.where(n >= m, np.exp(np.maximum(n - m, 0) * lg), 0.0)
    before = np.exp((n + 1.0 + P - 1.0 - m) * lg)
    return np.concatenate([own, before], 2).astype(np.float32)


def layout(a):
    eye = np.eye(P, dtype=np.float32)
    tri = -np.tril(np.ones((P, P), np.float32))
    w2 = a["w_in_2"][0]
    u, q, k, v, qi, ki, wi, gs, ga = np.split(w2, np.cumsum([512, 512, 128, 128, 256, 32, 8, 1024])[:8], axis=1)
    pair = np.concatenate([np.concatenate([np.arange(64 * j, 64 * j + 64), np.arange(64 * (j + 4), 64 * (j + 4) + 64)])
                           for j in range(4)])
    stream = []
    for i in range(DEPTH):
        stream += [_chunks(a["ada_w"][i, 0])]
        stream += [_chunks(a["sb_w_in"][0]), _chunks(a["sb_w_out"][0])] if i == 0 else [
            _chunks(a["ret_w_in"][0])] + [_chunks(a["ret_w_out"][0][r:r + D, c:c + COLS])
                                          for c in (0, COLS) for r in (0, D)]
        stream += [_chunks(a["ada_w"][i, 1])]
        stream += _experts(a["moe_w_gate"][i], a["moe_w_up"][i], a["moe_w_down"][i])
    stream += [_chunks(u), _chunks(q[:, pair]), _chunks(np.concatenate([k, qi, ki, ki, ki, ki], 1)),
               _short(np.concatenate([v, wi], 1)), _chunks(gs), _chunks(ga), _short(a["w_glu_2"][0]),
               _chunks(a["w_ssm_up_2"][0]), _chunks(a["w_attn_up_2"][0][pair]), _chunks(a["w_out_2"][0]),
               _chunks(a["peer_wq_2"][0])]
    keys = np.stack([a["peer_k1_2"][0], a["peer_k2_2"][0]], 1)
    stream += [_short(keys.reshape(-1, P).T)]
    stream = np.concatenate(stream)
    assert stream.shape == (CHUNKS, P, CHUNK)
    states = lambda s: s[0].reshape(16, P).T
    cz = np.zeros((2, 16, P, P), np.float32)
    for n, c in enumerate((a["c_re_2"][0], a["c_im_2"][0])):
        for g in range(32):
            col = 16 * (g % 8)
            cz[n, g // 2, 64 * (g % 2):64 * (g % 2) + 64, col:col + 16] = c[g].T
    out = {
        "stream": stream,
        "x_tokens": a["x"][0].reshape(TT, P, D).transpose(1, 0, 2),
        "c_cols": a["c"].reshape(KD, P).T,
        "ada_b": a["ada_b"].reshape(4, 3 * D),
        "ln_g": a["ln_g"].reshape(4, D),
        "ln_b": a["ln_b"].reshape(4, D),
        "consts": np.stack([eye, tri, -np.ones((P, P), np.float32), _swap(128), _swap(64), _swap(32),
                            np.tile(np.arange(P, dtype=np.float32), (P, 1))], 1),
        "router_w": a["router_w"].reshape(KD, P, EXPERTS).transpose(1, 0, 2),
        "router_b": a["router_b"].reshape(1, EXPERTS),
        "positions": a["positions"].reshape(1, T),
        "inv_freq": (np.float32(1.0) / (np.float32(10000.0) ** (np.arange(0, 128, 2, dtype=np.float32) / np.float32(128)))
                     ).astype(np.float32)[np.arange(P) % 64].reshape(P, 1),
        "decay": _retention_decay(),
        "ret_gn_g": a["ret_gn_g"].reshape(1, 2 * D),
        "rope64": _rope_rows(64),
        "rope32": _rope_rows(32),
        "norm1_g": a["norm1_g_2"].reshape(1, D),
        "norm2_g": a["norm2_g_2"].reshape(1, D),
        "norm_f_g": a["norm_f_g_2"].reshape(1, D),
        "a_re": states(a["a_re_2"]),
        "a_im": states(a["a_im_2"]),
        "log_dt": np.repeat(a["log_dt_2"][0], 64).reshape(16, P).T,
        "b_re": a["b_re_2"][0].reshape(16, P, 16).transpose(1, 0, 2),
        "b_im": a["b_im_2"][0].reshape(16, P, 16).transpose(1, 0, 2),
        "c_re": cz[0].transpose(1, 0, 2),
        "c_im": cz[1].transpose(1, 0, 2),
        "d_skip": a["d_skip_2"].reshape(4, P).T,
        "peer_u": a["peer_u_2"][0].reshape(P, P, KD, P).transpose(0, 3, 2, 1).reshape(P, P, KD * P),
        "peer_v": a["peer_v_2"][0].reshape(P, P, D),
    }
    return {k: np.ascontiguousarray(v) for k, v in out.items()}


def kernel(**inputs):
    from concourse import bacc
    from concourse.bass_utils import run_bass_kernel_spmd

    nc = bacc.Bacc("TRN2", target_bir_lowering=False, num_devices=1)
    arrays = layout({k: np.asarray(v) for k, v in inputs.items()})
    aps = {k: nc.dram_tensor(f"in_{k}", v.shape, mybir.dt.from_np(v.dtype), kind="ExternalInput").ap()
           for k, v in arrays.items()}
    out = nc.dram_tensor("out", (1, T, D), F32, kind="ExternalOutput").ap()
    program(nc, aps, out)
    result = run_bass_kernel_spmd(nc, [{f"in_{k}": v for k, v in arrays.items()}], core_ids=[0])
    return result.results[0]["out"]
```

```python
from contextlib import ExitStack

import concourse.bass as bass
import numpy as np
from concourse import mybir
from concourse.alu_op_type import AluOpType as ALU

F32 = mybir.dt.float32
I32 = mybir.dt.int32
F32R = mybir.dt.float32r
U32 = mybir.dt.uint32
ACT = mybir.ActivationFunctionType
AX = mybir.AxisListType

P = 128
T = 256
TT = T // P
D = 1024
KD = D // P
CHUNK = 4096
COLS = CHUNK // KD
RING = 3
DEPTH = 2
ALPHA = float((2 * DEPTH) ** 0.25)
LN_EPS = 1e-5
RMS_EPS = 1e-6
SB_HEADS = 16
SB_DIM = D // SB_HEADS
RET_HEADS = 8
RET_V = 2 * D // RET_HEADS
EXPERTS = 16
GROUPS = 4
PER_GROUP = EXPERTS // GROUPS
IDX_SCALE = 1.0 / 16.0
NEG = -1e30
TWO_PI = float(np.float32(6.283185))
ROUND = 12582912.0

STREAM = [("ada00", 6), ("sb_in", 6), ("sb_out", 2),
          ("ada01", 6), ("moe0", 3 * EXPERTS),
          ("ada10", 6), ("ret_in", 12), ("ret_out", 4),
          ("ada11", 6), ("moe1", 3 * EXPERTS),
          ("in2", 8), ("w_glu", 1), ("ssm_up", 1), ("attn_up", 1), ("w_out2", 2), ("peer_wq", 4), ("peer_keys", 1)]
START = {}
_n = 0
for _name, _count in STREAM:
    START[_name] = _n
    _n += _count
CHUNKS = _n
ADA_ROW = {"ada00": 0, "ada01": 1, "ada10": 2, "ada11": 3}
SHORT = {START["in2"] + 3: KD * 136, START["w_glu"]: 4 * 512, START["peer_keys"]: 2048}


def next_start(name):
    order = [n for n, _ in STREAM]
    i = order.index(name)
    return START[order[i + 1]] if i + 1 < len(order) else CHUNKS


class Core:

    def __init__(self, nc, ctx, inputs):
        self.nc = nc
        self.ctx = ctx
        self.A = inputs
        self.fetched = 0
        self.bank = ctx.enter_context(nc.psum_tensor("bank", [P, 8, 512], F32))
        self.consts = self.sb("consts", [P, 7, P])
        self.ident = self.consts[:, 0, :]
        self.tri_neg = self.consts[:, 1, :]
        self.ones_neg = self.consts[:, 2, :]
        self.swap128 = self.consts[:, 3, :]
        self.swap64 = self.consts[:, 4, :]
        self.swap32 = self.consts[:, 5, :]
        self.iota = self.consts[:, 6, :]
        self.x = self.sb("x", [P, TT, D])
        self.landed = [nc.alloc_semaphore(f"landed{s}") for s in range(RING)]
        self.chunk_used = nc.alloc_semaphore("chunk_used")
        self.stored = nc.alloc_semaphore("stored")
        self.stage_sems = []
        self.loaded = nc.alloc_semaphore("consts_loaded")

    def sb(self, name, shape, dt=F32):
        return self.ctx.enter_context(self.nc.sbuf_tensor(name, shape, dt))

    def sem(self, name):
        self.stage_sems.append(self.nc.alloc_semaphore(name))
        return self.stage_sems[-1]

    def recycle_sems(self):
        self.nc.clear_and_free_semaphores(self.stage_sems)
        self.nc.all_engine_barrier()
        self.stage_sems = []


class Chain:

    def __init__(self, eng, sem):
        self.eng, self.sem, self.n = eng, sem, 0

    def step(self, ins):
        self.n += 1
        ins.then_inc(self.sem, 1)
        return ins

    def settle(self):
        self.eng.wait_ge(self.sem, self.n)

    def do(self, ins):
        self.step(ins)
        self.settle()



def fetch_chunks(sp, K, upto):
    upto = min(upto, CHUNKS)
    for n in range(K.fetched, upto):
        if n >= RING:
            sp.wait_ge(K.chunk_used, n - RING + 1)
        size = SHORT.get(n, CHUNK)
        sp.dma_start(K.ring[:, n % RING, 0:size], K.A["stream"][n, :, 0:size]).then_inc(K.landed[n % RING], 16)
    K.fetched = max(K.fetched, upto)


def wait_chunk(pe, K, n):
    pe.wait_ge(K.landed[n % RING], 16 * (n // RING + 1))


def feature_product(pe, K, n, xT, bank0, slot=None, land=None):
    if n is not None:
        slot, land = n % RING, 16 * (n // RING + 1)
    pe.wait_ge(K.landed[slot], land)
    w = K.ring[:, slot, :].rearrange("p (k c) -> p k c", k=KD)
    for c in range(4):
        out = K.bank[:, bank0 + c // 2, (c % 2) * T:(c % 2 + 1) * T]
        for k in range(KD):
            last = pe.matmul(out, w[:, k, c * P:(c + 1) * P], xT[:, k, :], start=(k == 0), stop=(k == KD - 1))
    last.then_inc(K.chunk_used, 1)


def token_product(pe, K, n, xT, banks, cols=COLS, kt=KD, start=True, stop=True):
    wait_chunk(pe, K, n)
    w = K.ring[:, n % RING, 0:kt * cols].rearrange("p (k c) -> p k c", k=kt)
    for tt in range(TT):
        for k in range(kt):
            last = pe.matmul(banks[tt], xT[:, k, tt * P:(tt + 1) * P], w[:, k, :],
                             start=(start and k == 0), stop=(stop and k == kt - 1))
    last.then_inc(K.chunk_used, 1)


class SplitProducts:

    Q = 4

    def __init__(self, K, scope, name, n0, x=None):
        split = lambda n, shape: scope.enter_context(K.nc.sbuf_tensor(f"{name}_{n}", [P] + shape, F32R))
        self.K, self.n0 = K, n0
        self.w_hi, self.w_lo = split("w_hi", [self.Q, KD * P]), split("w_lo", [self.Q, KD * P])
        self.x_hi, self.x_lo = x or (split("x_hi", [KD, T]), split("x_lo", [KD, T]))
        self.hi_made, self.lo_made, self.used, self.x_high, self.x_low = (
            K.sem(f"{name}_{s}") for s in ("w_high", "w_low", "w_used", "x_high", "x_low"))

    def quarter(self, n, q, by_columns):
        w = self.K.ring[:, n % RING, :]
        if by_columns:
            return w.rearrange("p (k c) -> p k c", k=KD)[:, :, q * P:(q + 1) * P]
        return w.rearrange("p (q k c) -> p q k c", q=self.Q, k=2)[:, q, :, :]

    def shaped(self, w, q, by_columns):
        return w[:, q, :].rearrange("p (k c) -> p k c", k=KD if by_columns else 2)

    def high_x(self, act):
        act.activation(self.x_hi[:], self.K.hT[:], ACT.Copy).then_inc(self.x_high, 1)

    def low_x(self, dve):
        dve.wait_ge(self.x_high, 1)
        dve.tensor_tensor(self.x_lo[:], self.K.hT[:], self.x_hi[:].bitcast(F32), ALU.subtract).then_inc(self.x_low, 1)

    def high(self, act, n, by_columns):
        act.wait_ge(self.K.landed[n % RING], 16 * (n // RING + 1))
        for q in range(self.Q):
            done = self.Q * (n - self.n0) + q
            if done >= self.Q:
                act.wait_ge(self.used, done - self.Q + 1)
            act.activation(self.shaped(self.w_hi, q, by_columns), self.quarter(n, q, by_columns),
                           ACT.Copy).then_inc(self.hi_made, 1)

    def low(self, pool, n, by_columns):
        for q in range(self.Q):
            pool.wait_ge(self.hi_made, self.Q * (n - self.n0) + q + 1)
            pool.tensor_tensor(self.shaped(self.w_lo, q, by_columns), self.quarter(n, q, by_columns),
                               self.shaped(self.w_hi, q, by_columns).bitcast(F32), ALU.subtract).then_inc(self.lo_made, 1)

    def feature_product(self, pe, n, bank0):
        pe.wait_ge(self.x_low, 1)
        for q in range(self.Q):
            pe.wait_ge(self.lo_made, self.Q * (n - self.n0) + q + 1)
            out = self.K.bank[:, bank0 + q // 2, (q % 2) * T:(q % 2 + 1) * T]
            high, low = (self.shaped(w, q, True) for w in (self.w_hi, self.w_lo))
            for k in range(KD):
                pe.matmul(out, high[:, k, :], self.x_hi[:, k, :], start=(k == 0), stop=False)
                pe.matmul(out, high[:, k, :], self.x_lo[:, k, :], start=False, stop=False)
                last = pe.matmul(out, low[:, k, :], self.x_hi[:, k, :], start=False, stop=(k == KD - 1))
            last.then_inc(self.used, 1)
        pe.wait_ge(self.used, self.Q * (n - self.n0 + 1))
        pe.sem_inc(self.K.chunk_used, 1)

    def token_product(self, pe, n, banks, part=0, start=True, stop=True):
        for q in range(self.Q):
            pe.wait_ge(self.lo_made, self.Q * (n - self.n0) + q + 1)
            high, low = (self.shaped(w, q, False) for w in (self.w_hi, self.w_lo))
            for tt in range(TT):
                for k2 in range(2):
                    k = 2 * q + k2
                    mine = slice(tt * P, (tt + 1) * P)
                    x_hi, x_lo = self.x_hi[:, part + k, mine], self.x_lo[:, part + k, mine]
                    pe.matmul(banks[tt], x_hi, high[:, k2, :], start=(start and k == 0), stop=False)
                    pe.matmul(banks[tt], x_hi, low[:, k2, :], start=False, stop=False)
                    last = pe.matmul(banks[tt], x_lo, high[:, k2, :], start=False, stop=(stop and k == KD - 1))
            last.then_inc(self.used, 1)
        pe.wait_ge(self.used, self.Q * (n - self.n0 + 1))
        pe.sem_inc(self.K.chunk_used, 1)



def load_stage(K, scope):
    nc = K.nc
    K.hT = scope.enter_context(nc.sbuf_tensor("hT", [P, KD, T], F32))
    K.mod = scope.enter_context(nc.sbuf_tensor("mod", [P, 3 * D], F32))
    K.ring = scope.enter_context(nc.sbuf_tensor("ring", [P, RING, CHUNK], F32))
    K.silu_c = scope.enter_context(nc.sbuf_tensor("silu_c", [P, KD], F32))
    K.c_wide = scope.enter_context(nc.sbuf_tensor("c_wide", [P, KD, P], F32))
    c_in, act_done, wide_done = K.sem("c_in"), K.sem("silu_c_done"), K.sem("c_wide_done")
    with nc.Block() as block:
        @block.sync
        def _(sp):
            sp.dma_start(K.silu_c[:], K.A["c_cols"]).then_inc(c_in, 16)
            fetch_chunks(sp, K, RING)

        @block.scalar
        def _(act):
            act.dma_start(K.consts[:], K.A["consts"]).then_inc(K.loaded, 16)
            act.dma_start(K.x[:], K.A["x_tokens"]).then_inc(K.loaded, 16)
            act.wait_ge(c_in, 16)
            act.activation(K.silu_c[:], K.silu_c[:], ACT.Silu).then_inc(act_done, 1)

        @block.vector
        def _(dve):
            dve.wait_ge(act_done, 1)
            dve.tensor_copy(K.c_wide[:], K.silu_c[:].unsqueeze(2).to_broadcast([P, KD, P])).then_inc(wide_done, 1)
            dve.wait_ge(wide_done, 1)



class AdaLN:

    def __init__(self, K, name):
        self.K, self.name, self.row = K, name, ADA_ROW[name]
        self.bias_in, self.h_ready, self.turned, self.evac = (
            K.sem(f"{name}_{s}") for s in ("bias_in", "h", "turned", "evac"))
        self.h_scope = ExitStack()
        self.h = self.h_scope.enter_context(K.nc.sbuf_tensor(f"{name}_hbuf", [P, TT, D], F32, side="right"))

    def bias(self, eng, cols):
        row = self.K.A["ada_b"][self.row:self.row + 1, cols]
        eng.dma_start(self.K.mod[:, cols], row.to_broadcast([P, cols.stop - cols.start])).then_inc(self.bias_in, 16)

    def tensor(self, pe, y_read=None):
        K, n0 = self.K, START[self.name]
        for j in range(6):
            wait_chunk(pe, K, n0 + j)
            if j == 4 and y_read is not None:
                pe.wait_ge(y_read, 1)
            w = K.ring[:, (n0 + j) % RING, :].rearrange("p (k c) -> p k c", k=KD)
            for k in range(KD):
                last = pe.matmul(K.bank[:, (4 + j) % 8, :], K.c_wide[:, k, :], w[:, k, :], start=(k == 0), stop=(k == KD - 1))
            last.then_inc(K.chunk_used, 1)
        pe.wait_ge(K.loaded, 32)
        turn_tokens(pe, K, self.h, self.h_ready, self.turned)

    def vector(self, dve, c, biases):
        K, n0 = self.K, START[self.name]
        dve.wait_ge(self.bias_in, 16 * biases)
        dve.wait_ge(K.loaded, 32)
        for j in range(6):
            dve.wait_ge(K.chunk_used, n0 + j + 1)
            part = K.mod[:, j * COLS:(j + 1) * COLS]
            c.step(dve.scalar_tensor_tensor(part, K.bank[:, (4 + j) % 8, :], 0.0 if j < 2 else 1.0, part, ALU.add, ALU.add))
        for tt in range(TT):
            c.settle()
            c.do(dve.tensor_tensor(self.h[:, tt, :], K.x[:, tt, :], K.mod[:, D:2 * D], ALU.mult))
            dve.tensor_tensor(self.h[:, tt, :], self.h[:, tt, :], K.mod[:, 0:D], ALU.add).then_inc(self.h_ready, 1)


def ada_stage(K, name):
    nc = K.nc
    ada = AdaLN(K, name)
    with nc.Block() as block:
        @block.sync
        def _(sp):
            fetch_chunks(sp, K, next_start(name) + RING)

        @block.scalar
        def _(act):
            ada.bias(act, slice(0, 3 * D))
            evacuate_turned(act, K, ada.turned, ada.evac)

        @block.tensor
        def _(pe):
            ada.tensor(pe)

        @block.vector
        def _(dve):
            ada.vector(dve, Chain(dve, K.sem(f"{name}_dve")), 1)
    ada.h_scope.close()


def turn_tokens(pe, K, h, h_ready, turned):
    for tt in range(TT):
        pe.wait_ge(h_ready, tt + 1)
        for k in range(KD):
            out = K.bank[:, (6 + k // 2) % 8, (k % 2) * T + tt * P:(k % 2) * T + (tt + 1) * P]
            last = pe.transpose(out, h[:, tt, k * P:(k + 1) * P], K.ident)
    last.then_inc(turned, 1)


def evacuate_turned(act, K, turned, evac):
    act.wait_ge(turned, 1)
    for b in range(4):
        act.activation(K.hT[:, 2 * b:2 * b + 2, :], K.bank[:, (6 + b) % 8, :].rearrange("p (k t) -> p k t", k=2),
                       ACT.Copy).then_inc(evac, 1)



def layer_norm_stage(K, name, row, project, following=None, products=None):
    nc = K.nc
    rows_in, chain, y_read, var_ready, rstd_ready = (
        K.sem(f"{name}_norm_{s}") for s in ("rows_in", "dve", "y_read", "var", "std"))
    ada = AdaLN(K, following) if isinstance(following, str) else following
    with ExitStack() as stage, nc.Block() as block:
        sb = lambda n, s: stage.enter_context(nc.sbuf_tensor(f"{name}_{n}", s, F32))
        g_row, b_row = sb("g", [P, D]), sb("b", [P, D])
        s = sb("s", [P, TT, D])
        stats, mv, std = sb("stats", [P, TT, 2, 6]), sb("mv", [P, TT, 2]), sb("std", [P, TT])
        eps = sb("eps", [P, 1])

        @block.sync
        def _(sp):
            sp.dma_start(g_row[:], K.A["ln_g"][row:row + 1, :].to_broadcast([P, D])).then_inc(rows_in, 16)
            sp.dma_start(b_row[:], K.A["ln_b"][row:row + 1, :].to_broadcast([P, D])).then_inc(rows_in, 16)
            if ada:
                fetch_chunks(sp, K, next_start(ada.name) + RING)

        if products:
            @block.gpsimd
            def _(pool):
                for n in range(START[name], next_start(name)):
                    products.low(pool, n, False)

        @block.tensor
        def _(pe):
            if project is not None:
                project(pe)
            if ada:
                ada.tensor(pe, y_read)

        @block.scalar
        def _(act):
            if ada:
                ada.bias(act, slice(0, 2 * D))
            if products:
                for n in range(START[name], next_start(name)):
                    products.high(act, n, False)
            act.wait_ge(var_ready, 1)
            act.activation(std[:], mv[:, :, 1], ACT.Sqrt, bias=eps[:]).then_inc(rstd_ready, 1)
            if ada:
                act.wait_ge(y_read, TT)
                ada.bias(act, slice(2 * D, 3 * D))
                evacuate_turned(act, K, ada.turned, ada.evac)

        @block.vector
        def _(dve):
            c = Chain(dve, chain)
            c.step(dve.memset(eps[:], LN_EPS))
            dve.wait_ge(K.chunk_used, next_start(name))
            for tt in range(TT):
                y = K.bank[:, 2 * tt:2 * tt + 2, :].rearrange("p b c -> p (b c)")
                dve.tensor_tensor(s[:, tt, :], y, K.mod[:, 2 * D:3 * D], ALU.mult).then_inc(y_read, 1)
            for tt in range(TT):
                dve.wait_ge(y_read, tt + 1)
                c.do(dve.scalar_tensor_tensor(s[:, tt, :], K.x[:, tt, :], ALPHA, s[:, tt, :], ALU.mult, ALU.add))
                for j in range(2):
                    c.step(dve.bn_stats(stats[:, tt, j, :], s[:, tt, j * 512:(j + 1) * 512]))
                c.settle()
                last = dve.bn_aggr(mv[:, tt, :], stats[:, tt, :, :])
                if tt == 0:
                    c.step(last)
            last.then_inc(var_ready, 1)
            dve.wait_ge(rstd_ready, 1)
            c.do(dve.reciprocal(std[:], std[:]))
            dve.wait_ge(rows_in, 32)
            for tt in range(TT):
                c.do(dve.tensor_scalar(s[:, tt, :], s[:, tt, :], mv[:, tt, 0:1], std[:, tt:tt + 1], ALU.subtract, ALU.mult))
                c.do(dve.tensor_tensor(s[:, tt, :], s[:, tt, :], g_row[:], ALU.mult))
                c.step(dve.tensor_tensor(K.x[:, tt, :], s[:, tt, :], b_row[:], ALU.add))
            c.settle()
            if ada:
                ada.vector(dve, c, 2)
    return ada



def stick_breaking_stage(K):
    nc = K.nc
    n0 = START["sb_in"]
    W = T + P
    act_done, dve_done, q_zeroed, zeroed = (K.sem(f"sb_{s}") for s in ("act_done", "dve_done", "q_zeroed", "v_zeroed"))
    with ExitStack() as stage:
        sb = lambda n, s: stage.enter_context(nc.sbuf_tensor(f"sb_{n}", s, F32))
        oT = sb("oT", [P, KD, T])
        heads = stage.enter_context(ExitStack())
        sb = lambda n, s: heads.enter_context(nc.sbuf_tensor(f"sb_{n}", s, F32))
        qz = sb("qz", [P, SB_HEADS, T])
        kT = sb("kT", [P, KD, T])
        vz = sb("vz", [P, TT, SB_HEADS, P])

        with ExitStack() as scope, nc.Block() as block:
            products = SplitProducts(K, scope, "sb_in", n0)

            @block.sync
            def _(sp):
                fetch_chunks(sp, K, START["sb_out"] + RING)

            @block.gpsimd
            def _(pool):
                for j in range(6):
                    products.low(pool, n0 + j, j < 4)

            @block.tensor
            def _(pe):
                for j in range(6):
                    b = 2 * j % 8
                    if j >= 4:
                        pe.wait_ge(act_done, j - 3)
                        pe.wait_ge(dve_done, j - 3)
                    if j < 4:
                        products.feature_product(pe, n0 + j, b)
                    else:
                        products.token_product(pe, n0 + j, [K.bank[:, b + tt, :] for tt in range(TT)])

            def empty(eng, i, done):
                def scaled(out, src, scale):
                    if i == 0:
                        return eng.activation(out, src, ACT.Copy, scale=scale)
                    return eng.tensor_scalar(out, src, scale, None, ALU.mult)

                eng.wait_ge(q_zeroed, 1)
                for j in range(6):
                    if i == 0 and j < 5:
                        products.high(eng, n0 + j + 1, j + 1 < 4)
                    if j == 4:
                        eng.wait_ge(zeroed, 1)
                    src = K.bank[:, 2 * j % 8 + i, :]
                    eng.wait_ge(K.chunk_used, n0 + j + 1)
                    if 2 <= j < 4:
                        c = 4 * (j - 2) + 2 * i
                        scaled(kT[:, c:c + 2, :], src.rearrange("p (c t) -> p c t", c=2), 1.0).then_inc(done, 1)
                        continue
                    for half in range(2):
                        lo = half * SB_DIM
                        if j < 2:
                            head = 8 * j + 4 * i + half
                            last = scaled(qz[lo:lo + SB_DIM, head:head + 3:2, :],
                                          src[lo:lo + SB_DIM, :].rearrange("p (c t) -> p c t", c=2), SB_DIM ** -0.5)
                        else:
                            head = 8 * (j - 4) + half
                            heads_v = src.rearrange("p (h two d) -> p h two d", two=2, d=SB_DIM)
                            last = scaled(vz[:, i, head:head + 7:2, lo:lo + SB_DIM], heads_v[:, :, half, :], 1.0)
                    last.then_inc(done, 1)

            @block.scalar
            def _(act):
                products.high_x(act)
                products.high(act, n0, True)
                empty(act, 0, act_done)

            @block.vector
            def _(dve):
                products.low_x(dve)
                dve.memset(qz[:], 0.0).then_inc(q_zeroed, 1)
                dve.memset(vz[:], 0.0).then_inc(zeroed, 1)
                empty(dve, 1, dve_done)

        z_made, z_abs, soft, sp_made, sp_masked, s_made, a_made, a_masked, o_made, o_done = (
            K.sem(f"sb_{s}") for s in ("z_made", "z_abs", "soft", "sp_made", "sp_masked", "s_made", "a_made",
                                       "a_masked", "o_made", "o_done"))
        act_chain = K.sem("sb_act")
        with nc.Block() as block:
            NB = 3
            zabs, soft_b, sp_b, a_b = (sb(n, [P, NB, W]) for n in ("zabs", "softb", "spb", "ab"))
            zbank = lambda h: K.bank[:, h % 2, 0:W]
            sbank = lambda h: K.bank[:, 2 + h % 2, 0:W]

            def diagonal(buf):
                return buf.rearrange("p (b q) -> p b q", q=P)[:, 0:3:2, :]

            @block.tensor
            def _(pe):
                def scores(h, out, tile, stop):
                    if tile == 0:
                        return pe.matmul(out[:, 0:T], kT[:, h // 2, 0:P], qz[:, h, :], start=True, stop=stop)
                    return pe.matmul(out[:, T:W], kT[:, h // 2, P:T], qz[:, h, P:T], start=True, stop=stop)

                for i in range(SB_HEADS + 3):
                    if i < SB_HEADS:
                        if i >= 2:
                            pe.wait_ge(sp_made, i - 1)
                        scores(i, zbank(i), 0, True)
                        scores(i, zbank(i), 1, True).then_inc(z_made, 1)
                    h = i - 1
                    if 0 <= h < SB_HEADS:
                        if h >= 2:
                            pe.wait_ge(a_made, h - 1)
                        scores(h, sbank(h), 0, False)
                        pe.wait_ge(sp_masked, h + 1)
                        sp = sp_b[:, h % NB, :]
                        pe.matmul(sbank(h)[:, P:T], K.ones_neg, sp[:, T:W], start=False, stop=False)
                        pe.matmul(sbank(h)[:, 0:T], K.tri_neg, sp[:, 0:T], start=False, stop=True)
                        scores(h, sbank(h), 1, False)
                        pe.matmul(sbank(h)[:, T:W], K.tri_neg, sp[:, T:W], start=False, stop=True).then_inc(s_made, 1)
                    h = i - 3
                    if h >= 0:
                        pair, a = h // 2, a_b[:, h % NB, :]
                        out = K.bank[:, 4 + pair % 2, 0:T]
                        if h % 2 == 0 and pair >= 2:
                            pe.wait_ge(o_done, pair - 1)
                        pe.wait_ge(a_masked, h + 1)
                        parts = [(out, vz[:, 0, h, :], a[:, 0:T]), (out[:, P:T], vz[:, 1, h, :], a[:, T:W])]
                        for n, (o, v, prob) in enumerate(parts if h % 2 == 0 else parts[::-1]):
                            last = pe.matmul(o, v, prob, start=(h % 2 == 0 and n == 0), stop=(h % 2 == 1 and n == 1),
                                             skip_group_check=True)
                        last.then_inc(o_made, 1)

            @block.vector
            def _(dve):
                for i in range(SB_HEADS + 4):
                    h = i - 1
                    if 0 <= h < SB_HEADS:
                        dve.wait_ge(soft, 2 * h + 2)
                        if h >= NB:
                            dve.wait_ge(s_made, h - NB + 1)
                        dve.scalar_tensor_tensor(sp_b[:, h % NB, :], zbank(h), 0.0, soft_b[:, h % NB, :], ALU.max,
                                                 ALU.add).then_inc(sp_made, 1)
                    h = i - 4
                    if h >= 0 and h % 2 == 1:
                        dve.wait_ge(o_made, h + 1)
                        dve.tensor_copy(oT[:, h // 2, :], K.bank[:, 4 + h // 2 % 2, 0:T]).then_inc(o_done, 1)

            @block.scalar
            def _(act):
                act.preload_act_table_set("natural_log_exp_and_others")
                for i in range(SB_HEADS + 1):
                    if i < SB_HEADS:
                        act.wait_ge(z_made, i + 1)
                        act.activation(zabs[:, i % NB, :], zbank(i), ACT.Abs).then_inc(z_abs, 1)
                        act.wait_ge(z_abs, i + 1)
                        if i >= NB:
                            act.wait_ge(sp_made, i - NB + 1)
                        act.activation(zabs[:, i % NB, :], zabs[:, i % NB, :], ACT.Exp, scale=-1.0).then_inc(soft, 1)
                        act.wait_ge(soft, 2 * i + 1)
                        act.activation(soft_b[:, i % NB, :], zabs[:, i % NB, :], ACT.Ln, bias=1.0).then_inc(soft, 1)
                    h = i - 1
                    if h >= 0:
                        act.wait_ge(s_made, h + 1)
                        if h >= NB:
                            act.wait_ge(o_made, h - NB + 1)
                        act.activation(a_b[:, h % NB, :], sbank(h), ACT.Exp).then_inc(a_made, 1)

            @block.gpsimd
            def _(pool):
                mask = dict(compare_op=ALU.is_gt, fill=0.0, base=0, pattern=[[0, 2], [1, P]], channel_multiplier=-1)
                for i in range(SB_HEADS + 1):
                    if i < SB_HEADS:
                        pool.wait_ge(sp_made, i + 1)
                        d = diagonal(sp_b[:, i % NB, :])
                        pool.affine_select(out=d, in_=d, **mask).then_inc(sp_masked, 1)
                    if i >= 1:
                        pool.wait_ge(a_made, i)
                        d = diagonal(a_b[:, (i - 1) % NB, :])
                        pool.affine_select(out=d, in_=d, **mask).then_inc(a_masked, 1)

        heads.close()

        def project(pe):
            for dh in range(2):
                token_product(pe, K, START["sb_out"] + dh, oT, [K.bank[:, 2 * tt + dh, :] for tt in range(TT)])
        return layer_norm_stage(K, "sb_out", 0, project, "ada01")



def moe_stage(K, layer, ada, following=None):
    nc = K.nc
    h = ada.h
    name = f"moe{layer}"
    n0, n_end = START[name], next_start(name)
    s_ = lambda s: K.sem(f"{name}_{s}")
    small_in, logits_made, exp_ready, exp_made, group_ready, ranks_made, weights_ready, flag_ready = (
        s_(s) for s in ("small_in", "logits", "exp_ready", "exp_made", "group", "ranks", "weights", "flag"))
    silu_done, prod_done, hidden_done, chain, spread, copied = (
        s_(s) for s in ("silu", "prod", "hidden", "dve", "spread", "copied"))
    with ExitStack() as stage:
        sb = lambda n, s, dt=F32: stage.enter_context(nc.sbuf_tensor(f"{name}_{n}", s, dt))
        w_room = sb("w_room", [P, EXPERTS * T])
        room = sb("room", [P, EXPERTS * T])
        hot = sb("hot", [P, TT, GROUPS, P])
        hotT = sb("hotT", [P, GROUPS, T])
        eq = sb("eq", [P, TT, P])
        gated_s, hidden_s = sb("gated_s", [P, COLS]), sb("hidden_s", [P, COLS])
        slot_w = sb("slot_w", [P, EXPERTS])
        Q = 4
        split = lambda n, shape: stage.enter_context(nc.sbuf_tensor(f"{name}_{n}", [P] + shape, F32R))
        w_hi, w_lo = split("w_hi", [Q, CHUNK // Q]), split("w_lo", [Q, CHUNK // Q])
        slots_hi, slots_lo = split("slots_hi", [KD * P]), split("slots_lo", [KD * P])
        hid_hi, hid_lo = split("hid_hi", [4 * P]), split("hid_lo", [4 * P])
        router = sb("router", [P, KD, EXPERTS])
        router_b = sb("router_b", [P, EXPERTS])
        lg, pr, ex = (sb(n, [P, TT, EXPERTS]) for n in ("lg", "pr", "ex"))
        pairs = sb("pairs", [P, TT * GROUPS, 6])
        col = sb("col", [P, 9, TT])
        grp = sb("grp", [P, 4, TT, GROUPS])
        group = sb("group", [P, TT, GROUPS])
        rank_in = sb("rank_in", [P, TT, GROUPS])
        order = sb("order", [P, GROUPS])
        flag = sb("flag", [P, 1], I32)
        top = sb("top", [P, TT, 8])
        top_i = sb("top_i", [P, TT, 8], U32)
        top_f = sb("top_f", [P, TT, 8])
        pick = sb("pick", [P, 2, EXPERTS])
        comb = sb("comb", [P, TT, P])

        def route(dve, c):
            bc = lambda a, n: a.unsqueeze(2).to_broadcast([P, TT, n])
            c.step(dve.memset(comb[:], 0.0))
            c.step(dve.tensor_scalar(order[:], K.iota[:, 0:GROUPS], -1.0, float(GROUPS), ALU.mult, ALU.add))
            dve.wait_ge(logits_made, 1)
            c.do(dve.tensor_tensor(lg[:], K.bank[:, 0, 0:TT * EXPERTS].rearrange("p (t e) -> p t e", t=TT),
                                   router_b[:].unsqueeze(1).to_broadcast([P, TT, EXPERTS]), ALU.add))
            c.do(dve.tensor_reduce(col[:, 0, :], lg[:], AX.X, ALU.max))
            dve.tensor_tensor(pr[:], lg[:], bc(col[:, 0, :], EXPERTS), ALU.subtract).then_inc(exp_ready, 1)
            dve.wait_ge(exp_made, 1)
            c.do(dve.tensor_reduce(col[:, 1, :], ex[:], AX.X, ALU.add))
            c.do(dve.reciprocal(col[:, 1, :], col[:, 1, :]))
            c.do(dve.tensor_tensor(pr[:], ex[:], bc(col[:, 1, :], EXPERTS), ALU.mult))
            g4 = pr[:].rearrange("p t (g e) -> p (t g) e", e=PER_GROUP)
            c.step(dve.tensor_tensor(pairs[:, :, 0:3], g4[:, :, 0:3], g4[:, :, 1:4], ALU.add))
            c.step(dve.tensor_tensor(pairs[:, :, 3:5], g4[:, :, 0:2], g4[:, :, 2:4], ALU.add))
            c.do(dve.tensor_tensor(pairs[:, :, 5:6], g4[:, :, 0:1], g4[:, :, 3:4], ALU.add))
            c.do(dve.tensor_reduce(grp[:, 0, :, :].rearrange("p t g -> p (t g)"), pairs[:], AX.X, ALU.max))
            c.do(dve.tensor_reduce(col[:, 2, :], grp[:, 0, :, :], AX.X, ALU.max))
            c.do(dve.tensor_tensor(grp[:, 1, :, :], grp[:, 0, :, :], bc(col[:, 2, :], GROUPS), ALU.is_ge))
            c.do(dve.tensor_tensor(grp[:, 2, :, :], grp[:, 1, :, :], order[:].unsqueeze(1).to_broadcast([P, TT, GROUPS]),
                                   ALU.mult))
            c.do(dve.tensor_reduce(col[:, 3, :], grp[:, 2, :, :], AX.X, ALU.max))
            dve.tensor_tensor(group[:], grp[:, 2, :, :], bc(col[:, 3, :], GROUPS), ALU.is_equal).then_inc(group_ready, 1)
            dve.wait_ge(group_ready, 1)
            chosen = group[:].rearrange("p t g -> p (t g)").unsqueeze(2).to_broadcast([P, TT * GROUPS, PER_GROUP])
            lg4 = lg[:].rearrange("p t (g e) -> p (t g) e", e=PER_GROUP)
            pr4 = pr[:].rearrange("p t (g e) -> p (t g) e", e=PER_GROUP)
            c.step(dve.tensor_scalar(pr4, chosen, -NEG, NEG, ALU.mult, ALU.add))
            c.do(dve.tensor_tensor(lg4, lg4, chosen, ALU.mult))
            c.do(dve.tensor_tensor(lg[:], lg[:], pr[:], ALU.add))
            for tt in range(TT):
                c.step(dve.max(top[:, tt, :], lg[:, tt, :]))
            c.settle()
            for tt in range(TT):
                c.step(dve.max_index(top_i[:, tt, :], top[:, tt, :], lg[:, tt, :]))
            dve.tensor_tensor(col[:, 4, :], top[:, :, 1], top[:, :, 0], ALU.subtract).then_inc(exp_ready, 1)
            c.settle()
            c.do(dve.tensor_copy(top_f[:], top_i[:]))
            dve.wait_ge(ranks_made, 1)
            c.step(dve.tensor_reduce(col[:, 7, 0:1], K.bank[:, 3, 0:GROUPS], AX.X, ALU.min))
            c.do(dve.tensor_tensor(rank_in[:], K.bank[:, 1:1 + TT, 0:GROUPS], group[:], ALU.mult))
            dve.tensor_scalar(flag[:], col[:, 7, 0:1], -float(P), None, ALU.is_lt).then_inc(flag_ready, 1)
            c.do(dve.tensor_reduce(col[:, 8, :], rank_in[:], AX.X, ALU.add))
            c.do(dve.tensor_scalar(col[:, 8, :], col[:, 8, :], -1.0, -1.0, ALU.mult, ALU.add))
            for tt in range(TT):
                c.step(dve.tensor_scalar(eq[:, tt, :], K.iota, col[:, 8, tt:tt + 1], None, ALU.is_equal))
            dve.wait_ge(flag_ready, 1)
            dve.wait_ge(exp_made, 2)
            c.do(dve.tensor_scalar(col[:, 6, :], col[:, 5, :], 1.0, None, ALU.add))
            c.do(dve.reciprocal(col[:, 6, :], col[:, 6, :]))
            c.do(dve.tensor_tensor(col[:, 7, :], col[:, 5, :], col[:, 6, :], ALU.mult))

        def combine(dve, c):
            for tt in range(TT):
                for m in range(2):
                    c.step(dve.tensor_scalar(pick[:, m, :], K.iota[:, 0:EXPERTS], top_f[:, tt, m:m + 1],
                                             col[:, 6 + m, tt:tt + 1], ALU.is_equal, ALU.mult))
                c.settle()
                c.do(dve.tensor_tensor(comb[:, tt, 0:EXPERTS], pick[:, 0, :], pick[:, 1, :], ALU.add))
            dve.sem_inc(weights_ready, 1)

        made, spread_w, hot_ready, wide_ready, gathered, slots_h, slots_l = (
            s_(s) for s in ("made", "spread_w", "hot_ready", "wide", "gathered", "slots_h", "slots_l"))
        hi_done, lo_done, q_used, turned, hid_h, hid_l, taken = (
            s_(s) for s in ("hi", "lo", "q_used", "turned", "hid_h", "hid_l", "taken"))
        y_all = w_room[:].rearrange("p (g d) -> p g d", g=GROUPS)
        LAST_DOWN = n_end - 1 - n0

        def number(i, r):
            return r if i is None else PER_GROUP * i + (PER_GROUP + r)

        def chunk(i, r, m):
            if i is None:
                return max(3 * r - 1, 0) + m, 0
            return 3 * (PER_GROUP + r) - 1 + m, 3 * PER_GROUP * i

        def tensor_gathered(pe):
            pe.sem_inc(q_used, Q)
            pe.wait_ge(hot_ready, TT)

            def gather(i):
                for k in range(KD):
                    for tt in range(TT):
                        if i is None:
                            one = hot[:, tt, 0, :]
                        else:
                            one = hot[:, tt, bass.ds(i + 1, 1), :].rearrange("p o s -> p (o s)")
                        last = pe.matmul(K.bank[:, 2 + k // 4, k % 4 * P:(k % 4 + 1) * P], h[:, tt, k * P:(k + 1) * P],
                                         one, start=(tt == 0), stop=(tt == 1))
                last.then_inc(gathered, 1)

            gather(None)
            for g in range(GROUPS):
                for tt in range(TT):
                    last = pe.transpose(K.bank[:, 4 + g // 2, (g % 2) * T + tt * P:(g % 2) * T + (tt + 1) * P],
                                        hot[:, tt, g, :], K.ident)
            last.then_inc(made, 1)
            pe.wait_ge(weights_ready, 1)
            for g in range(GROUPS):
                mine = slice(g * PER_GROUP, (g + 1) * PER_GROUP)
                for tt in range(TT):
                    last = pe.matmul(K.bank[:, 6, mine], hot[:, tt, g, :], comb[:, tt, mine], start=(tt == 0), stop=(tt == 1))
            last.then_inc(spread_w, 1)

            def quarters(c, product):
                for q in range(Q):
                    pe.wait_ge(lo_done, Q * c[1] + (Q * c[0] + q + 1))
                    product(q, w_hi[:, q, :], w_lo[:, q, :]).then_inc(q_used, 1)

            def up_product(i, r, m):
                def product(q, high, low):
                    for k in (2 * q, 2 * q + 1):
                        x_high, x_low = slots_hi[:, k * P:(k + 1) * P], slots_lo[:, k * P:(k + 1) * P]
                        cols = slice(k % 2 * COLS, (k % 2 + 1) * COLS)
                        pe.matmul(K.bank[:, m, :], x_high, high[:, cols], start=(k == 0), stop=False)
                        pe.matmul(K.bank[:, m, :], x_high, low[:, cols], start=False, stop=False)
                        last = pe.matmul(K.bank[:, m, :], x_low, high[:, cols], start=False, stop=(k == KD - 1))
                    return last
                quarters(chunk(i, r, m), product)

            def turn_hidden(e):
                pe.wait_ge(hidden_done, e)
                for k in range(4):
                    last = pe.transpose(K.bank[:, 4, k * P:(k + 1) * P], hidden_s[:, k * P:(k + 1) * P], K.ident)
                last.then_inc(turned, 1)

            def down_product(c, e, r):
                def product(q, high, low):
                    x_high, x_low = hid_hi[:, q * P:(q + 1) * P], hid_lo[:, q * P:(q + 1) * P]
                    for x, w, first, final in ((x_high, high, True, False), (x_high, low, False, False), (x_low, high, False, True)):
                        for dh in range(2):
                            last = pe.matmul(K.bank[:, 6 + dh, :], x, w[:, dh * 512:(dh + 1) * 512],
                                             start=(first and r == 0 and q == 0),
                                             stop=(final and r == PER_GROUP - 1 and q == Q - 1))
                    return last
                pe.wait_ge(hid_l, e)
                quarters(c, product)

            def experts(i):
                for r in range(PER_GROUP):
                    e = number(i, r)
                    if r == 0 and i is not None:
                        gather(i)
                        down_product(chunk(i, -1, 2), PER_GROUP * i + (PER_GROUP - 1), 2)
                    if r == 0:
                        pe.wait_ge(slots_l, 1 if i is None else i + 2)
                    if i is not None or r:
                        pe.wait_ge(silu_done, e)
                    up_product(i, r, 0)
                    if i is not None or r:
                        turn_hidden(e)
                    up_product(i, r, 1)
                    if r < PER_GROUP - 1 and (i is not None or r):
                        if r == 1 and i is not None:
                            pe.wait_ge(taken, i + 1)
                        down_product(chunk(i, r, 2), e, (r - 1) % PER_GROUP)

            experts(None)
            with pe.Fori(0, GROUPS - 1) as i:
                experts(i)
            down_product((LAST_DOWN - 1, 0), EXPERTS - 1, PER_GROUP - 2)
            turn_hidden(EXPERTS)
            down_product((LAST_DOWN, 0), EXPERTS, PER_GROUP - 1)
            pe.wait_ge(taken, GROUPS)
            for tt in range(TT):
                for dh in range(2):
                    for g in range(GROUPS):
                        pe.matmul(K.bank[:, 2 * tt + dh, :], hotT[:, g, tt * P:(tt + 1) * P],
                                  y_all[:, g, dh * 512:(dh + 1) * 512], start=(g == 0), stop=(g == GROUPS - 1))

        def scalar_gathered(act):
            def high(c, after=None):
                at = n0 + c[0]
                for q in range(Q):
                    if q == 0:
                        act.wait_ge(K.landed[at % RING], 16 * (at // RING + 1) if isinstance(c[1], int) else
                                    16 * (3 * PER_GROUP // RING) * c[2] + 16 * (at // RING + 1))
                    act.wait_ge(q_used, Q * c[1] + (Q * c[0] + q + 1))
                    act.activation(w_hi[:, q, :], K.ring[:, at % RING, q * CHUNK // Q:(q + 1) * CHUNK // Q],
                                   ACT.Copy).then_inc(hi_done, 1)
                    if after and q in after:
                        after[q]()

            def of(i, r, m):
                return chunk(i, r, m) + (i,)

            def slots_high(i):
                act.wait_ge(gathered, 1 if i is None else i + 2)
                act.activation(slots_hi[:], K.bank[:, 2:4, :].rearrange("p b c -> p (b c)"), ACT.Copy).then_inc(slots_h, 1)

            def hidden_high(e):
                act.wait_ge(turned, e)
                act.activation(hid_hi[:], K.bank[:, 4, :], ACT.Copy).then_inc(hid_h, 1)

            def silu_gate(i, r, e):
                c = chunk(i, r, 0)
                act.wait_ge(q_used, Q * c[1] + (Q * c[0] + 2 * Q))
                if i is not None or r:
                    act.wait_ge(hidden_done, e)
                act.activation(gated_s[:], K.bank[:, 0, :], ACT.Silu).then_inc(silu_done, 1)

            def take(g, done):
                act.wait_ge(q_used, done)
                out = y_all[:, g, :] if isinstance(g, int) else y_all[:, bass.ds(g, 1), :].rearrange("p o d -> p (o d)")
                act.activation(out, K.bank[:, 6:8, :].rearrange("p b c -> p (b c)"), ACT.Copy).then_inc(taken, 1)

            slots_high(None)
            act.wait_ge(made, 1)
            act.activation(hotT[:].rearrange("p g t -> p (g t)"), K.bank[:, 4:6, :].rearrange("p b c -> p (b c)"), ACT.Copy).then_inc(copied, 1)

            def experts(i):
                for r in range(PER_GROUP):
                    e = number(i, r)
                    if r == 0 and i is not None:
                        high(of(i, -1, 2), {1: lambda: slots_high(i)})
                    if r == 1 and i is not None:
                        high(of(i, r, 0), {1: lambda: take(i, Q * 3 * PER_GROUP * i + Q * (3 * PER_GROUP + 3))})
                    else:
                        high(of(i, r, 0))
                    after = {2: lambda: silu_gate(i, r, e)}
                    if i is not None or r:
                        after[1] = lambda: hidden_high(e)
                    high(of(i, r, 1), after)
                    if r < PER_GROUP - 1 and (i is not None or r):
                        high(of(i, r, 2))

            experts(None)
            with act.Fori(0, GROUPS - 1) as i:
                experts(i)
            high((LAST_DOWN - 1, 0, None))
            high((LAST_DOWN, 0, None), {1: lambda: hidden_high(EXPERTS)})
            take(GROUPS - 1, Q * (LAST_DOWN + 2))

        def vector_gathered(dve, c_):
            for tt in range(TT):
                dve.tensor_tensor(hot[:, tt, :, :], eq[:, tt, :].unsqueeze(1).to_broadcast([P, GROUPS, P]),
                                  group[:, tt, :].unsqueeze(2).to_broadcast([P, GROUPS, P]), ALU.mult).then_inc(hot_ready, 1)
            combine(dve, c_)

            def low(c, after=None):
                at = n0 + c[0]
                for q in range(Q):
                    dve.wait_ge(hi_done, Q * c[1] + (Q * c[0] + q + 1))
                    dve.tensor_tensor(w_lo[:, q, :], K.ring[:, at % RING, q * CHUNK // Q:(q + 1) * CHUNK // Q],
                                      w_hi[:, q, :].bitcast(F32), ALU.subtract).then_inc(lo_done, 1)
                    if after and q in after:
                        after[q]()
                dve.wait_ge(lo_done, Q * c[1] + (Q * c[0] + Q))
                dve.sem_inc(K.chunk_used, 1)

            def slots_low(i):
                dve.wait_ge(slots_h, 1 if i is None else i + 2)
                dve.tensor_tensor(slots_lo[:], K.bank[:, 2:4, :].rearrange("p b c -> p (b c)"), slots_hi[:].bitcast(F32),
                                  ALU.subtract).then_inc(slots_l, 1)

            def hidden_low(e):
                dve.wait_ge(hid_h, e)
                dve.tensor_tensor(hid_lo[:], K.bank[:, 4, :], hid_hi[:].bitcast(F32), ALU.subtract).then_inc(hid_l, 1)

            def make_hidden(i, r, e, c=None):
                c = c or chunk(i, r, 1)
                dve.wait_ge(q_used, Q * c[1] + (Q * c[0] + 2 * Q))
                dve.wait_ge(silu_done, e + 1)
                if i is not None or r:
                    dve.wait_ge(turned, e)
                w = slot_w[:, e:e + 1] if isinstance(e, int) else slot_w[:, bass.ds(e, 1)]
                dve.scalar_tensor_tensor(hidden_s[:], K.bank[:, 1, :], w, gated_s[:], ALU.mult, ALU.mult).then_inc(hidden_done, 1)

            slots_low(None)
            dve.wait_ge(spread_w, 1)
            c_.do(dve.tensor_copy(slot_w[:], K.bank[:, 6, 0:EXPERTS]))

            def experts(i):
                for r in range(PER_GROUP):
                    e = number(i, r)
                    if r == 0 and i is not None:
                        low(chunk(i, -1, 2), {1: lambda: slots_low(i), 2: lambda: make_hidden(i, -1, PER_GROUP * i + (PER_GROUP - 1))})
                    if r == 1 and i is None:
                        low(chunk(i, r, 0), {1: lambda: make_hidden(None, 0, 0)})
                    else:
                        low(chunk(i, r, 0))
                    low(chunk(i, r, 1), {1: lambda: hidden_low(e)} if i is not None or r else None)
                    if r < PER_GROUP - 1 and (i is not None or r):
                        low(chunk(i, r, 2), {1: lambda: make_hidden(i, r, e)})

            experts(None)
            with dve.Fori(0, GROUPS - 1) as i:
                experts(i)
            low((LAST_DOWN - 1, 0), {1: lambda: make_hidden(None, PER_GROUP - 1, EXPERTS - 1, (LAST_DOWN - 2, 0))})
            low((LAST_DOWN, 0), {1: lambda: hidden_low(EXPERTS)})

        w_all = w_room[:].rearrange("p (e t) -> p e t", e=EXPERTS)
        diag = room[:].rearrange("p (e t) -> p e t", e=EXPERTS)
        hid = room[:, 2048:4096].rearrange("p (b k t) -> p b k t", b=2, k=4)
        gated, prod = room[:, 0:1024].rearrange("p (j c) -> p j c", j=2), room[:, 1024:2048].rearrange("p (c t) -> p c t", c=4)
        LOOPS = (EXPERTS - 2) // 2

        def tensor_dense(pe):
            def down(slot, land, e_parity, start, stop):
                pe.wait_ge(K.landed[slot], land)
                w = K.ring[:, slot, :].rearrange("p (k c) -> p k c", k=4)
                for tt in range(TT):
                    for k in range(4):
                        for dh in range(2):
                            last = pe.matmul(K.bank[:, 2 * tt + dh, :], hid[:, e_parity, k, tt * P:(tt + 1) * P],
                                             w[:, k, dh * 512:(dh + 1) * 512], start=(start and k == 0),
                                             stop=(stop and k == 3))
                last.then_inc(K.chunk_used, 1)

            pe.wait_ge(weights_ready, 1)
            for tt in range(TT):
                last = pe.transpose(K.bank[:, 1, tt * P:(tt + 1) * P], comb[:, tt, :], K.ident)
            last.then_inc(made, 1)
            pe.wait_ge(wide_ready, 1)
            for n in range(EXPERTS // 2):
                if n >= 4:
                    pe.wait_ge(copied, n - 3)
                pe.matmul(K.bank[:, n % 4, :], K.ones_neg, diag[:, 2 * n:2 * n + 2, :], start=True,
                          stop=True).then_inc(spread, 1)
            feature_product(pe, K, n0, K.hT, 4)
            feature_product(pe, K, n0 + 1, K.hT, 6)
            pe.wait_ge(silu_done, 2)
            feature_product(pe, K, n0 + 2, K.hT, 4)
            pe.wait_ge(prod_done, 2)
            feature_product(pe, K, n0 + 3, K.hT, 6)
            pe.wait_ge(hidden_done, 1)
            pe.wait_ge(copied, 8)
            down((n0 + 4) % RING, 16 * ((n0 + 4) // RING + 1), 0, True, False)
            with pe.Fori(0, LOOPS) as i:
                for r in range(2):
                    c = n0 + 5 + 3 * r
                    slot = [(c + m) % RING for m in range(3)]
                    land = [16 * (6 // RING) * i + 16 * ((c + m) // RING + 1) for m in range(3)]
                    pe.wait_ge(silu_done, 4 * i + (4 + 2 * r))
                    feature_product(pe, K, None, K.hT, 4, slot[0], land[0])
                    pe.wait_ge(prod_done, 4 * i + (4 + 2 * r))
                    feature_product(pe, K, None, K.hT, 6, slot[1], land[1])
                    pe.wait_ge(hidden_done, 2 * i + (2 + r))
                    down(slot[2], land[2], 1 - r, False, False)
            pe.wait_ge(hidden_done, EXPERTS)
            down((n_end - 1) % RING, 16 * ((n_end - 1) // RING + 1), 1, False, True)

        def scalar_dense(act):
            def silu_gate(e, gate_chunks):
                act.wait_ge(K.chunk_used, gate_chunks)
                for j in range(2):
                    if not (isinstance(e, int) and e == 0):
                        act.wait_ge(prod_done, 2 * e - 1 + j)
                    act.activation(gated[:, j, :], K.bank[:, 4 + j, :], ACT.Silu).then_inc(silu_done, 1)

            for n in range(EXPERTS // 2):
                act.wait_ge(spread, n + 1)
                act.activation(w_all[:, 2 * n:2 * n + 2, :], K.bank[:, n % 4, :].rearrange("p (e t) -> p e t", e=2),
                               ACT.Copy, scale=-1.0).then_inc(copied, 1)
            silu_gate(0, n0 + 1)
            silu_gate(1, n0 + 3)
            with act.Fori(0, LOOPS) as i:
                for r in range(2):
                    silu_gate(2 * i + (2 + r), 6 * i + (n0 + 6 + 3 * r))

        def vector_dense(dve, c):
            def make_hidden(e, parity, up_chunks):
                dve.wait_ge(K.chunk_used, up_chunks)
                if not (isinstance(e, int) and e == 0):
                    dve.wait_ge(hidden_done, e)
                for j in range(2):
                    dve.wait_ge(silu_done, 2 * e + j + 1)
                    dve.tensor_tensor(prod[:, 2 * j:2 * j + 2, :], gated[:, j, :].rearrange("p (c t) -> p c t", c=2),
                                      K.bank[:, 6 + j, :].rearrange("p (c t) -> p c t", c=2), ALU.mult).then_inc(prod_done, 1)
                if isinstance(e, int) and e == 0:
                    dve.wait_ge(copied, 8)
                dve.wait_ge(prod_done, 2 * e + 2)
                w = w_all[:, e, :] if isinstance(e, int) else w_all[:, bass.ds(e, 1), :].rearrange("p o t -> p (o t)")
                dve.tensor_tensor(hid[:, parity, :, :], prod[:], w.unsqueeze(1).to_broadcast([P, 4, T]),
                                  ALU.mult).then_inc(hidden_done, 1)

            combine(dve, c)
            dve.wait_ge(made, 1)
            dve.tensor_tensor(diag[:], K.bank[:, 1, 0:T].unsqueeze(1).to_broadcast([P, EXPERTS, T]),
                              K.ident[:, 0:EXPERTS].unsqueeze(2).to_broadcast([P, EXPERTS, T]),
                              ALU.mult).then_inc(wide_ready, 1)
            make_hidden(0, 0, n0 + 2)
            make_hidden(1, 1, n0 + 4)
            with dve.Fori(0, LOOPS) as i:
                for r in range(2):
                    make_hidden(2 * i + (2 + r), r, 6 * i + (n0 + 7 + 3 * r))

        with nc.Block() as block:
            @block.sync
            def _(sp):
                sp.dma_start(router[:], K.A["router_w"]).then_inc(small_in, 16)
                sp.dma_start(router_b[:], K.A["router_b"].to_broadcast([P, EXPERTS])).then_inc(small_in, 16)
                LOOPS = (n_end - n0 - RING) // RING
                assert K.fetched == n0 + RING and (n_end - n0) % RING == 0
                with sp.Fori(0, LOOPS) as i:
                    for j in range(RING):
                        slot = (n0 + j) % RING
                        sp.wait_ge(K.chunk_used, RING * i + (n0 + j + 1))
                        sp.dma_start(K.ring[:, slot, :], K.A["stream"][RING * i + (n0 + RING + j)]).then_inc(K.landed[slot], 16)
                K.fetched = n_end
                fetch_chunks(sp, K, n_end + RING)

            @block.tensor
            def _(pe):
                pe.wait_ge(small_in, 32)
                for tt in range(TT):
                    for k in range(KD):
                        last = pe.matmul(K.bank[:, 0, tt * EXPERTS:(tt + 1) * EXPERTS], K.hT[:, k, tt * P:(tt + 1) * P],
                                         router[:, k, :], start=(k == 0), stop=(k == KD - 1))
                last.then_inc(logits_made, 1)
                pe.wait_ge(group_ready, 1)
                pe.matmul(K.bank[:, 1, 0:GROUPS], K.tri_neg, group[:, 0, :], start=True, stop=False)
                pe.matmul(K.bank[:, 1, 0:GROUPS], K.ones_neg, group[:, 1, :], start=False, stop=True)
                pe.matmul(K.bank[:, 2, 0:GROUPS], K.tri_neg, group[:, 1, :], start=True, stop=True)
                pe.matmul(K.bank[:, 3, 0:GROUPS], K.ones_neg, group[:, 0, :], start=True, stop=False)
                pe.matmul(K.bank[:, 3, 0:GROUPS], K.ones_neg, group[:, 1, :], start=False, stop=True).then_inc(ranks_made, 1)
                pe.wait_ge(flag_ready, 1)
                crowded = pe.value_load(flag[0:1, 0:1])
                with pe.If(crowded):
                    tensor_dense(pe)
                with pe.Else():
                    tensor_gathered(pe)

            @block.scalar
            def _(act):
                act.wait_ge(exp_ready, 1)
                act.activation(ex[:], pr[:], ACT.Exp).then_inc(exp_made, 1)
                act.wait_ge(exp_ready, 2)
                act.activation(col[:, 5, :], col[:, 4, :], ACT.Exp).then_inc(exp_made, 1)
                act.wait_ge(flag_ready, 1)
                crowded = act.value_load(flag[0:1, 0:1])
                with act.If(crowded):
                    scalar_dense(act)
                with act.Else():
                    scalar_gathered(act)

            @block.vector
            def _(dve):
                c = Chain(dve, chain)
                route(dve, c)
                crowded = dve.value_load(flag[0:1, 0:1])
                steps = c.n
                with dve.If(crowded):
                    vector_dense(dve, c)
                with dve.Else():
                    c.n = steps
                    vector_gathered(dve, c)
    ada.h_scope.close()
    return layer_norm_stage(K, name, 2 * layer + 1, None, following)



def sine_tables(dve, c, turns, scratch, cos_in, sin_in):
    c.do(dve.tensor_scalar(scratch, turns, ROUND, -ROUND, ALU.add, ALU.add))
    c.step(dve.tensor_tensor(sin_in, turns, scratch, ALU.subtract))
    c.do(dve.tensor_scalar(cos_in, turns, 0.25, None, ALU.add))
    c.do(dve.tensor_scalar(scratch, cos_in, ROUND, -ROUND, ALU.add, ALU.add))
    return dve.tensor_tensor(cos_in, cos_in, scratch, ALU.subtract)


def retention_stage(K):
    nc = K.nc
    n0 = START["ret_in"]
    s_ = lambda s: K.sem(f"ret_{s}")
    small_in, pos_in, turns_ready, trig_ready, chain = (s_(s) for s in ("small_in", "pos_in", "turns", "trig", "dve"))
    act_done, dve_done, swapped, rotated = (s_(s) for s in ("act_done", "dve_done", "swapped", "rotated"))
    s_made, decayed, o_made, o_copied, gn_in = (s_(s) for s in ("s_made", "decayed", "o_made", "o_copied", "gn_in"))
    var_ready, std_ready, out_ready, turned, x_low = (
        s_(s) for s in ("var", "std", "out", "turned", "x_low"))
    with ExitStack() as stage:
        sb = lambda n, s, dt=F32: stage.enter_context(nc.sbuf_tensor(f"ret_{n}", s, dt))
        qkT = sb("qkT", [P, 2 * KD, T])
        heads = stage.enter_context(ExitStack())
        sb = lambda n, s, dt=F32: heads.enter_context(nc.sbuf_tensor(f"ret_{n}", s, dt))
        gate = sb("gate", [P, TT, 2 * D])
        v = sb("v", [P, TT, 2 * D])
        o = sb("o", [P, TT, 2 * D])
        decay = sb("decay", [P, RET_HEADS, 2 * P])
        scr = K.mod[:, 0:1024].rearrange("p (n c) -> p n c", n=2)
        trig = K.mod[:, 1024:1024 + 2 * T].rearrange("p (n t) -> p n t", n=2)
        freq = sb("freq", [P, 1])
        stats, mv, std = sb("stats", [P, RET_HEADS, TT, 6]), sb("mv", [P, RET_HEADS, TT, 2]), sb("std", [P, RET_HEADS, TT])
        eps = sb("eps", [P, 1])

        with ExitStack() as scope, nc.Block() as block:
            products = SplitProducts(K, scope, "ret_in", n0)
            pos = o[:, 0, 0:T].bitcast(I32)
            ang = o[:, 0, T:2 * T]

            @block.sync
            def _(sp):
                sp.dma_start(pos, K.A["positions"].to_broadcast([P, T])).then_inc(pos_in, 16)
                sp.dma_start(freq[:], K.A["inv_freq"]).then_inc(pos_in, 16)
                sp.dma_start(decay[:], K.A["decay"]).then_inc(small_in, 16)
                sp.dma_start(o[:, 1, :], K.A["ret_gn_g"].to_broadcast([P, 2 * D])).then_inc(gn_in, 16)
                fetch_chunks(sp, K, START["ret_out"] + RING)

            @block.tensor
            def _(pe):
                for j in range(12):
                    b = 2 * j % 6
                    if j >= 3:
                        pe.wait_ge(act_done, j - 2)
                        pe.wait_ge(dve_done, j - 2)
                    if j < 4:
                        products.feature_product(pe, n0 + j, b)
                    else:
                        products.token_product(pe, n0 + j, [K.bank[:, b + tt, :] for tt in range(TT)])
                    if 1 <= j <= 4:
                        for i in range(2):
                            n = 2 * (j - 1) + i
                            pe.wait_ge(act_done if i == 0 else dve_done, j)
                            if n >= 2:
                                pe.wait_ge(rotated, n - 1)
                            pe.matmul(K.bank[:, 6 + n % 2, :], K.swap128, qkT[:, 2 * n:2 * n + 2, :], start=True,
                                      stop=True).then_inc(swapped, 1)

            def source(j, i):
                return K.bank[:, 2 * j % 6 + i, :]

            @block.gpsimd
            def _(pool):
                for j in range(12):
                    products.low(pool, n0 + j, j < 4)

            @block.scalar
            def _(act):
                products.high_x(act)
                products.high(act, n0, True)
                act.wait_ge(turns_ready, 1)
                act.activation(trig, trig, ACT.Sin, scale=TWO_PI).then_inc(trig_ready, 1)
                for j in range(12):
                    if j < 11:
                        products.high(act, n0 + j + 1, j + 1 < 4)
                    act.wait_ge(K.chunk_used, n0 + j + 1)
                    if j < 4:
                        act.activation(qkT[:, 4 * j:4 * j + 2, :], source(j, 0).rearrange("p (c t) -> p c t", c=2),
                                       ACT.Copy, scale=1.0 if j < 2 else P ** -0.5).then_inc(act_done, 1)
                    elif j < 8:
                        act.activation(v[:, 0, (j - 4) * 512:(j - 3) * 512], source(j, 0), ACT.Copy).then_inc(act_done, 1)
                    else:
                        for i in range(TT):
                            last = act.activation(gate[:, i, (j - 8) * 512:(j - 7) * 512], source(j, i), ACT.Silu)
                        last.then_inc(act_done, 1)

            @block.vector
            def _(dve):
                c = Chain(dve, chain)
                products.low_x(dve)
                c.step(dve.memset(eps[:], LN_EPS))
                dve.wait_ge(pos_in, 32)
                c.do(dve.tensor_copy(ang, pos))
                c.do(dve.tensor_scalar(ang, ang, freq[:, 0:1], 1.0 / (2.0 * np.pi), ALU.mult, ALU.mult))
                sine_tables(dve, c, ang, scr[:, 0, 0:T], trig[:, 0, :], trig[:, 1, :]).then_inc(turns_ready, 1)

                def rotate(n):
                    x = qkT[:, 2 * n:2 * n + 2, :]
                    two = lambda r: trig[:, r, :].unsqueeze(1).to_broadcast([P, 2, T])
                    s2 = scr[:, n % 2, :].rearrange("p (c t) -> p c t", c=2)
                    dve.wait_ge(swapped, n + 1)
                    c.step(dve.tensor_tensor(s2, K.bank[:, 6 + n % 2, :].rearrange("p (c t) -> p c t", c=2), two(1), ALU.mult))
                    c.do(dve.tensor_tensor(x, x, two(0), ALU.mult))
                    dve.tensor_tensor(x, x, s2, ALU.add).then_inc(rotated, 1)

                for j in range(12):
                    if j == 1:
                        dve.wait_ge(trig_ready, 1)
                    dve.wait_ge(K.chunk_used, n0 + j + 1)
                    if j < 4:
                        dve.tensor_scalar(qkT[:, 4 * j + 2:4 * j + 4, :], source(j, 1).rearrange("p (c t) -> p c t", c=2),
                                          1.0 if j < 2 else P ** -0.5, None, ALU.mult).then_inc(dve_done, 1)
                    elif j < 8:
                        dve.tensor_copy(v[:, 1, (j - 4) * 512:(j - 3) * 512], source(j, 1)).then_inc(dve_done, 1)
                    else:
                        dve.wait_ge(act_done, j + 1)
                        dve.wait_ge(gn_in, 16)
                        cols = slice((j - 8) * 512, (j - 7) * 512)
                        dve.tensor_tensor(gate[:, :, cols], gate[:, :, cols],
                                          o[:, 1, cols].unsqueeze(1).to_broadcast([P, TT, 512]), ALU.mult).then_inc(dve_done, 1)
                    if 1 <= j <= 4:
                        rotate(2 * (j - 1))
                        rotate(2 * (j - 1) + 1)

        W = T + P
        with nc.Block() as block:
            sbank = lambda h: K.bank[:, h % 2, 0:W]
            obank = lambda h: K.bank[:, 2 + h % 2, :]
            s_b = scr[:, :, 0:W]

            @block.tensor
            def _(pe):
                for i in range(RET_HEADS + 1):
                    if i < RET_HEADS:
                        if i >= 2:
                            pe.wait_ge(decayed, i - 1)
                        qT, kT = qkT[:, i, :], qkT[:, KD + i, :]
                        pe.matmul(sbank(i)[:, 0:T], kT[:, 0:P], qT, start=True, stop=True)
                        pe.matmul(sbank(i)[:, T:W], kT[:, P:T], qT[:, P:T], start=True, stop=True).then_inc(s_made, 1)
                    h = i - 1
                    if h >= 0:
                        if h >= 2:
                            pe.wait_ge(o_copied, h - 1)
                        pe.wait_ge(decayed, h + 1)
                        s, vh = s_b[:, h % 2, :], v[:, :, h * RET_V:(h + 1) * RET_V]
                        pe.matmul(obank(h)[:, 0:RET_V], s[:, 0:P], vh[:, 0, :], start=True, stop=True)
                        pe.matmul(obank(h)[:, RET_V:], s[:, P:T], vh[:, 0, :], start=True, stop=False)
                        pe.matmul(obank(h)[:, RET_V:], s[:, T:W], vh[:, 1, :], start=False, stop=True).then_inc(o_made, 1)

            @block.scalar
            def _(act):
                for h in range(RET_HEADS):
                    act.wait_ge(o_made, h + 1)
                    act.activation(o[:, :, h * RET_V:(h + 1) * RET_V], obank(h).rearrange("p (t e) -> p t e", t=TT),
                                   ACT.Copy).then_inc(o_copied, 1)
                act.wait_ge(var_ready, 1)
                act.activation(std[:], mv[:, :, :, 1], ACT.Sqrt, bias=eps[:]).then_inc(std_ready, 1)

            @block.vector
            def _(dve):
                c = Chain(dve, K.sem("ret_dve2"))
                dve.wait_ge(small_in, 16)
                for i in range(RET_HEADS + 1):
                    if i < RET_HEADS:
                        dve.wait_ge(s_made, i + 1)
                        if i >= 2:
                            dve.wait_ge(o_made, i - 1)
                        s = s_b[:, i % 2, :]
                        dve.tensor_tensor(s[:, 0:T], sbank(i)[:, 0:T], decay[:, i, :], ALU.mult)
                        dve.tensor_tensor(s[:, T:W], sbank(i)[:, T:W], decay[:, i, 0:P], ALU.mult).then_inc(decayed, 1)
                    h = i - 1
                    if h >= 0:
                        dve.wait_ge(o_copied, h + 1)
                        for tt in range(TT):
                            c.step(dve.bn_stats(stats[:, h, tt, :], o[:, tt, h * RET_V:(h + 1) * RET_V]))
                c.settle()
                for h in range(RET_HEADS):
                    for tt in range(TT):
                        last = c.step(dve.bn_aggr(mv[:, h, tt, :], stats[:, h, tt, :]))
                c.settle()
                dve.sem_inc(var_ready, 1)
                dve.wait_ge(std_ready, 1)
                c.do(dve.reciprocal(std[:], std[:]))
                for h in range(RET_HEADS):
                    cols = slice(h * RET_V, (h + 1) * RET_V)
                    for tt in range(TT):
                        c.step(dve.tensor_scalar(o[:, tt, cols], o[:, tt, cols], mv[:, h, tt, 0:1], std[:, h, tt:tt + 1],
                                                 ALU.subtract, ALU.mult))
                    c.settle()
                    dve.tensor_tensor(o[:, :, cols], o[:, :, cols], gate[:, :, cols], ALU.mult).then_inc(out_ready, 1)

        ada = AdaLN(K, "ada11")
        x_hi, x_lo = (stage.enter_context(nc.sbuf_tensor(f"ret_x_{n}", [P, 2 * KD, T], F32R, side="right")) for n in ("hi", "lo"))
        x_high = K.sem("ret_x_high")
        with nc.Block() as block:
            @block.tensor
            def _(pe):
                for k in range(2 * KD):
                    for tt in range(TT):
                        out = K.bank[:, k // 2, (k % 2) * T + tt * P:(k % 2) * T + (tt + 1) * P]
                        last = pe.transpose(out, o[:, tt, k * P:(k + 1) * P], K.ident)
                    if k % 2:
                        last.then_inc(turned, 1)

            @block.scalar
            def _(act):
                for b in range(8):
                    act.wait_ge(turned, b + 1)
                    act.activation(x_hi[:, 2 * b:2 * b + 2, :], K.bank[:, b, :].rearrange("p (k t) -> p k t", k=2),
                                   ACT.Copy).then_inc(x_high, 1)

            @block.vector
            def _(dve):
                for b in range(8):
                    dve.wait_ge(x_high, b + 1)
                    dve.tensor_tensor(x_lo[:, 2 * b:2 * b + 2, :], K.bank[:, b, :].rearrange("p (k t) -> p k t", k=2),
                                      x_hi[:, 2 * b:2 * b + 2, :].bitcast(F32), ALU.subtract).then_inc(x_low, 1)
                dve.wait_ge(x_low, 8)
        heads.close()
        products = SplitProducts(K, stage, "ret_out", START["ret_out"], (x_hi, x_lo))

        def project(pe):
            for dh in range(2):
                for r in range(2):
                    products.token_product(pe, START["ret_out"] + 2 * dh + r, [K.bank[:, 2 * tt + dh, :] for tt in range(TT)],
                                           r * KD, start=(r == 0), stop=(r == 1))
        return layer_norm_stage(K, "ret_out", 2, project, ada, products)



def rms_norm_turn_stage(K, name, gain, before=None, keep=None, out=None):
    nc = K.nc
    row_in, chain, ss_ready, std_ready, h_ready, turned, evac = (
        K.sem(f"{name}_{s}") for s in ("row_in", "dve", "ss", "std", "h", "turned", "evac"))
    with ExitStack() as stage, nc.Block() as block:
        sb = lambda n, s: stage.enter_context(nc.sbuf_tensor(f"{name}_{n}", s, F32))
        g_row, h = sb("g", [P, D]), sb("hbuf", [P, TT, D])
        ss, eps = sb("ss", [P, TT]), sb("eps", [P, 1])

        @block.sync
        def _(sp):
            sp.dma_start(g_row[:], K.A[gain].to_broadcast([P, D])).then_inc(row_in, 16)
            if out is not None:
                sp.wait_ge(h_ready, TT)
                sp.dma_start(out, h[:]).then_inc(K.stored, 16)
                sp.wait_ge(K.stored, 16)

        @block.scalar
        def _(act):
            for tt in range(TT):
                act.wait_ge(ss_ready, tt + 1)
                act.activation(h[:, tt, :], K.x[:, tt, :], ACT.Square, accum_out=ss[:, tt:tt + 1]).then_inc(std_ready, 1)
            act.wait_ge(std_ready, TT)
            act.activation(ss[:], ss[:], ACT.Sqrt, bias=eps[:], scale=1.0 / D).then_inc(std_ready, 1)
            if out is None:
                evacuate_turned(act, K, turned, evac)

        if out is None:
            @block.tensor
            def _(pe):
                turn_tokens(pe, K, h, h_ready, turned)

        @block.vector
        def _(dve):
            c = Chain(dve, chain)
            c.do(dve.memset(eps[:], RMS_EPS))
            for tt in range(TT):
                if before is not None:
                    before(dve, c, tt)
                    c.settle()
                dve.sem_inc(ss_ready, 1)
            dve.wait_ge(std_ready, TT + 1)
            c.do(dve.reciprocal(ss[:], ss[:]))
            dve.wait_ge(row_in, 16)
            for tt in range(TT):
                dve.scalar_tensor_tensor(h[:, tt, :], K.x[:, tt, :], ss[:, tt:tt + 1], g_row[:], ALU.mult,
                                         ALU.mult).then_inc(h_ready, 1)


S5_TILES = 16


def projection_and_s5_stage(K, S):
    nc = K.nc
    n0 = START["in2"]
    act_done, dve_done, swapped, rotated, rope_in, zeroed, chain, gates_done, pool_chain = (
        K.sem(f"in2_{s}") for s in ("act_done", "dve_done", "swapped", "rotated", "rope_in", "zeroed", "dve", "gates", "pool"))
    s_ = lambda s: K.sem(f"s5_{s}")
    small_in, trig_ready, trig_done, b_ready, turned, b_copied = (
        s_(s) for s in ("small_in", "trig_ready", "trig_done", "b_ready", "turned", "b_copied"))
    bu_made, w_used, s_ready, y_made, y_taken, tab_ready, tab_done = (
        s_(s) for s in ("bu_made", "w_used", "s_ready", "y_made", "y_taken", "tab_ready", "tab_done"))
    NT = S5_TILES
    with ExitStack() as stage, nc.Block() as block:
        rope = K.c_wide[:].rearrange("p k c -> p (k c)").rearrange("p (a b t) -> p a b t", a=2, b=2)
        kT = S.yaT[:, 0:2, :]
        scr = K.mod[:, 2 * D:3 * D].rearrange("p (a b t) -> p a b t", a=2, b=2)
        sb = lambda n, s: stage.enter_context(nc.sbuf_tensor(f"s5_{n}", s, F32))
        par = sb("par", [P, 3, NT])
        col = sb("col", [P, 16, NT])
        b_in = sb("b_in", [P, 2, NT, 16])
        b_bar = sb("b_bar", [P, 2, NT, 16])
        b_pad = sb("b_pad", [P, 2, P])
        bT = sb("bT", [P, 2, 2, P])
        cz = sb("cz", [P, 2, NT, P])
        d_skip = sb("d_skip", [P, 4])
        tab = sb("tab", [P, 2, 2, T])
        turns = sb("turns", [P, 2, T])
        w, m, st = (K.mod[:, i * D:(i + 1) * D].rearrange("p (a b t) -> p a b t", a=2, b=2) for i in range(3))
        y = S.yT

        @block.sync
        def _(sp):
            sp.dma_start(rope[:, 0, :, :], K.A["rope64"]).then_inc(rope_in, 16)
            sp.dma_start(rope[:, 1, :, :], K.A["rope32"]).then_inc(rope_in, 16)
            for i, n in enumerate(("a_re", "a_im", "log_dt")):
                sp.dma_start(par[:, i, :], K.A[n]).then_inc(small_in, 16)
            sp.dma_start(b_in[:, 0, :, :], K.A["b_re"]).then_inc(small_in, 16)
            sp.dma_start(b_in[:, 1, :, :], K.A["b_im"]).then_inc(small_in, 16)
            sp.dma_start(d_skip[:], K.A["d_skip"]).then_inc(small_in, 16)
            sp.dma_start(cz[:, 0, :, :], K.A["c_re"]).then_inc(small_in, 16)
            sp.dma_start(cz[:, 1, :, :], K.A["c_im"]).then_inc(small_in, 16)
            fetch_chunks(sp, K, next_start("in2") + RING)

        @block.gpsimd
        def _(pool):
            pool.memset(S.kz[:], 0.0).then_inc(zeroed, 1)
            pool.memset(S.kiz[:], 0.0).then_inc(zeroed, 1)
            pool.memset(S.vz[:], 0.0).then_inc(zeroed, 1)
            c = Chain(pool, pool_chain)
            theta = col[:, 7, :]
            pool.wait_ge(trig_ready, 2)
            pool.wait_ge(K.loaded, 32)
            for j in range(NT):
                if j >= 2:
                    pool.wait_ge(s_ready, j - 1)
                c.step(pool.tensor_scalar(turns[:, 0, 0:P], K.iota, theta[:, j:j + 1], None, ALU.mult))
                c.do(pool.tensor_scalar(turns[:, 0, P:T], K.iota, float(P), theta[:, j:j + 1], ALU.add, ALU.mult))
                sine_tables(pool, c, turns[:, 0, :], turns[:, 1, :], tab[:, j % 2, 0, :], tab[:, j % 2, 1, :]).then_inc(tab_ready, 1)
                pool.wait_ge(tab_ready, j + 1)

        def pair(n):
            return [S.qT[:, 0:2, :], S.qT[:, 2:4, :], kT, S.qiT[:]][n]

        def project_tensor(pe):
            def swap(n, wait, count):
                pe.wait_ge(wait, count)
                if n >= 2:
                    pe.wait_ge(rotated, n - 1)
                out = K.bank[:, 6 + n % 2, :]
                if n == 2:
                    pe.matmul(out[:, 0:T], K.swap64, kT[:, 0, :], start=True, stop=True)
                    pe.matmul(out[:, T:], K.swap32, kT[:, 1, :], start=True, stop=True).then_inc(swapped, 1)
                else:
                    pe.matmul(out, K.swap32 if n == 3 else K.swap64, pair(n), start=True, stop=True).then_inc(swapped, 1)

            for j in range(4):
                b = 2 * j % 6
                if j == 3:
                    pe.wait_ge(act_done, 1)
                    pe.wait_ge(dve_done, 1)
                if j < 3:
                    feature_product(pe, K, n0 + j, K.hT, b)
                else:
                    cols = 136
                    token_product(pe, K, n0 + j, K.hT, [K.bank[:, b + tt, 0:cols] for tt in range(TT)], cols=cols)
                if j == 2:
                    swap(0, act_done, 2)
                    swap(1, dve_done, 2)
                if j == 3:
                    pe.wait_ge(act_done, 3)
                    swap(2, dve_done, 3)
                    swap(3, dve_done, 3)

        def source(j, i):
            return K.bank[:, 2 * j % 6 + i, :]

        tiles = lambda a: a.rearrange("p (c t) -> p c t", c=2)

        def project_scalar(act):
            for j in range(4):
                act.wait_ge(K.chunk_used, n0 + j + 1)
                if j < 2:
                    dst = S.uT[:, 0:2, :] if j == 0 else S.qT[:, 0:2, :]
                    act.activation(dst, tiles(source(j, 0)), ACT.Copy).then_inc(act_done, 1)
                elif j == 2:
                    act.activation(kT[:, 0, :], source(j, 0)[:, 0:T], ACT.Copy)
                    act.activation(S.qiT[:, 0, :], source(j, 0)[:, T:], ACT.Copy).then_inc(act_done, 1)
                else:
                    act.wait_ge(zeroed, 3)
                    v = source(j, 0)
                    act.activation(S.vz[:, 0, 0, 0:64], v[:, 0:64], ACT.Copy)
                    act.activation(S.vz[:, 1, 0, 64:P], v[:, 64:P], ACT.Copy)
                    act.activation(S.wi[:, 0, :], v[:, P:136], ACT.Copy, scale=IDX_SCALE).then_inc(act_done, 1)

        def gate_product(pe, j):
            n, q = n0 + 4 + j // 4, j % 4
            if q == 0:
                wait_chunk(pe, K, n)
                pe.wait_ge(rotated, 4)
                if j:
                    pe.wait_ge(gates_done, j // 4)
            w = K.ring[:, n % RING, :].rearrange("p (k c) -> p k c", k=KD)
            for k in range(4 * (q % 2), 4 * (q % 2) + 4):
                last = pe.matmul(K.bank[:, 6 + q // 2, :], K.hT[:, k, q // 2 * P:(q // 2 + 1) * P], w[:, k, :],
                                 start=(k == 0), stop=(k == KD - 1))
            if q == 3:
                last.then_inc(K.chunk_used, 1)

        def take_gate(act, n):
            act.wait_ge(K.chunk_used, n0 + 4 + n + 1)
            for i in range(TT):
                last = act.activation(S.gates[:, n // 2, i, n % 2 * COLS:(n % 2 + 1) * COLS], K.bank[:, 6 + i, :], ACT.Sigmoid)
            last.then_inc(gates_done, 1)

        def project_vector(dve, c):
            def rotate(n):
                x, s2 = pair(n), scr[:, n % 2, :, :]
                which = rope[:, 1 if n == 3 else 0, :, :]
                two = lambda r: which[:, r, :].unsqueeze(1).to_broadcast([P, 2, T])
                if n == 2:
                    two = lambda r: rope[:, :, r, :]
                dve.wait_ge(swapped, n + 1)
                c.step(dve.tensor_tensor(s2, tiles(K.bank[:, 6 + n % 2, :]), two(1), ALU.mult))
                c.do(dve.tensor_tensor(x, x, two(0), ALU.mult))
                if n != 2:
                    dve.tensor_tensor(x, x, s2, ALU.add).then_inc(rotated, 1)
                    return
                dve.wait_ge(zeroed, 3)
                for h in range(2):
                    r = slice(64 * h, 64 * h + 64)
                    c.step(dve.tensor_tensor(S.kz[r, h, :], kT[r, 0, :], s2[r, 0, :], ALU.add))
                for h in range(4):
                    r = slice(32 * h, 32 * h + 32)
                    last = dve.tensor_tensor(S.kiz[r, h, :], kT[r, 1, :], s2[r, 1, :], ALU.add)
                last.then_inc(rotated, 1)

            dve.wait_ge(rope_in, 32)
            for j in range(4):
                dve.wait_ge(K.chunk_used, n0 + j + 1)
                if j < 2:
                    dst = S.uT[:, 2:4, :] if j == 0 else S.qT[:, 2:4, :]
                    dve.tensor_copy(dst, tiles(source(j, 1))).then_inc(dve_done, 1)
                elif j == 2:
                    c.step(dve.tensor_copy(S.qiT[:, 1, :], source(j, 1)[:, 0:T]))
                    dve.tensor_copy(kT[:, 1, :], source(j, 1)[:, T:]).then_inc(dve_done, 1)
                else:
                    dve.wait_ge(zeroed, 3)
                    v = source(j, 1)
                    c.step(dve.tensor_copy(S.vz[:, 0, 1, 0:64], v[:, 0:64]))
                    c.step(dve.tensor_copy(S.vz[:, 1, 1, 64:P], v[:, 64:P]))
                    dve.tensor_scalar(S.wi[:, 1, :], v[:, P:136], IDX_SCALE, None, ALU.mult).then_inc(dve_done, 1)
                    for n in range(4):
                        rotate(n)
            dve.wait_ge(rotated, 4)

        def s5_scalar_start(act):
            act.wait_ge(trig_ready, 1)
            act.activation(col[:, 0, :], par[:, 2, :], ACT.Exp).then_inc(trig_done, 1)
            act.wait_ge(trig_ready, 2)
            act.activation(col[:, 2, :], col[:, 1, :], ACT.Exp).then_inc(trig_done, 1)
            act.activation(col[:, 12:14, :], col[:, 6:8, :], ACT.Sin, scale=TWO_PI).then_inc(trig_done, 1)

        def s5_scalar(act):
            for j in range(NT):
                if j >= 4 and j % 4 == 0:
                    take_gate(act, j // 4 - 1)
                act.wait_ge(tab_ready, j + 1)
                act.activation(tab[:, j % 2, :, :], tab[:, j % 2, :, :], ACT.Sin, scale=TWO_PI).then_inc(tab_done, 1)
                act.wait_ge(turned, j + 1)
                if j >= 2:
                    act.wait_ge(bu_made, j - 1)
                act.activation(bT[:, j % 2, :, :], K.bank[:, j % 2, 0:2 * P].rearrange("p (r s) -> p r s", r=2),
                               ACT.Copy).then_inc(b_copied, 1)
            take_gate(act, 3)

        def outputs(pe, j):
            pe.wait_ge(s_ready, j + 1)
            if j % 4 == 0 and j >= 8:
                pe.wait_ge(y_taken, j // 4 - 1)
            out = K.bank[:, 4 + j // 4 % 2, 0:T]
            pe.matmul(out, cz[:, 0, j, :], st[:, j % 2, 0, :], start=(j % 4 == 0), stop=False)
            pe.matmul(out, cz[:, 1, j, :], st[:, j % 2, 1, :], start=False, stop=(j % 4 == 3)).then_inc(y_made, 1)

        def s5_tensor(pe):
            pe.wait_ge(act_done, 4)
            pe.wait_ge(dve_done, 4)
            for j in range(NT):
                pe.wait_ge(b_ready, j + 1)
                if j >= 2:
                    pe.wait_ge(b_copied, j - 1)
                for r in range(2):
                    last = pe.transpose(K.bank[:, j % 2, r * P:(r + 1) * P], b_pad[:, r, :], K.ident)
                last.then_inc(turned, 1)
                pe.wait_ge(b_copied, j + 1)
                if j >= 2:
                    pe.wait_ge(w_used, j - 1)
                for r in range(2):
                    last = pe.matmul(K.bank[:, 2 + j % 2, r * T:(r + 1) * T], bT[:, j % 2, r, :], S.uT[:, j // 4, :],
                                     start=True, stop=True)
                last.then_inc(bu_made, 1)
                gate_product(pe, j)
                if j >= 1:
                    outputs(pe, j - 1)
            outputs(pe, NT - 1)

        def take(dve, c, n):
            dve.wait_ge(y_made, 4 * n + 4)
            dve.scalar_tensor_tensor(y[:, n, :], S.uT[:, n, :], d_skip[:, n:n + 1], K.bank[:, 4 + n % 2, 0:T],
                                     ALU.mult, ALU.add).then_inc(y_taken, 1)

        def s5_vector_start(dve, c):
            C = lambda i: col[:, i, :]
            tt = lambda out, a, b, op: c.do(dve.tensor_tensor(out, a, b, op))
            dve.wait_ge(small_in, 16 * 8)
            dve.sem_inc(trig_ready, 1)
            dve.wait_ge(trig_done, 1)
            tt(C(1), par[:, 0, :], C(0), ALU.mult)
            tt(C(3), par[:, 1, :], C(0), ALU.mult)
            c.do(dve.tensor_scalar(C(3), C(3), 1.0 / (2.0 * np.pi), None, ALU.mult))
            sine_tables(dve, c, C(3), C(4), C(6), C(7)).then_inc(trig_ready, 1)
            dve.wait_ge(trig_ready, 2)
            c.step(dve.memset(b_pad[:], 0.0))
            dve.wait_ge(trig_done, 3)
            tt(C(12), C(12), C(2), ALU.mult)
            tt(C(13), C(13), C(2), ALU.mult)
            c.do(dve.tensor_scalar(C(12), C(12), -1.0, None, ALU.add))
            tt(C(8), par[:, 0, :], par[:, 0, :], ALU.mult)
            tt(C(9), par[:, 1, :], par[:, 1, :], ALU.mult)
            tt(C(8), C(8), C(9), ALU.add)
            c.do(dve.reciprocal(C(8), C(8)))
            tt(C(9), C(12), par[:, 0, :], ALU.mult)
            tt(C(10), C(13), par[:, 1, :], ALU.mult)
            tt(C(9), C(9), C(10), ALU.add)
            tt(C(10), C(13), par[:, 0, :], ALU.mult)
            tt(C(11), C(12), par[:, 1, :], ALU.mult)
            tt(C(10), C(10), C(11), ALU.subtract)
            tt(C(9), C(9), C(8), ALU.mult)
            tt(C(10), C(10), C(8), ALU.mult)
            wide = lambda i: C(i).unsqueeze(2).to_broadcast([P, NT, 16])
            scratch = m[:, 0, 0, :].rearrange("p (j n) -> p j n", j=NT)
            for out, a, b, op in ((0, 9, 10, ALU.subtract), (1, 10, 9, ALU.add)):
                tt(b_bar[:, out, :, :], b_in[:, 0, :, :], wide(a), ALU.mult)
                tt(scratch, b_in[:, 1, :, :], wide(b), ALU.mult)
                tt(b_bar[:, out, :, :], b_bar[:, out, :, :], scratch, op)
            c.do(dve.tensor_scalar(cz[:, 1, :, :], cz[:, 1, :, :], -1.0, None, ALU.mult))

        def s5_vector(dve, c):
            def pad_b(j):
                if j >= 1:
                    dve.wait_ge(turned, j)
                    old = 32 * ((j - 1) % 4)
                    c.do(dve.memset(b_pad[:, :, old:old + 32], 0.0))
                at = 32 * (j % 4)
                for half in range(2):
                    r = slice(64 * half, 64 * half + 64)
                    last = dve.tensor_copy(b_pad[r, :, at + 16 * half:at + 16 * half + 16], b_bar[r, :, j, :])
                    if half == 0:
                        c.step(last)
                last.then_inc(b_ready, 1)
                dve.wait_ge(b_ready, j + 1)

            pad_b(0)
            for j in range(NT):
                if j + 1 < NT:
                    pad_b(j + 1)
                dve.wait_ge(bu_made, j + 1)
                dve.wait_ge(tab_done, j + 1)
                bu = K.bank[:, 2 + j % 2, :].rearrange("p (r t) -> p r t", r=2)
                two = lambda i: tab[:, j % 2, i, :].unsqueeze(1).to_broadcast([P, 2, T])
                c.step(dve.tensor_tensor(w[:, 0, :, :], bu, two(0), ALU.mult))
                dve.tensor_tensor(m[:, 0, :, :], bu, two(1), ALU.mult).then_inc(w_used, 1)
                c.settle()
                dve.wait_ge(w_used, j + 1)
                c.step(dve.tensor_tensor(w[:, 0, 0, :], w[:, 0, 0, :], m[:, 0, 1, :], ALU.add))
                c.do(dve.tensor_tensor(w[:, 0, 1, :], w[:, 0, 1, :], m[:, 0, 0, :], ALU.subtract))
                decay = col[:, 2, j:j + 1].to_broadcast([P, T])
                for r in range(2):
                    c.step(dve.tensor_tensor_scan(w[:, 1, r, :], decay, w[:, 0, r, :], 0.0, ALU.mult, ALU.add))
                c.settle()
                c.step(dve.tensor_tensor(m[:, 0, :, :], w[:, 1, :, :], two(0), ALU.mult))
                c.do(dve.tensor_tensor(m[:, 1, :, :], w[:, 1, :, :], two(1), ALU.mult))
                if j >= 2:
                    dve.wait_ge(y_made, j - 1)
                c.do(dve.tensor_tensor(st[:, j % 2, 0, :], m[:, 0, 0, :], m[:, 1, 1, :], ALU.subtract))
                dve.tensor_tensor(st[:, j % 2, 1, :], m[:, 0, 1, :], m[:, 1, 0, :], ALU.add).then_inc(s_ready, 1)
                dve.wait_ge(s_ready, j + 1)
                if j % 4 == 3 and j >= 7:
                    take(dve, c, j // 4 - 1)
            take(dve, c, 3)

        @block.tensor
        def _(pe):
            project_tensor(pe)
            s5_tensor(pe)

        @block.scalar
        def _(act):
            s5_scalar_start(act)
            project_scalar(act)
            s5_scalar(act)

        @block.vector
        def _(dve):
            c = Chain(dve, chain)
            s5_vector_start(dve, c)
            project_vector(dve, c)
            s5_vector(dve, c)



SEL = 64
TAKEN = -3e38


def sparse_attention_stage(K, S):
    nc = K.nc
    s_ = lambda s: K.sem(f"dsa_{s}")
    idx_made, relu_done, score_ready, score_masked, pick_ready, pick_masked, chain = (
        s_(s) for s in ("idx_made", "relu", "score", "score_masked", "pick", "pick_masked", "dve"))
    l_made, l_used, max_ready, exp_done, p_ready, turned, pT_ready, o_made, o_copied = (
        s_(s) for s in ("l_made", "l_used", "max", "exp", "p", "turned", "pT", "o_made", "o_copied"))
    with ExitStack() as stage, nc.Block() as block:
        sb = lambda n, s, dt=F32: stage.enter_context(nc.sbuf_tensor(f"dsa_{n}", s, dt))
        rel = sb("rel", [P, 2, 2, T])
        score = sb("score", [P, TT, T])
        work = sb("work", [P, T])
        top = sb("top", [P, 8])
        bias = sb("bias", [P, TT, T])
        lg = sb("lg", [P, 2, 2, T])
        mx, total = sb("mx", [P, 2, 2]), sb("total", [P, 2, 2])
        pT = sb("pT", [P, 2, 4, P])
        units = [(tt, j) for tt in range(TT) for j in range(4)]

        @block.tensor
        def _(pe):
            n = 0
            for tt in range(TT):
                for pair in range(4):
                    if n >= 2:
                        pe.wait_ge(relu_done, n - 1)
                    for r in range(2):
                        h = 2 * pair + r
                        last = pe.matmul(K.bank[:, 6 + n % 2, r * T:r * T + (tt + 1) * P],
                                         S.qiT[:, h // 4, tt * P:(tt + 1) * P], S.kiz[:, h % 4, 0:(tt + 1) * P],
                                         start=True, stop=True)
                    last.then_inc(idx_made, 1)
                    n += 1

            def logits(n):
                tt, j = units[n]
                if n >= 2:
                    pe.wait_ge(l_used, n - 1)
                for h in range(2):
                    last = pe.matmul(K.bank[:, n % 2, h * T:h * T + (tt + 1) * P], S.qT[:, j, tt * P:(tt + 1) * P],
                                     S.kz[:, h, 0:(tt + 1) * P], start=True, stop=True)
                last.then_inc(l_made, 1)

            def turn(n):
                tt, j = units[n]
                pe.wait_ge(p_ready, n + 1)
                if n >= 2:
                    pe.wait_ge(pT_ready, n - 1)
                for h in range(2):
                    for kt in range(tt + 1):
                        m = h * (tt + 1) + kt
                        last = pe.transpose(K.bank[:, 2 + n % 2, m * P:(m + 1) * P], lg[:, n % 2, h, kt * P:(kt + 1) * P],
                                            K.ident)
                last.then_inc(turned, 1)

            def values(n):
                tt, j = units[n]
                pe.wait_ge(pT_ready, n + 1)
                if n >= 2:
                    pe.wait_ge(o_copied, n - 1)
                parts = [(h, kt) for h in range(2) for kt in range(tt + 1)]
                for m, (h, kt) in enumerate(parts):
                    last = pe.matmul(K.bank[:, 4 + n % 2, 0:P], S.vz[:, h, kt, :], pT[:, n % 2, m, :],
                                     start=(m == 0), stop=(m == len(parts) - 1))
                last.then_inc(o_made, 1)

            for i in range(len(units) + 2):
                if i < len(units):
                    logits(i)
                if 1 <= i <= len(units):
                    turn(i - 1)
                if i >= 2:
                    values(i - 2)

        @block.scalar
        def _(act):
            n = 0
            for tt in range(TT):
                for pair in range(4):
                    act.wait_ge(idx_made, n + 1)
                    if n >= 2:
                        act.wait_ge(score_ready, n - 1)
                    w = (tt + 1) * P
                    act.activation(rel[:, n % 2, :, 0:w], K.bank[:, 6 + n % 2, :].rearrange("p (h s) -> p h s", h=2)[:, :, 0:w],
                                   ACT.Relu).then_inc(relu_done, 1)
                    n += 1
            for n, (tt, j) in enumerate(units):
                act.wait_ge(max_ready, n + 1)
                w = (tt + 1) * P
                for h in range(2):
                    last = act.activation(lg[:, n % 2, h, 0:w], lg[:, n % 2, h, 0:w], ACT.Exp, bias=mx[:, n % 2, h:h + 1],
                                          accum_out=total[:, n % 2, h:h + 1])
                    if h == 0:
                        last.then_inc(exp_done, 1)
                last.then_inc(exp_done, 1)
                act.wait_ge(turned, n + 1)
                if n >= 2:
                    act.wait_ge(o_made, n - 1)
                act.activation(pT[:, n % 2, 0:2 * (tt + 1), :],
                               K.bank[:, 2 + n % 2, 0:2 * w].rearrange("p (m t) -> p m t", t=P), ACT.Copy).then_inc(pT_ready, 1)

        @block.gpsimd
        def _(pool):
            for tt in range(TT):
                own = slice(tt * P, (tt + 1) * P)
                pool.wait_ge(score_ready, 4 * (tt + 1))
                pool.affine_select(out=score[:, tt, own], in_=score[:, tt, own], compare_op=ALU.is_ge, fill=NEG, base=0,
                                   pattern=[[-1, P]], channel_multiplier=1).then_inc(score_masked, 1)
                pool.wait_ge(pick_ready, tt + 1)
                pool.affine_select(out=bias[:, tt, own], in_=bias[:, tt, own], compare_op=ALU.is_ge, fill=NEG, base=0,
                                   pattern=[[-1, P]], channel_multiplier=1).then_inc(pick_masked, 1)

        @block.vector
        def _(dve):
            c = Chain(dve, chain)
            n = 0
            for tt in range(TT):
                w = (tt + 1) * P
                for pair in range(4):
                    dve.wait_ge(relu_done, n + 1)
                    for r in range(2):
                        h = 2 * pair + r
                        x, wi = rel[:, n % 2, r, 0:w], S.wi[:, tt, h:h + 1]
                        if h == 0:
                            c.do(dve.tensor_scalar(score[:, tt, 0:w], x, wi, None, ALU.mult))
                            continue
                        last = dve.scalar_tensor_tensor(score[:, tt, 0:w], x, wi, score[:, tt, 0:w], ALU.mult, ALU.add)
                        if r == 0:
                            c.do(last)
                    last.then_inc(score_ready, 1)
                    dve.wait_ge(score_ready, n + 1)
                    n += 1
            for tt in range(TT):
                w = (tt + 1) * P
                dve.wait_ge(score_masked, tt + 1)
                src = score[:, tt, 0:w]
                for r in range(SEL // 8):
                    c.do(dve.max(top[:], src))
                    c.do(dve.match_replace(work[:, 0:w], top[:], src, TAKEN))
                    src = work[:, 0:w]
                c.do(dve.tensor_scalar(work[:, 0:w], work[:, 0:w], 0.5 * TAKEN, -NEG, ALU.is_lt, ALU.mult))
                dve.tensor_scalar(bias[:, tt, 0:w], work[:, 0:w], NEG, None, ALU.add).then_inc(pick_ready, 1)
                dve.wait_ge(pick_ready, tt + 1)

            def scores(n):
                tt, j = units[n]
                w = (tt + 1) * P
                if j == 0:
                    dve.wait_ge(pick_masked, tt + 1)
                dve.wait_ge(l_made, n + 1)
                if n >= 2:
                    dve.wait_ge(turned, n - 1)
                x = lg[:, n % 2, :, 0:w]
                dve.scalar_tensor_tensor(x, K.bank[:, n % 2, :].rearrange("p (h s) -> p h s", h=2)[:, :, 0:w], 0.125,
                                         bias[:, tt, 0:w].unsqueeze(1).to_broadcast([P, 2, w]), ALU.mult,
                                         ALU.add).then_inc(l_used, 1)
                dve.wait_ge(l_used, n + 1)
                c.do(dve.tensor_reduce(mx[:, n % 2, :], x, AX.X, ALU.max))
                dve.tensor_scalar(mx[:, n % 2, :], mx[:, n % 2, :], -1.0, None, ALU.mult).then_inc(max_ready, 1)

            def divide(n):
                tt, j = units[n]
                w = (tt + 1) * P
                dve.wait_ge(exp_done, 2 * n + 2)
                c.do(dve.reciprocal(total[:, n % 2, :], total[:, n % 2, :]))
                x = lg[:, n % 2, :, 0:w]
                dve.tensor_tensor(x, x, total[:, n % 2, :].unsqueeze(2).to_broadcast([P, 2, w]), ALU.mult).then_inc(p_ready, 1)

            def take(n):
                tt, j = units[n]
                dve.wait_ge(o_made, n + 1)
                dve.tensor_copy(S.yaT[:, j, tt * P:(tt + 1) * P], K.bank[:, 4 + n % 2, 0:P]).then_inc(o_copied, 1)

            for i in range(len(units) + 2):
                if i < len(units):
                    scores(i)
                if 1 <= i <= len(units):
                    divide(i - 1)
                if i >= 2:
                    take(i - 2)



def join_stage(K, S):
    nc = K.nc
    s_ = lambda s: K.sem(f"join_{s}")
    gelu_done, sig_done, y_ready, chain, m_ready, turned, evac = (
        s_(s) for s in ("gelu", "sig", "y", "dve", "m", "turned", "evac"))
    with ExitStack() as stage, nc.Block() as block:
        sig = stage.enter_context(nc.sbuf_tensor("join_sig", [P, 4, T], F32))
        n_glu, n_ssm, n_attn, n_out = (START[n] for n in ("w_glu", "ssm_up", "attn_up", "w_out2"))

        @block.sync
        def _(sp):
            fetch_chunks(sp, K, next_start("w_out2") + RING)

        @block.scalar
        def _(act):
            act.activation(S.yT[:], S.yT[:], ACT.Gelu_apprx_tanh).then_inc(gelu_done, 1)
            act.wait_ge(K.chunk_used, n_glu + 1)
            act.activation(sig[:], K.bank[:, 0:2, :].rearrange("p b (c t) -> p (b c) t", c=2), ACT.Sigmoid).then_inc(sig_done, 1)
            evacuate_turned(act, K, turned, evac)

        @block.tensor
        def _(pe):
            pe.wait_ge(gelu_done, 1)
            wait_chunk(pe, K, n_glu)
            w = K.ring[:, n_glu % RING, 0:4 * 512].rearrange("p (k c) -> p k c", k=4)
            for i in range(4):
                for k in range(4):
                    last = pe.matmul(K.bank[:, i // 2, (i % 2) * T:(i % 2 + 1) * T], w[:, k, i * P:(i + 1) * P],
                                     S.yT[:, k, :], start=(k == 0), stop=(k == 3))
            last.then_inc(K.chunk_used, 1)
            pe.wait_ge(y_ready, 1)
            for n, xT, b in ((n_ssm, S.yT, 0), (n_attn, S.yaT, 4)):
                wait_chunk(pe, K, n)
                w = K.ring[:, n % RING, :].rearrange("p (k c) -> p k c", k=4)
                for tt in range(TT):
                    for dh in range(2):
                        for k in range(4):
                            last = pe.matmul(K.bank[:, b + 2 * tt + dh, :], xT[:, k, tt * P:(tt + 1) * P],
                                             w[:, k, dh * 512:(dh + 1) * 512], start=(k == 0), stop=(k == 3))
                last.then_inc(K.chunk_used, 1)
            turn_tokens(pe, K, S.gates[:, 0, :, :], m_ready, turned)
            pe.wait_ge(evac, 4)
            for dh in range(2):
                token_product(pe, K, n_out + dh, K.hT, [K.bank[:, 2 * tt + dh, :] for tt in range(TT)])

        @block.vector
        def _(dve):
            c = Chain(dve, chain)
            dve.wait_ge(sig_done, 1)
            dve.tensor_tensor(S.yT[:], S.yT[:], sig[:], ALU.mult).then_inc(y_ready, 1)
            gs, ga = S.gates[:, 0, :, :], S.gates[:, 1, :, :]
            product = lambda b: K.bank[:, b:b + 4, :].rearrange("p (t b) c -> p t (b c)", t=TT)
            dve.wait_ge(K.chunk_used, n_ssm + 1)
            c.step(dve.tensor_tensor(gs, gs, product(0), ALU.mult))
            dve.wait_ge(K.chunk_used, n_attn + 1)
            c.do(dve.tensor_tensor(ga, ga, product(4), ALU.mult))
            dve.tensor_tensor(gs, gs, ga, ALU.add).then_inc(m_ready, TT)


def add_banks(K):
    def add(dve, c, tt):
        x = K.x[:, tt, :]
        c.do(dve.tensor_tensor(x, x, K.bank[:, 2 * tt:2 * tt + 2, :].rearrange("p b c -> p (b c)"), ALU.add))
    return add


class Second:

    def __init__(self, nc, scope):
        sb = lambda n, s: scope.enter_context(nc.sbuf_tensor(n, s, F32))
        self.uT = sb("uT", [P, 4, T])
        self.qT = sb("qT", [P, 4, T])
        self.qiT = sb("qiT", [P, 2, T])
        self.kz = sb("kz", [P, 2, T])
        self.kiz = sb("kiz", [P, 4, T])
        self.vz = sb("vz", [P, 2, TT, P])
        self.wi = sb("wi", [P, TT, 8])
        self.gates = sb("gates", [P, 2, TT, D])
        self.yT = sb("ysT", [P, 4, T])
        self.yaT = sb("yaT", [P, 4, T])



PK_HEADS = 8
PK = 128
TOP = 16
U_SLOTS = 3
V_SLOTS = 3


def peer_query_stage(K, scores, h_hi, h_lo):
    nc = K.nc
    n_wq, n_keys = START["peer_wq"], START["peer_keys"]
    act_done, dve_done, s_made = (K.sem(f"peerq_{s}") for s in ("act_done", "dve_done", "s_made"))
    with ExitStack() as stage, nc.Block() as block:
        qT = stage.enter_context(nc.sbuf_tensor("peer_qT", [P, 2 * PK_HEADS, T], F32))
        products = SplitProducts(K, stage, "peer_wq", n_wq, (h_hi, h_lo))

        @block.sync
        def _(sp):
            fetch_chunks(sp, K, CHUNKS)

        @block.tensor
        def _(pe):
            for j in range(4):
                products.feature_product(pe, n_wq + j, 2 * j)
            wait_chunk(pe, K, n_keys)
            keys = K.ring[:, n_keys % RING, 0:2048].rearrange("p (m n) -> p m n", n=PK)
            for n in range(8):
                tt, g = n // 4, n % 4
                for done in (act_done, dve_done):
                    done_to = max(g, n // 2) + 1
                    pe.wait_ge(done, done_to)
                for i in range(4):
                    m = 4 * g + i
                    last = pe.matmul(K.bank[:, n, i * PK:(i + 1) * PK], qT[:, m, tt * P:(tt + 1) * P], keys[:, m, :],
                                     start=True, stop=True)
                last.then_inc(s_made, 1)

        tiles = lambda b: K.bank[:, b, :].rearrange("p (c t) -> p c t", c=2)

        @block.gpsimd
        def _(pool):
            for j in range(4):
                products.low(pool, n_wq + j, True)

        @block.scalar
        def _(act):
            products.high_x(act)
            products.high(act, n_wq, True)
            for j in range(4):
                if j < 3:
                    products.high(act, n_wq + j + 1, True)
                act.wait_ge(K.chunk_used, n_wq + j + 1)
                act.activation(qT[:, 4 * j:4 * j + 2, :], tiles(2 * j), ACT.Copy).then_inc(act_done, 1)
            for n in range(0, 8, 2):
                act.wait_ge(s_made, n + 1)
                act.activation(scores[:, n // 4, n % 4 * 512:(n % 4 + 1) * 512], K.bank[:, n, :], ACT.Copy)

        @block.vector
        def _(dve):
            products.low_x(dve)
            for j in range(4):
                dve.wait_ge(K.chunk_used, n_wq + j + 1)
                dve.tensor_copy(qT[:, 4 * j + 2:4 * j + 4, :], tiles(2 * j + 1)).then_inc(dve_done, 1)
            for n in range(1, 8, 2):
                dve.wait_ge(s_made, n + 1)
                dve.tensor_copy(scores[:, n // 4, n % 4 * 512:(n % 4 + 1) * 512], K.bank[:, n, :])


def top_sixteen(dve, c, values, index, src):
    c.do(dve.max(values[:, 0:8], src))
    c.do(dve.max_index(index[:, 0:8], values[:, 0:8], src))
    c.do(dve.match_replace(src, values[:, 0:8], src, TAKEN))
    c.do(dve.max(values[:, 8:TOP], src))
    c.step(dve.max_index(index[:, 8:TOP], values[:, 8:TOP], src))


def peer_stage(K, scores, scores_scope, h_hi, h_lo, h_scope):
    nc = K.nc
    s_ = lambda s: K.sem(f"peer_{s}")
    u_in = [s_(f"u_in{i}") for i in range(U_SLOTS)]
    v_in = [s_(f"v_in{i}") for i in range(V_SLOTS)]
    gelu_done, chain, exp_ready, exp_done = (s_(s) for s in ("gelu", "dve", "exp_ready", "exp_done"))
    with ExitStack() as stage:
        H = stage.enter_context(nc.sbuf_tensor("H", [P, PK, T], F32))
        sel = stage.enter_context(nc.sbuf_tensor("sel", [P, 3, TT, P], F32))
        route = stage.enter_context(ExitStack())
        sb = lambda n, s, dt=F32: route.enter_context(nc.sbuf_tensor(f"peer_{n}", s, dt))
        u = sb("u", [P, U_SLOTS, KD, PK])
        val = sb("val", [P, 2, TOP])
        idx = sb("idx", [P, 2, TOP], U32)
        idx_f = sb("idx_f", [P, PK_HEADS, 2, TOP])
        cand = sb("cand", [P, 2 * P])
        best = sb("best", [P, PK_HEADS, TOP])
        pos = sb("pos", [P, PK_HEADS, TOP], U32)
        part = sb("part", [P, 2, PK_HEADS, TOP], U32)
        part_f = sb("part_f", [P, 2, PK_HEADS, TOP])
        hot = sb("hot", [P, TOP, TOP])
        col = sb("col", [P, 2, PK_HEADS])

        HALVES = 3
        u_hi, u_lo = (route.enter_context(nc.sbuf_tensor(f"peer_{n}", [P, HALVES, KD // 2, PK], F32R)) for n in ("u_hi", "u_lo"))
        hi_made, lo_made, halves_used = (s_(s) for s in ("u_hi", "u_lo", "halves_used"))
        TURNS = PK // U_SLOTS

        def u_tiles(eng, step, peeled=0):
            for n in range(peeled * U_SLOTS):
                step(n, n % U_SLOTS, 16 * (n // U_SLOTS + 1))
            with eng.Fori(peeled, TURNS) as g:
                for i in range(U_SLOTS):
                    step(g * U_SLOTS + i, i, 16 * g + 16)
            for n in range(TURNS * U_SLOTS, PK):
                step(n, n % U_SLOTS, 16 * (n // U_SLOTS + 1))

        with nc.Block() as block:
            @block.sync
            def _(sp):
                for i in range(U_SLOTS):
                    sp.dma_start(u[:, i, :, :], K.A["peer_u"][i]).then_inc(u_in[i], 16)
                with sp.Fori(0, (PK - U_SLOTS) // U_SLOTS) as g:
                    for i in range(U_SLOTS):
                        sp.wait_ge(lo_made, 2 * U_SLOTS * g + 2 * (i + 1))
                        sp.dma_start(u[:, i, :, :], K.A["peer_u"][g * U_SLOTS + (U_SLOTS + i)]).then_inc(u_in[i], 16)
                for n in range((PK - U_SLOTS) // U_SLOTS * U_SLOTS + U_SLOTS, PK):
                    sp.wait_ge(lo_made, 2 * (n - U_SLOTS + 1))
                    sp.dma_start(u[:, n % U_SLOTS, :, :], K.A["peer_u"][n]).then_inc(u_in[n % U_SLOTS], 16)

            @block.tensor
            def _(pe):
                pe.sem_inc(halves_used, HALVES)

                def tile(n, i, land):
                    pe.wait_ge(gelu_done, n + 1)
                    out = K.bank[:, i, 0:T]
                    for half in range(2):
                        pe.wait_ge(lo_made, 2 * n + (half + 1))
                        b = (2 * i + half) % HALVES
                        for k2 in range(KD // 2):
                            k = KD // 2 * half + k2
                            pe.matmul(out, u_hi[:, b, k2, :], h_hi[:, k, :], start=(k == 0), stop=False)
                            pe.matmul(out, u_hi[:, b, k2, :], h_lo[:, k, :], start=False, stop=False)
                            last = pe.matmul(out, u_lo[:, b, k2, :], h_hi[:, k, :], start=False, stop=(k == KD - 1))
                        last.then_inc(halves_used, 1)

                u_tiles(pe, tile)

            @block.gpsimd
            def _(pool):
                def low(n, i, land):
                    pool.wait_ge(u_in[i], land)
                    for half in range(2):
                        pool.wait_ge(hi_made, 2 * n + (half + 1))
                        b = (2 * i + half) % HALVES
                        pool.tensor_tensor(u_lo[:, b, :, :], u[:, i, KD // 2 * half:KD // 2 * (half + 1), :],
                                           u_hi[:, b, :, :].bitcast(F32), ALU.subtract).then_inc(lo_made, 1)

                u_tiles(pool, low)

            @block.scalar
            def _(act):
                act.sem_inc(gelu_done, U_SLOTS)

                def gelu(n, i):
                    act.wait_ge(halves_used, 2 * n + (2 + HALVES))
                    out = H[:, n, :] if isinstance(n, int) else H[:, bass.ds(n, 1), :].rearrange("p o t -> p (o t)")
                    act.activation(out, K.bank[:, i, 0:T], ACT.Gelu_apprx_tanh).then_inc(gelu_done, 1)

                def high(n, i, land):
                    act.wait_ge(u_in[i], land)
                    for half in range(2):
                        act.wait_ge(halves_used, 2 * n + (half + 1))
                        b = (2 * i + half) % HALVES
                        act.activation(u_hi[:, b, :, :], u[:, i, KD // 2 * half:KD // 2 * (half + 1), :],
                                       ACT.Copy).then_inc(hi_made, 1)
                    if not (isinstance(n, int) and n == 0):
                        gelu(n - 1, (i - 1) % U_SLOTS)

                u_tiles(act, high, peeled=1)
                gelu(PK - 1, (PK - 1) % U_SLOTS)
                for tt in range(TT):
                    act.wait_ge(exp_ready, tt + 1)
                    act.activation(sel[:, 2, tt, :], sel[:, 2, tt, :], ACT.Exp).then_inc(exp_done, 1)

            @block.vector
            def _(dve):
                c = Chain(dve, chain)
                wide = lambda a: a.unsqueeze(2).to_broadcast([P, PK_HEADS, TOP])
                flat = lambda a: a.rearrange("p h k -> p (h k)")
                for tt in range(TT):
                    for h in range(PK_HEADS):
                        for half in range(2):
                            m = 2 * h + half
                            top_sixteen(dve, c, val[:, half, :], idx[:, half, :], scores[:, tt, m * PK:(m + 1) * PK])
                        c.settle()
                        c.step(dve.tensor_copy(idx_f[:, h, :, :], idx[:]))
                        c.do(dve.tensor_tensor(cand[:].rearrange("p (a b) -> p a b", a=TOP),
                                               val[:, 0, :].unsqueeze(2).to_broadcast([P, TOP, TOP]),
                                               val[:, 1, :].unsqueeze(1).to_broadcast([P, TOP, TOP]), ALU.add))
                        top_sixteen(dve, c, best[:, h, :], pos[:, h, :], cand[:])
                        c.settle()
                    c.step(dve.tensor_scalar(part[:, 0, :, :], pos[:], 4, None, ALU.logical_shift_right))
                    c.do(dve.tensor_scalar(part[:, 1, :, :], pos[:], TOP - 1, None, ALU.bitwise_and))
                    c.do(dve.tensor_copy(part_f[:], part[:]))
                    for half in range(2):
                        for h in range(PK_HEADS):
                            c.do(dve.tensor_tensor(hot[:], part_f[:, half, h, :].unsqueeze(2).to_broadcast([P, TOP, TOP]),
                                                   K.iota[:, 0:TOP].unsqueeze(1).to_broadcast([P, TOP, TOP]), ALU.is_equal))
                            c.do(dve.tensor_tensor(hot[:], hot[:], idx_f[:, h, half, :].unsqueeze(1).to_broadcast([P, TOP, TOP]),
                                                   ALU.mult))
                            c.do(dve.tensor_reduce(sel[:, half, tt, h * TOP:(h + 1) * TOP], hot[:], AX.X, ALU.add))
                    gate = sel[:, 2, tt, :].rearrange("p (h k) -> p h k", k=TOP)
                    dve.tensor_tensor(gate, best[:], wide(best[:, :, 0]), ALU.subtract).then_inc(exp_ready, 1)
                    dve.wait_ge(exp_ready, tt + 1)
                for tt in range(TT):
                    gate = sel[:, 2, tt, :].rearrange("p (h k) -> p h k", k=TOP)
                    dve.wait_ge(exp_done, tt + 1)
                    c.do(dve.tensor_reduce(col[:, tt, :], gate, AX.X, ALU.add))
                    c.do(dve.reciprocal(col[:, tt, :], col[:, tt, :]))
                    c.do(dve.tensor_tensor(gate, gate, wide(col[:, tt, :]), ALU.mult))
        route.close()
        scores_scope.close()
        h_scope.close()

        v = stage.enter_context(nc.sbuf_tensor("peer_v", [P, V_SLOTS, D], F32))
        hots = stage.enter_context(ExitStack())
        sb = lambda n, s, dt=F32: hots.enter_context(nc.sbuf_tensor(f"peer_{n}", s, dt))
        selT = sb("selT", [P, 2, T])
        QT = 4
        a_hot = sb("a_hot", [P, 2, QT, P])
        b_hot = sb("b_hot", [P, 2, QT, P])
        away = sb("away", [P, 2, QT, P])
        neg_i1 = sb("neg_i1", [P, T])
        turned, selT_done, hot_ready, g_made, g_used = (s_(s) for s in ("turned", "selT", "hot", "g_made", "g_used"))
        neg_ready, away_made, b_ready = (s_(s) for s in ("neg", "away", "b_ready"))
        with nc.Block() as block:
            @block.sync
            def _(sp):
                for i in range(V_SLOTS):
                    sp.dma_start(v[:, i, :], K.A["peer_v"][i]).then_inc(v_in[i], 16)

            @block.tensor
            def _(pe):
                for r in range(3):
                    for tt in range(TT):
                        last = pe.transpose(K.bank[:, r, tt * P:(tt + 1) * P], sel[:, r, tt, :], K.ident)
                last.then_inc(turned, 1)
                with pe.Fori(0, T // (2 * QT)) as g:
                    for b in range(2):
                        pe.wait_ge(hot_ready, 2 * g + (b + 1))
                        pe.wait_ge(b_ready, 2 * g + (b + 1))
                        pe.wait_ge(g_used, 2 * g + (b + 1))
                        for q in range(QT):
                            last = pe.matmul(K.bank[:, 3 + b, q * P:(q + 1) * P], a_hot[:, b, q, :], b_hot[:, b, q, :],
                                             start=True, stop=True)
                        last.then_inc(g_made, 1)

            @block.scalar
            def _(act):
                act.wait_ge(turned, 1)
                act.activation(neg_i1[:], K.bank[:, 0, 0:T], ACT.Copy, scale=-1.0).then_inc(neg_ready, 1)
                act.wait_ge(neg_ready, 1)

                def one_hot(b, first, count, used=None):
                    for q in range(QT):
                        at = bass.ds(first + q, 1) if used is not None else slice(first + q, first + q + 1)
                        last = act.activation(away[:, b, q, :], K.iota, ACT.Square, bias=neg_i1[:, at])
                    last.then_inc(away_made, 1)
                    act.wait_ge(away_made, count)
                    if used is not None:
                        act.wait_ge(g_made, used)
                    act.activation(b_hot[:, b, :, :], away[:, b, :, :], ACT.Relu, scale=-4.0, bias=1.0).then_inc(b_ready, 1)

                one_hot(0, 0, 1)
                one_hot(1, QT, 2)
                with act.Fori(0, T // (2 * QT) - 1) as g:
                    for b in range(2):
                        one_hot(b, g * 2 * QT + (2 * QT + b * QT), 2 * g + (3 + b), 2 * g + (b + 1))

            @block.vector
            def _(dve):
                dve.sem_inc(g_used, 2)
                dve.wait_ge(turned, 1)
                dve.wait_ge(neg_ready, 1)
                dve.tensor_copy(selT[:], K.bank[:, 1:3, 0:T]).then_inc(selT_done, 1)
                dve.wait_ge(selT_done, 1)

                def one_hots(g, b, ahead):
                    for q in range(QT):
                        at = bass.ds(g * 2 * QT + (ahead + q), 1) if not isinstance(g, int) else slice(ahead + q, ahead + q + 1)
                        last = dve.tensor_scalar(a_hot[:, b, q, :], K.iota, selT[:, 0, at], selT[:, 1, at],
                                                 ALU.is_equal, ALU.mult)
                    last.then_inc(hot_ready, 1)

                def gate_h(g, b, count):
                    dve.wait_ge(g_made, count)
                    h = H[:, :, bass.ds(g * 2 * QT + b * QT, QT)]
                    dve.tensor_tensor(h, h, K.bank[:, 3 + b, :].rearrange("p (q i) -> p i q", q=QT),
                                      ALU.mult).then_inc(g_used, 1)

                one_hots(0, 0, 0)
                one_hots(0, 1, QT)
                with dve.Fori(0, T // (2 * QT) - 1) as g:
                    for b in range(2):
                        gate_h(g, b, 2 * g + (b + 1))
                        one_hots(g, b, 2 * QT + b * QT)
                g = T // (2 * QT) - 1
                for b in range(2):
                    dve.wait_ge(g_made, 2 * g + b + 1)
                    h = H[:, :, 2 * QT * g + b * QT:2 * QT * g + (b + 1) * QT]
                    dve.tensor_tensor(h, h, K.bank[:, 3 + b, :].rearrange("p (q i) -> p i q", q=QT), ALU.mult).then_inc(g_used, 1)
        hots.close()

        BUFS = 3
        hi_ready, lo_ready, used = (s_(s) for s in ("hi", "lo", "used"))
        split = lambda n, shape: stage.enter_context(nc.sbuf_tensor(f"peer_{n}", [P, BUFS] + shape, F32R))
        v_hi, v_lo, h_hi, h_lo = split("v_hi", [D]), split("v_lo", [D]), split("h_hi", [T]), split("h_lo", [T])
        with nc.Block() as block:
            LOOPS = (PK - 2) // V_SLOTS

            @block.sync
            def _(sp):
                with sp.Fori(0, (PK - V_SLOTS) // V_SLOTS) as g:
                    for i in range(V_SLOTS):
                        sp.wait_ge(lo_ready, g * V_SLOTS + (i + 1))
                        sp.dma_start(v[:, i, :], K.A["peer_v"][g * V_SLOTS + (V_SLOTS + i)]).then_inc(v_in[i], 16)
                for n in range((PK - V_SLOTS) // V_SLOTS * V_SLOTS + V_SLOTS, PK):
                    sp.wait_ge(lo_ready, n - V_SLOTS + 1)
                    sp.dma_start(v[:, n % V_SLOTS, :], K.A["peer_v"][n]).then_inc(v_in[n % V_SLOTS], 16)

            def tiles(eng, step):
                with eng.Fori(0, PK // V_SLOTS) as g:
                    for i in range(V_SLOTS):
                        step(g * V_SLOTS + i, i, 16 * g + 16)
                for n in range(PK // V_SLOTS * V_SLOTS, PK):
                    step(n, n % V_SLOTS, 16 * (n // V_SLOTS + 1))

            def h_tile(n):
                return H[:, n, :] if isinstance(n, int) else H[:, bass.ds(n, 1), :].rearrange("p o t -> p (o t)")

            @block.tensor
            def _(pe):
                pe.sem_inc(used, BUFS)

                def product(n, b, start, stop):
                    pe.wait_ge(lo_ready, n + 1)
                    for tt in range(TT):
                        mine = slice(tt * P, (tt + 1) * P)
                        for h, v_part, first, last_one in ((h_hi, v_hi, True, False), (h_hi, v_lo, False, False),
                                                           (h_lo, v_hi, False, True)):
                            for dh in range(2):
                                last = pe.matmul(K.bank[:, 2 * tt + dh, :], h[:, b, mine],
                                                 v_part[:, b, dh * 512:(dh + 1) * 512], start=start and first,
                                                 stop=stop and last_one)
                    last.then_inc(used, 1)

                product(0, 0, True, False)
                with pe.Fori(0, LOOPS) as g:
                    for i in range(V_SLOTS):
                        product(g * V_SLOTS + (1 + i), (1 + i) % BUFS, False, False)
                product(PK - 1, (PK - 1) % BUFS, False, True)

            @block.scalar
            def _(act):
                def high(n, i, land):
                    act.wait_ge(v_in[i], land)
                    act.wait_ge(used, n + 1)
                    act.activation(h_hi[:, i % BUFS, :], h_tile(n), ACT.Copy)
                    act.activation(v_hi[:, i % BUFS, :], v[:, i, :], ACT.Copy).then_inc(hi_ready, 1)

                tiles(act, high)

            @block.vector
            def _(dve):
                def low(n, i, land):
                    dve.wait_ge(v_in[i], land)
                    dve.wait_ge(hi_ready, n + 1)
                    b = i % BUFS
                    dve.tensor_tensor(h_lo[:, b, :], h_tile(n), h_hi[:, b, :].bitcast(F32), ALU.subtract)
                    dve.tensor_tensor(v_lo[:, b, :], v[:, i, :], v_hi[:, b, :].bitcast(F32), ALU.subtract).then_inc(lo_ready, 1)

                tiles(dve, low)



def program(nc, inputs, out):
    with ExitStack() as ctx:
        K = Core(nc, ctx, inputs)
        with ExitStack() as scope:
            load_stage(K, scope)
            ada_stage(K, "ada00")
            ada = stick_breaking_stage(K)
            moe_stage(K, 0, ada, "ada10").h_scope.close()
            K.recycle_sems()
            ada = retention_stage(K)
            moe_stage(K, 1, ada)
            rms_norm_turn_stage(K, "norm1", "norm1_g")
            with ExitStack() as second:
                S = Second(nc, second)
                projection_and_s5_stage(K, S)
                sparse_attention_stage(K, S)
                join_stage(K, S)
            K.recycle_sems()
            rms_norm_turn_stage(K, "norm2", "norm2_g", before=add_banks(K))
            h_scope, scores_scope = ctx.enter_context(ExitStack()), ctx.enter_context(ExitStack())
            h_hi, h_lo = (h_scope.enter_context(nc.sbuf_tensor(f"peer_hn_{n}", [P, KD, T], F32R, side="right")) for n in ("hi", "lo"))
            scores = scores_scope.enter_context(nc.sbuf_tensor("peer_scores", [P, TT, 2048], F32, side="right"))
            peer_query_stage(K, scores, h_hi, h_lo)
        peer_stage(K, scores, scores_scope, h_hi, h_lo, h_scope)
        rms_norm_turn_stage(K, "norm_f", "norm_f_g", before=add_banks(K),
                            out=out[0].rearrange("(t p) d -> p t d", p=P))



def _chunks(w):
    rows, cols = w.shape
    kt = rows // P
    c = CHUNK // kt
    return w.reshape(kt, P, cols // c, c).transpose(2, 1, 0, 3).reshape(cols // c, P, CHUNK)


def _short(w):
    rows, cols = w.shape
    out = np.zeros((1, P, CHUNK), w.dtype)
    out[0, :, 0:rows // P * cols] = w.reshape(rows // P, P, cols).transpose(1, 0, 2).reshape(P, -1)
    return out


def _experts(gate, up, down):
    parts = []
    for e in range(EXPERTS):
        parts += [_chunks(gate[e]), _chunks(up[e])]
        if e:
            parts.append(_chunks(down[e - 1]))
    return parts + [_chunks(down[EXPERTS - 1])]


def _swap(dim):
    m = np.zeros((P, P), np.float32)
    for base in range(0, P, dim):
        for i in range(dim // 2):
            m[base + dim // 2 + i, base + i] = -1.0
            m[base + i, base + dim // 2 + i] = 1.0
    return m


def _rope_rows(dim):
    inv = (np.float32(10000.0) ** (-np.arange(0, dim, 2, dtype=np.float32) / np.float32(dim))).astype(np.float32)
    ang = np.arange(T, dtype=np.float32)[None, :] * inv[np.arange(P) % (dim // 2)][:, None]
    return np.stack([np.cos(ang), np.sin(ang)], 1).astype(np.float32)


def _retention_decay():
    h = np.arange(RET_HEADS, dtype=np.float32)
    lg = np.log(np.float32(1.0) - np.exp2(np.float32(-5.0) - h)).astype(np.float64)
    m, n = np.arange(P)[:, None, None], np.arange(P)[None, None, :]
    lg = lg[None, :, None]
    own = np.where(n >= m, np.exp(np.maximum(n - m, 0) * lg), 0.0)
    before = np.exp((n + 1.0 + P - 1.0 - m) * lg)
    return np.concatenate([own, before], 2).astype(np.float32)


def layout(a):
    eye = np.eye(P, dtype=np.float32)
    tri = -np.tril(np.ones((P, P), np.float32))
    w2 = a["w_in_2"][0]
    u, q, k, v, qi, ki, wi, gs, ga = np.split(w2, np.cumsum([512, 512, 128, 128, 256, 32, 8, 1024])[:8], axis=1)
    pair = np.concatenate([np.concatenate([np.arange(64 * j, 64 * j + 64), np.arange(64 * (j + 4), 64 * (j + 4) + 64)])
                           for j in range(4)])
    stream = []
    for i in range(DEPTH):
        stream += [_chunks(a["ada_w"][i, 0])]
        stream += [_chunks(a["sb_w_in"][0]), _chunks(a["sb_w_out"][0])] if i == 0 else [
            _chunks(a["ret_w_in"][0])] + [_chunks(a["ret_w_out"][0][r:r + D, c:c + COLS])
                                          for c in (0, COLS) for r in (0, D)]
        stream += [_chunks(a["ada_w"][i, 1])]
        stream += _experts(a["moe_w_gate"][i], a["moe_w_up"][i], a["moe_w_down"][i])
    stream += [_chunks(u), _chunks(q[:, pair]), _chunks(np.concatenate([k, qi, ki, ki, ki, ki], 1)),
               _short(np.concatenate([v, wi], 1)), _chunks(gs), _chunks(ga), _short(a["w_glu_2"][0]),
               _chunks(a["w_ssm_up_2"][0]), _chunks(a["w_attn_up_2"][0][pair]), _chunks(a["w_out_2"][0]),
               _chunks(a["peer_wq_2"][0])]
    keys = np.stack([a["peer_k1_2"][0], a["peer_k2_2"][0]], 1)
    stream += [_short(keys.reshape(-1, P).T)]
    stream = np.concatenate(stream)
    assert stream.shape == (CHUNKS, P, CHUNK)
    states = lambda s: s[0].reshape(16, P).T
    cz = np.zeros((2, 16, P, P), np.float32)
    for n, c in enumerate((a["c_re_2"][0], a["c_im_2"][0])):
        for g in range(32):
            col = 16 * (g % 8)
            cz[n, g // 2, 64 * (g % 2):64 * (g % 2) + 64, col:col + 16] = c[g].T
    out = {
        "stream": stream,
        "x_tokens": a["x"][0].reshape(TT, P, D).transpose(1, 0, 2),
        "c_cols": a["c"].reshape(KD, P).T,
        "ada_b": a["ada_b"].reshape(4, 3 * D),
        "ln_g": a["ln_g"].reshape(4, D),
        "ln_b": a["ln_b"].reshape(4, D),
        "consts": np.stack([eye, tri, -np.ones((P, P), np.float32), _swap(128), _swap(64), _swap(32),
                            np.tile(np.arange(P, dtype=np.float32), (P, 1))], 1),
        "router_w": a["router_w"].reshape(KD, P, EXPERTS).transpose(1, 0, 2),
        "router_b": a["router_b"].reshape(1, EXPERTS),
        "positions": a["positions"].reshape(1, T),
        "inv_freq": (np.float32(1.0) / (np.float32(10000.0) ** (np.arange(0, 128, 2, dtype=np.float32) / np.float32(128)))
                     ).astype(np.float32)[np.arange(P) % 64].reshape(P, 1),
        "decay": _retention_decay(),
        "ret_gn_g": a["ret_gn_g"].reshape(1, 2 * D),
        "rope64": _rope_rows(64),
        "rope32": _rope_rows(32),
        "norm1_g": a["norm1_g_2"].reshape(1, D),
        "norm2_g": a["norm2_g_2"].reshape(1, D),
        "norm_f_g": a["norm_f_g_2"].reshape(1, D),
        "a_re": states(a["a_re_2"]),
        "a_im": states(a["a_im_2"]),
        "log_dt": np.repeat(a["log_dt_2"][0], 64).reshape(16, P).T,
        "b_re": a["b_re_2"][0].reshape(16, P, 16).transpose(1, 0, 2),
        "b_im": a["b_im_2"][0].reshape(16, P, 16).transpose(1, 0, 2),
        "c_re": cz[0].transpose(1, 0, 2),
        "c_im": cz[1].transpose(1, 0, 2),
        "d_skip": a["d_skip_2"].reshape(4, P).T,
        "peer_u": a["peer_u_2"][0].reshape(P, P, KD, P).transpose(0, 3, 2, 1).reshape(P, P, KD * P),
        "peer_v": a["peer_v_2"][0].reshape(P, P, D),
    }
    return {k: np.ascontiguousarray(v) for k, v in out.items()}


def kernel(**inputs):
    from concourse import bacc
    from concourse.bass_utils import run_bass_kernel_spmd

    nc = bacc.Bacc("TRN2", target_bir_lowering=False, num_devices=1)
    arrays = layout({k: np.asarray(v) for k, v in inputs.items()})
    aps = {k: nc.dram_tensor(f"in_{k}", v.shape, mybir.dt.from_np(v.dtype), kind="ExternalInput").ap()
           for k, v in arrays.items()}
    out = nc.dram_tensor("out", (1, T, D), F32, kind="ExternalOutput").ap()
    program(nc, aps, out)
    result = run_bass_kernel_spmd(nc, [{f"in_{k}": v for k, v in arrays.items()}], core_ids=[0])
    return result.results[0]["out"]
```
